# Optimizing a Trainium2 kernel written in Bass

```python
import jax, jax.numpy as jnp
from jax import lax
import numpy as np

D_MODEL = 1024
BATCH = 1
SEQ = 512
DEPTH = 1

SSM_HEADS = 16
SSM_HEAD_DIM = 64
SSM_WIDTH = SSM_HEADS * SSM_HEAD_DIM
SSM_GROUPS = 2
SSM_STATE = 128
CONV_WIDTH = 4
CHUNK = 128
CONV_DIM = SSM_WIDTH + 2 * SSM_GROUPS * SSM_STATE
ATT_HEADS = 16
ATT_HEAD_DIM = 64
ATT_WIDTH = ATT_HEADS * ATT_HEAD_DIM
Q_BLOCK = 128
MIX_WIDTH = SSM_WIDTH + ATT_WIDTH
D_FF = 4 * D_MODEL
SPLITS = [SSM_WIDTH,
          SSM_WIDTH + CONV_DIM,
          SSM_WIDTH + CONV_DIM + SSM_HEADS,
          SSM_WIDTH + CONV_DIM + SSM_HEADS + ATT_WIDTH,
          SSM_WIDTH + CONV_DIM + SSM_HEADS + 2 * ATT_WIDTH,
          SSM_WIDTH + CONV_DIM + SSM_HEADS + 3 * ATT_WIDTH]
IN_COLS = SPLITS[-1] + ATT_HEADS
DEEPNORM_ALPHA = (2.0 * DEPTH) ** 0.25
DEEPNORM_BETA = (8.0 * DEPTH) ** -0.25
LN_EPS = 1e-5
RMS_EPS = 1e-5


def layer_norm(x, g, b):
    xf = x.astype(jnp.float32)
    mu = jnp.mean(xf, axis=-1, keepdims=True)
    var = jnp.mean(jnp.square(xf - mu), axis=-1, keepdims=True)
    return ((xf - mu) * lax.rsqrt(var + LN_EPS) * g + b).astype(x.dtype)

def rms_norm(x, w):
    xf = x.astype(jnp.float32)
    return xf * lax.rsqrt(jnp.mean(xf * xf, axis=-1, keepdims=True) + RMS_EPS) * w

def causal_depthwise_conv(u, w, b):
    out = lax.conv_general_dilated(
        u, w[:, None, :].astype(u.dtype), window_strides=(1,),
        padding=[(CONV_WIDTH - 1, 0)], dimension_numbers=('NWC', 'WIO', 'NWC'),
        feature_group_count=u.shape[-1])
    return out + b

def segsum(a):
    cs = jnp.cumsum(a, axis=-1)
    diff = cs[..., :, None] - cs[..., None, :]
    t = a.shape[-1]
    mask = jnp.tril(jnp.ones((t, t), dtype=bool))
    return jnp.where(mask, diff, -jnp.inf)

def ssd_chunked(xh, dt, A, Bm, Cm):
    b, s, h, p = xh.shape
    g, n = Bm.shape[-2], Bm.shape[-1]
    e = h // g
    nc = s // CHUNK
    xc = (xh.astype(jnp.float32) * dt[..., None]).reshape(b, nc, CHUNK, g, e, p)
    Bc = Bm.astype(jnp.float32).reshape(b, nc, CHUNK, g, n)
    Cc = Cm.astype(jnp.float32).reshape(b, nc, CHUNK, g, n)
    a = (dt * A).reshape(b, nc, CHUNK, g, e).transpose(0, 3, 4, 1, 2)
    a_cs = jnp.cumsum(a, axis=-1)
    decay_in = jnp.exp(segsum(a))
    cb = jnp.einsum('bclgn,bcsgn->bgcls', Cc, Bc)
    scores = cb[:, :, None] * decay_in
    y_diag = jnp.einsum('bgecls,bcsgep->bclgep', scores, xc)
    decay_to_end = jnp.exp(a_cs[..., -1:] - a_cs).transpose(0, 3, 4, 1, 2)
    states = jnp.einsum('bclgn,bclgep->bcgepn', Bc, xc * decay_to_end[..., None])
    chunk_tot = jnp.pad(a_cs[..., -1], [(0, 0), (0, 0), (0, 0), (1, 0)])
    decay_chunk = jnp.exp(segsum(chunk_tot))
    states = jnp.concatenate([jnp.zeros_like(states[:, :1]), states], axis=1)
    new_states = jnp.einsum('bgezc,bcgepn->bzgepn', decay_chunk, states)
    prev_states = new_states[:, :-1]
    decay_out = jnp.exp(a_cs).transpose(0, 3, 4, 1, 2)
    y_off = jnp.einsum('bclgn,bcgepn->bclgep', Cc, prev_states) * decay_out[..., None]
    return (y_diag + y_off).reshape(b, s, h, p)

def forgetting_attention(q, k, v, log_f):
    s, d = q.shape[1], q.shape[-1]
    scale = d ** -0.5
    cum = jnp.cumsum(log_f, axis=1).transpose(0, 2, 1)
    outs = []
    for i in range(s // Q_BLOCK):
        q0, q1 = i * Q_BLOCK, (i + 1) * Q_BLOCK
        logits = jnp.einsum('bqhd,bkhd->bhqk', q[:, q0:q1], k[:, :q1],
                            preferred_element_type=jnp.float32) * scale
        logits = logits + (cum[:, :, q0:q1, None] - cum[:, :, None, :q1])
        mask = jnp.arange(q0, q1)[:, None] >= jnp.arange(q1)[None, :]
        logits = jnp.where(mask, logits, -jnp.inf)
        probs = jax.nn.softmax(logits, axis=-1)
        outs.append(jnp.einsum('bhqk,bkhd->bqhd', probs.astype(v.dtype), v[:, :q1]))
    return jnp.concatenate(outs, axis=1)

def hybrid_mixer(h, w_in, conv_w, conv_b, dt_bias, a_log, d_skip, ssm_norm_w, f_bias,
                 attn_norm_w, w_out):
    b, s, _ = h.shape
    proj = jnp.einsum('bsd,dk->bsk', h, w_in)
    z, xbc, dt_raw, q, k, v, f_raw = jnp.split(proj, SPLITS, axis=-1)
    xbc = jax.nn.silu(causal_depthwise_conv(xbc, conv_w, conv_b))
    xs, Bm, Cm = jnp.split(xbc, [SSM_WIDTH, SSM_WIDTH + SSM_GROUPS * SSM_STATE], axis=-1)
    xs = xs.reshape(b, s, SSM_HEADS, SSM_HEAD_DIM)
    Bm = Bm.reshape(b, s, SSM_GROUPS, SSM_STATE)
    Cm = Cm.reshape(b, s, SSM_GROUPS, SSM_STATE)
    dt = jax.nn.softplus(dt_raw.astype(jnp.float32) + dt_bias)
    A = -jnp.exp(a_log.astype(jnp.float32))
    y = ssd_chunked(xs, dt, A, Bm, Cm) + d_skip[:, None] * xs
    y_ssm = rms_norm(y.reshape(b, s, SSM_WIDTH) * jax.nn.silu(z), ssm_norm_w)
    q = q.reshape(b, s, ATT_HEADS, ATT_HEAD_DIM)
    k = k.reshape(b, s, ATT_HEADS, ATT_HEAD_DIM)
    v = v.reshape(b, s, ATT_HEADS, ATT_HEAD_DIM)
    log_f = jax.nn.log_sigmoid(f_raw.astype(jnp.float32) + f_bias)
    y_att = forgetting_attention(q, k, v, log_f).reshape(b, s, ATT_WIDTH)
    y_att = rms_norm(y_att, attn_norm_w)
    y_mix = jnp.concatenate([y_ssm, y_att.astype(y_ssm.dtype)], axis=-1)
    return jnp.einsum('bsk,kd->bsd', y_mix.astype(h.dtype), w_out)

def first_inputs(seed: int = 0) -> dict:
    key = jax.random.key(seed)
    ks = jax.random.split(key, 24)
    f32 = jnp.float32
    nrm = lambda k, shape, s: jax.random.normal(k, shape, f32) * s
    dt0 = jnp.exp(jax.random.uniform(ks[6], (DEPTH, SSM_HEADS), f32,
                                     np.log(1e-3).astype(np.float32), np.log(1e-1).astype(np.float32)))
    return {
        "x": nrm(ks[0], (BATCH, SEQ, D_MODEL), 1.0),
        "c": nrm(ks[1], (BATCH, D_MODEL), 1.0),
        "w_ada": nrm(ks[2], (DEPTH, D_MODEL, 6 * D_MODEL), 0.5 * D_MODEL ** -0.5),
        "b_ada": nrm(ks[3], (DEPTH, 6 * D_MODEL), 0.01),
        "w_in": nrm(ks[4], (DEPTH, D_MODEL, IN_COLS), D_MODEL ** -0.5),
        "conv_w": nrm(ks[5], (DEPTH, CONV_WIDTH, CONV_DIM), CONV_WIDTH ** -0.5),
        "conv_b": nrm(ks[7], (DEPTH, CONV_DIM), 0.01),
        "dt_bias": dt0 + jnp.log(-jnp.expm1(-dt0)),
        "a_log": jnp.log(jax.random.uniform(ks[8], (DEPTH, SSM_HEADS), f32, 1.0, 16.0)),
        "d_skip": 1.0 + nrm(ks[9], (DEPTH, SSM_HEADS), 0.1),
        "ssm_norm_w": 1.0 + nrm(ks[10], (DEPTH, SSM_WIDTH), 0.05),
        "f_bias": jax.random.uniform(ks[11], (DEPTH, ATT_HEADS), f32, 1.0, 4.0),
        "attn_norm_w": 1.0 + nrm(ks[12], (DEPTH, ATT_WIDTH), 0.05),
        "w_out": nrm(ks[13], (DEPTH, MIX_WIDTH, D_MODEL), DEEPNORM_BETA * MIX_WIDTH ** -0.5),
        "ln1_g": 1.0 + nrm(ks[14], (DEPTH, D_MODEL), 0.05),
        "ln1_b": nrm(ks[15], (DEPTH, D_MODEL), 0.01),
        "w_ff_in": nrm(ks[16], (DEPTH, D_MODEL, D_FF), D_MODEL ** -0.5),
        "w_ff_out": nrm(ks[17], (DEPTH, D_FF, D_MODEL), DEEPNORM_BETA * D_FF ** -0.5),
        "ln2_g": 1.0 + nrm(ks[18], (DEPTH, D_MODEL), 0.05),
        "ln2_b": nrm(ks[19], (DEPTH, D_MODEL), 0.01),
    }

def first_block(x, c, w_ada, b_ada, w_in, conv_w, conv_b, dt_bias, a_log, d_skip, ssm_norm_w,
              f_bias, attn_norm_w, w_out, ln1_g, ln1_b, w_ff_in, w_ff_out, ln2_g, ln2_b):
    c_act = jax.nn.silu(c)
    for l in range(DEPTH):
        mod = jnp.einsum('bd,de->be', c_act, w_ada[l]) + b_ada[l]
        sh1, sc1, g1, sh2, sc2, g2 = [m[:, None, :] for m in jnp.split(mod, 6, axis=-1)]
        h = x * (1.0 + sc1) + sh1
        y = hybrid_mixer(h, w_in[l], conv_w[l], conv_b[l], dt_bias[l], a_log[l], d_skip[l],
                         ssm_norm_w[l], f_bias[l], attn_norm_w[l], w_out[l])
        x = layer_norm(DEEPNORM_ALPHA * x + (1.0 + g1) * y, ln1_g[l], ln1_b[l])
        h = x * (1.0 + sc2) + sh2
        ff = jnp.einsum('bsf,fd->bsd',
                        jnp.square(jax.nn.relu(jnp.einsum('bsd,df->bsf', h, w_ff_in[l]))),
                        w_ff_out[l])
        x = layer_norm(DEEPNORM_ALPHA * x + (1.0 + g2) * ff, ln2_g[l], ln2_b[l])
    return x


CHUNK_2 = 64
N_PREV_CHUNKS = 8
BAND = N_PREV_CHUNKS + 1

D_MIX = D_MODEL
HEAD_DIM = 64
ATTN_WIDTH = D_MIX // 2
N_ATTN_HEADS = ATTN_WIDTH // HEAD_DIM
CONV_WIDTH_2 = D_MIX // 4
CONV_K = 3
POOL_WIDTH = D_MIX - ATTN_WIDTH - CONV_WIDTH_2
POOL_WINDOWS = (2, 4, 8, 16)
N_POOL_GROUPS = len(POOL_WINDOWS)
POOL_GROUP = POOL_WIDTH // N_POOL_GROUPS
REL_CLIP = 128

D_IN = 3 * ATTN_WIDTH + 3 * CONV_WIDTH_2 + POOL_WIDTH
D_FF_2 = 4 * D_MODEL
EPS = 1e-6
NEG_INF = -1e30


def rms_norm_2(x, g):
    x32 = x.astype(jnp.float32)
    y = x32 * lax.rsqrt(jnp.mean(x32 * x32, axis=-1, keepdims=True) + EPS)
    return (y * g.astype(jnp.float32)).astype(x.dtype)

def chunked_band_attention(q, k, v, rel_bias):
    b, s, h, d = q.shape
    nc = s // CHUNK_2
    qc = q.reshape(b, nc, CHUNK_2, h, d)
    pad = ((0, 0), (N_PREV_CHUNKS, 0), (0, 0), (0, 0), (0, 0))
    kp = jnp.pad(k.reshape(b, nc, CHUNK_2, h, d), pad)
    vp = jnp.pad(v.reshape(b, nc, CHUNK_2, h, d), pad)
    band_idx = jnp.arange(nc)[:, None] + jnp.arange(BAND)[None, :]
    kb = kp[:, band_idx].reshape(b, nc, BAND * CHUNK_2, h, d)
    vb = vp[:, band_idx].reshape(b, nc, BAND * CHUNK_2, h, d)
    scores = jnp.einsum('bnqhd,bnkhd->bnhqk', qc, kb).astype(jnp.float32) * (d ** -0.5)
    qi = jnp.arange(CHUNK_2)[:, None]
    kj = jnp.arange(BAND * CHUNK_2)[None, :]
    dist = qi + N_PREV_CHUNKS * CHUNK_2 - kj
    bias = rel_bias[:, jnp.clip(dist, -REL_CLIP, REL_CLIP) + REL_CLIP].astype(jnp.float32)
    valid = jnp.repeat(band_idx >= N_PREV_CHUNKS, CHUNK_2, axis=1)
    scores = jnp.where(valid[None, :, None, None, :], scores + bias[None, None], NEG_INF)
    p = jax.nn.softmax(scores, axis=-1).astype(v.dtype)
    out = jnp.einsum('bnhqk,bnkhd->bnqhd', p, vb)
    return out.reshape(b, s, h * d)

def gated_short_conv(gb, gc, hin, conv_w):
    z = gc * hin
    s = z.shape[1]
    zp = jnp.pad(z, ((0, 0), (CONV_K - 1, 0), (0, 0)))
    y = sum(conv_w[i] * zp[:, i:i + s] for i in range(CONV_K))
    return gb * y

def multiscale_pool(u, pool_w, pool_scale):
    b, s, c = u.shape
    u32 = u.astype(jnp.float32)
    cs = jnp.concatenate([jnp.zeros((b, 1, c), jnp.float32), jnp.cumsum(u32, axis=1)], axis=1)
    pos1 = jnp.arange(s) + 1
    outs = []
    for g, w in enumerate(POOL_WINDOWS):
        sl = slice(g * POOL_GROUP, (g + 1) * POOL_GROUP)
        csg = cs[:, :, sl]
        lag = jnp.pad(csg[:, :s + 1 - w], ((0, 0), (w - 1, 0), (0, 0)))
        cnt = jnp.minimum(pos1, w).astype(jnp.float32)[None, :, None]
        m = (csg[:, 1:] - lag) / cnt - u32[:, :, sl]
        outs.append(jnp.einsum('bsc,cd->bsd', m.astype(u.dtype), pool_w[g]))
    return jnp.concatenate(outs, axis=-1) * pool_scale

def second_inputs(seed: int = 0) -> dict:
    key = jax.random.key(seed)
    ks = jax.random.split(key, 13)
    f32 = jnp.float32
    L = DEPTH
    x = jax.random.normal(ks[0], (BATCH, SEQ, D_MODEL), f32)
    norm1_g = 1.0 + 0.05 * jax.random.normal(ks[1], (L, D_MODEL), f32)
    w_in = jax.random.normal(ks[2], (L, D_MODEL, D_IN), f32) * D_MODEL ** -0.5
    q_norm_g = 1.0 + 0.05 * jax.random.normal(ks[3], (L, HEAD_DIM), f32)
    k_norm_g = 1.0 + 0.05 * jax.random.normal(ks[4], (L, HEAD_DIM), f32)
    rel_bias = 0.1 * jax.random.normal(ks[5], (L, N_ATTN_HEADS, 2 * REL_CLIP + 1), f32)
    conv_w = jax.random.normal(ks[6], (L, CONV_K, CONV_WIDTH_2), f32) * CONV_K ** -0.5
    pool_w = jax.random.normal(ks[7], (L, N_POOL_GROUPS, POOL_GROUP, POOL_GROUP), f32) * POOL_GROUP ** -0.5
    pool_scale = 0.5 + 0.1 * jax.random.normal(ks[8], (L, POOL_WIDTH), f32)
    w_out = jax.random.normal(ks[9], (L, D_MIX, D_MODEL), f32) * D_MIX ** -0.5
    norm2_g = 1.0 + 0.05 * jax.random.normal(ks[10], (L, D_MODEL), f32)
    w_mlp1 = jax.random.normal(ks[11], (L, D_MODEL, D_FF_2), f32) * D_MODEL ** -0.5
    w_mlp2 = jax.random.normal(ks[12], (L, D_FF_2, D_MODEL), f32) * D_FF_2 ** -0.5
    return {"x": x, "norm1_g": norm1_g, "w_in": w_in, "q_norm_g": q_norm_g,
            "k_norm_g": k_norm_g, "rel_bias": rel_bias, "conv_w": conv_w,
            "pool_w": pool_w, "pool_scale": pool_scale, "w_out": w_out,
            "norm2_g": norm2_g, "w_mlp1": w_mlp1, "w_mlp2": w_mlp2}

def second_block(x, norm1_g, w_in, q_norm_g, k_norm_g, rel_bias, conv_w, pool_w,
              pool_scale, w_out, norm2_g, w_mlp1, w_mlp2):
    b, s, _ = x.shape
    a = ATTN_WIDTH
    c = CONV_WIDTH_2
    for l in range(DEPTH):
        h = rms_norm_2(x, norm1_g[l])
        p = jnp.einsum('bsd,de->bse', h, w_in[l])
        q = p[..., 0:a].reshape(b, s, N_ATTN_HEADS, HEAD_DIM)
        k = p[..., a:2 * a].reshape(b, s, N_ATTN_HEADS, HEAD_DIM)
        v = p[..., 2 * a:3 * a].reshape(b, s, N_ATTN_HEADS, HEAD_DIM)
        o = 3 * a
        gb = p[..., o:o + c]
        gc = p[..., o + c:o + 2 * c]
        hin = p[..., o + 2 * c:o + 3 * c]
        u = p[..., o + 3 * c:]
        q = rms_norm_2(q, q_norm_g[l])
        k = rms_norm_2(k, k_norm_g[l])
        y_attn = chunked_band_attention(q, k, v, rel_bias[l])
        y_conv = gated_short_conv(gb, gc, hin, conv_w[l])
        y_pool = multiscale_pool(u, pool_w[l], pool_scale[l])
        mix = jnp.concatenate([y_attn, y_conv, y_pool], axis=-1)
        x = x + jnp.einsum('bse,ed->bsd', mix, w_out[l])
        h2 = rms_norm_2(x, norm2_g[l])
        f = jnp.square(jax.nn.relu(jnp.einsum('bsd,df->bsf', h2, w_mlp1[l])))
        x = x + jnp.einsum('bsf,fd->bsd', f, w_mlp2[l])
    return x


def setup_inputs(seed=0):
    out = dict(first_inputs(seed))
    for name, value in second_inputs(seed + 1).items():
        if name != "x":
            out[name + "_2"] = value
    return out


def reference(
    x, c, w_ada, b_ada, w_in, conv_w, conv_b, dt_bias, a_log, d_skip, ssm_norm_w, f_bias,
    attn_norm_w, w_out, ln1_g, ln1_b, w_ff_in, w_ff_out, ln2_g, ln2_b, norm1_g_2, w_in_2,
    q_norm_g_2, k_norm_g_2, rel_bias_2, conv_w_2, pool_w_2, pool_scale_2, w_out_2, norm2_g_2,
    w_mlp1_2, w_mlp2_2,
):
    x = first_block(
        x, c, w_ada, b_ada, w_in, conv_w, conv_b, dt_bias, a_log, d_skip, ssm_norm_w, f_bias,
        attn_norm_w, w_out, ln1_g, ln1_b, w_ff_in, w_ff_out, ln2_g, ln2_b,
    )
    return second_block(
        x, norm1_g_2, w_in_2, q_norm_g_2, k_norm_g_2, rel_bias_2, conv_w_2, pool_w_2,
        pool_scale_2, w_out_2, norm2_g_2, w_mlp1_2, w_mlp2_2,
    )


_drawn_inputs = setup_inputs


def setup_inputs(seed=0):
    import zlib

    import numpy as np

    out = dict(_drawn_inputs(seed))
    spreads = {}
    factors = {'b_ada': 2.808,
     'conv_b': 8.0,
     'ssm_norm_w': 2.728,
     'ln1_b': 4.015,
     'ln2_b': 4.179,
     'q_norm_g_2': 8.0,
     'k_norm_g_2': 8.0,
     'rel_bias_2': 8.0}
    for name, (base, spread) in spreads.items():
        noise = np.random.default_rng([zlib.crc32(name.encode()), seed]).standard_normal(out[name].shape)
        drawn = base * np.exp(spread * noise) if base else spread * noise
        out[name] = __import__('jax').numpy.asarray(drawn.astype(out[name].dtype))
    for name, factor in factors.items():
        out[name] = (out[name] * factor).astype(out[name].dtype)
    return out
```

```python
from contextlib import ExitStack

import numpy as np

import concourse.bass as bass
from concourse import mybir

F32 = mybir.dt.float32
F32R = mybir.dt.float32r
ALU = mybir.AluOpType
ACT = mybir.ActivationFunctionType
AX = mybir.AxisListType.X

P = 128
S = 512
D = 1024
TB = S // P
KT = D // P
SSM_W, SSM_H, HD, ST = 1024, 16, 64, 128
CONV_DIM = SSM_W + 2 * 2 * ST
CT = CONV_DIM // P
CW = 4
C_Z, C_XBC = 0, SSM_W
C_DT = C_XBC + CONV_DIM
C_Q = C_DT + SSM_H
C_K, C_V = C_Q + 1024, C_Q + 2048
C_F = C_Q + 3072
ALPHA = 2.0 ** 0.25
LN_EPS, RMS_EPS, EPS2 = 1e-5, 1e-5, 1e-6
FF = 4096
QUARTERS = FF // D
NEG = -1e30
H2 = 8
CLIP = 128
NREL = 2 * CLIP + 1
SB = [(4, 384), (6, 0), (4, 0), (5, 0)]
QO = [0, 128, 384, 768]

U_DTF = 0
U_Z = 1
U_XBC = U_Z + 4
U_WO1 = U_XBC + 6
U_V = U_WO1 + 4
U_QK = U_V + 4
U_WO2 = U_QK + 8
U_FF1 = U_WO2 + 4
U_QKV2 = U_FF1 + 8 * QUARTERS
U_CP = U_QKV2 + 6
U_WO3 = U_CP + 4
U_FF2 = U_WO3 + 4
UNITS = U_FF2 + 8 * QUARTERS
N_Z = (0, 0)
N_XBC = (1, 1)
N_WO1 = (4, 1)
N_V = (5, 2)
N_QK = (6, 3)
N_WO2 = (10, 3)
N_FF1 = (11, 4)
N_QKV2 = (N_FF1[0] + 2 * QUARTERS, N_FF1[1] + 2 * QUARTERS)
N_CP = (N_QKV2[0] + 2, N_QKV2[1] + 1)
N_WO3 = (N_CP[0] + 1, N_CP[1] + 1)
N_FF2 = (N_WO3[0] + 1, N_WO3[1] + 1)
T_H, T_SSM, T_ATT, T_X1 = 0, 8, 16, 24
T_HID1 = 32
T_N2 = T_HID1 + 32
T_MIX = T_N2 + 8
R_H, R_SSM, R_ATT, R_X1, R_N2, R_ATT2, R_N3 = 0, 8, 16, 24, 32, 40, 44
T_N3 = T_MIX + 8
T_HID2 = T_N3 + 8


class Link:

    def __init__(self, eng, sem):
        self.eng, self.sem, self.n, self.extra = eng, sem, 0, 0

    def __call__(self, ins):
        self.n += 1
        ins.then_inc(self.sem, 1)
        self.eng.wait_ge(self.sem, self.extra + self.n)

    def enter(self, i, per):
        self.start, self.per, self.extra = self.n, per, i * per

    def leave(self, times):
        assert self.n - self.start == self.per, (self.n - self.start, self.per)
        self.n, self.extra = self.start + times * self.per, 0


def build(nc, x, c, w_ada, b_ada, w_in, conv_w, conv_b, dt_bias, a_log, d_skip, ssm_norm_w, f_bias,
          attn_norm_w, w_out, ln1_g, ln1_b, w_ff_in, w_ff_out, ln2_g, ln2_b, norm1_g_2, w_in_2,
          q_norm_g_2, k_norm_g_2, rel_bias_2, conv_w_2, pool_w_2, pool_scale_2, w_out_2, norm2_g_2,
          w_mlp1_2, w_mlp2_2, out):
    with ExitStack() as ctx:
        def sb(name, shape, dt=F32):
            return ctx.enter_context(nc.sbuf_tensor(name, shape, dt))

        def sem(name):
            return ctx.enter_context(nc.semaphore(name))

        bank = [ctx.enter_context(nc.psum_tensor(f"bank{b}", [P, 512], F32)) for b in range(8)]

        raw = sb("raw", [P, 2, 2048])
        w_hi = sb("w_hi", [P, 2, 2048], F32R)
        w_lo = sb("w_lo", [P, 2, 2048], F32R)
        a_hi = [sb(f"a_hi{n}", [P, KT, S], F32R) for n in range(2)]
        a_lo = [sb(f"a_lo{n}", [P, KT, S], F32R) for n in range(2)]
        tmp = sb("tmp", [P, 2, S])
        arena = sb("arena", [P, 22528])

        def view(at, *dims):
            n = int(np.prod(dims))
            v = arena[:, at:at + n]
            if len(dims) == 2:
                v = v.rearrange("p (a b) -> p a b", a=dims[0])
            elif len(dims) == 3:
                v = v.rearrange("p (a b c) -> p a b c", a=dims[0], b=dims[1])
            return v

        xtok = view(15360, TB, D)
        ada = view(4096, 4, 8, 256)
        z_y = view(0, TB, D)
        xbc = view(4096, CT, S)
        dtf = view(19456, 6, S)
        xs = view(10240, TB, D)
        btok = view(14336, TB, 2, ST)
        bc = view(15360, 2, 16, P)
        yc = view(19456, 1024)
        xd = view(20480, 1024)
        prev = view(21504, 1024)
        cbm = view(4096, 4, 2 * P)
        off = view(5120, 1024)
        yacc = view(10240, TB, D)
        vtok = view(0, TB, D)
        att = view(4096, TB, D)
        ncb = view(8192, 2, S)
        ncm = view(9216, 2, S)
        qk = view(14336, 2, 4, S)
        prob = view(18432, 2, 1280)
        probT = view(20992, 1280)
        xre = view(0, TB, D)
        x1 = view(14336, TB, D)
        row = view(18432, 3, D)
        rl = view(0, 2, S)
        n2 = view(0, TB, D)
        qkv2 = view(4096, 3, TB, 512)
        sq2 = view(0, TB, 512)
        qkT2 = view(10240, 2, 4, S)
        cp = view(18432, 8, S)
        relt = view(2048, 2, H2, P)
        prob2 = view(4096, 2, 1280)
        prob2T = view(6656, 1280)
        att2 = view(0, TB, 512)

        ident = sb("ident", [P, P])
        flip = sb("flip", [P, P])
        masks = sb("masks", [P, 2, P])
        keep = masks[:, 0]
        hide = masks[:, 1]
        poolw = masks
        ones = sb("ones", [P, P])
        vec_in = view(14336, 2, P)
        vec = sb("vec", [P, 2, P])
        cact = sb("cact", [P, KT])
        mod = sb("mod", [P, 48])
        col64 = sb("col64", [64, 4])
        dsk = sb("dsk", [P, SSM_H])
        dta = view(6144, 8, 64)
        ex = sb("ex", [P, 3, SSM_H])
        st = sb("st", [P, 64])
        st2 = sb("st2", [P, 64])
        stat = sb("stat", [P, 8, 6])
        mv = sb("mv", [P, TB, 2])
        nhalf = sb("nhalf", [P, 64])
        relc = sb("relc", [P, H2])
        pinv = sb("pinv", [P, 2, 16])
        acs_d = nc.dram_tensor("acs_d", (16, S), F32).ap()
        ncum_d = nc.dram_tensor("ncum_d", (16, S), F32).ap()
        ext_d = nc.dram_tensor("ext_d", (H2, 512), F32).ap()

        v0, v1 = vec[:, 0, :], vec[:, 1, :]
        V_BADA, V_CONVW, V_CONVB, V_SSM = 0, 48, 96, 108
        V_ATT, V_N1, V_N2, V_CW2, V_PS, V_QG, V_KG, V_C = 0, 8, 16, 24, 30, 32, 33, 34
        V1_ROWS = 42

        mxs, rsum, rinv = sb("mxs", [P, 2, 4]), sb("rsum", [P, 2, 4]), sb("rinv", [P, 2, 4])

        landed = [sem("landed0"), sem("landed1")]
        w_hi_made, w_lo_made, ticks = sem("w_hi_made"), sem("w_lo_made"), sem("ticks")
        evac = [sem("evac0"), sem("evac1")]
        turned = sem("turned")
        tile_made, a_hi_made, a_lo_made = sem("tile_made"), sem("a_hi_made"), sem("a_lo_made")
        dve_link, act_link, pool_link = sem("dve_link"), sem("act_link"), sem("pool_link")
        cleared, consts = sem("cleared"), sem("consts")
        vecs_in, vecs_t, vecs_made, c_made = sem("vecs_in"), sem("vecs_t"), sem("vecs_made"), sem("c_made")
        x_in, small_in, mod_made, ada_used = sem("x_in"), sem("small_in"), sem("mod_made"), sem("ada_used")
        ada_in = [sem(f"ada_in{n}") for n in range(4)]
        dtf_abs, dtf_exp, a_col, scanned = sem("dtf_abs"), sem("dtf_exp"), sem("a_col"), sem("scanned")
        acs_out, cum_out, dta_t, dta_made = sem("acs_out"), sem("cum_out"), sem("dta_t"), sem("dta_made")
        conv_act, xs_t, xs_made, cb_done, cb_evac = sem("conv_act"), sem("xs_t"), sem("xs_made"), sem("cb_done"), sem("cb_evac")
        bc_in = [sem("bc_in0"), sem("bc_in1")]
        bc_sub, bc_exp, score_made = sem("bc_sub"), sem("bc_exp"), sem("score_made")
        ex_in, ex_made, xc_made, xd_made = sem("ex_in"), sem("ex_made"), sem("xc_made"), sem("xd_made")
        y_mm, st_mm, prev_made, y_made = sem("y_mm"), sem("st_mm"), sem("prev_made"), sem("y_made")
        y_sq, rs_made, y_norm = sem("y_sq"), sem("rs_made"), sem("y_norm")
        ncb_in = [sem("ncb_in0"), sem("ncb_in1")]
        ncm_made, s_mm, s_made, mx_made, p_made = sem("ncm_made"), sem("s_mm"), sem("s_made"), sem("mx_made"), sem("p_made")
        pt_t, pt_made, o_mm, o_made = sem("pt_t"), sem("pt_made"), sem("o_mm"), sem("o_made")
        rows_in, g_mm, g_made, xre_in, acc0 = sem("rows_in"), sem("g_mm"), sem("g_made"), sem("xre_in"), sem("acc0")
        ln_var, ln_rs, ln_made, sum_made = sem("ln_var"), sem("ln_rs"), sem("ln_made"), sem("sum_made")
        qk_sq, qk_rs, qk_made, q2_t, q2_made = sem("qk_sq"), sem("qk_rs"), sem("qk_made"), sem("q2_t"), sem("q2_made")
        ext_out, rel_in, rel_made, pool_in = sem("ext_out"), sem("rel_in"), sem("rel_made"), sem("pool_in")
        m_made, m_mm, out_sent = sem("m_made"), sem("m_mm"), sem("out_sent")

        w_in_v = w_in[0].rearrange("(k p) n -> p k n", p=P)
        w_ada_v = w_ada[0].rearrange("(k p) n -> p k n", p=P)
        w_out_v = w_out[0].rearrange("(k p) n -> p k n", p=P)
        w_in2_v = w_in_2[0].rearrange("(k p) n -> p k n", p=P)
        w_out2_v = w_out_2[0].rearrange("(k p) n -> p k n", p=P)
        ff_v = [(w_ff_in[0].rearrange("(k p) n -> p k n", p=P), w_ff_out[0].rearrange("(k p) n -> p k n", p=P)),
                (w_mlp1_2[0].rearrange("(k p) n -> p k n", p=P), w_mlp2_2[0].rearrange("(k p) n -> p k n", p=P))]
        x_v = x[0].rearrange("(t p) d -> p t d", p=P)
        out_v = out[0].rearrange("(t p) d -> p t d", p=P)
        block = ctx.enter_context(nc.Block())

        def rows_of(vector, n):
            return vector.rearrange("a (k p) -> (a k) p", k=n)


        def at(i, per, const):
            return i * per + const

        @block.sync
        def _(sp):
            def load(i, per, u0, src, k):
                if not (isinstance(i, int) and i * per + u0 < 2):
                    sp.wait_ge(w_lo_made, at(i, per, u0 - 1))
                sp.dma_start(raw[:, u0 % 2].rearrange("p (k n) -> p k n", k=k), src).then_inc(landed[u0 % 2], 16)

            def columns(i, per, u0, w, col):
                load(i, per, u0, w[:, :, bass.ds(col, 256)], 8)

            def rows(i, per, u0, w, k, col):
                load(i, per, u0, w[:, bass.ds(k, 4), bass.ds(col, 512)], 4)

            def four_rows(u0, w, k0, col0):
                for b in range(4):
                    rows(0, 0, u0 + b, w, k0 + 4 * (b % 2), col0 + 512 * (b // 2))

            def prelude():
                sp.wait_ge(cleared, 1)
                for at_, src, n, side in ((V_C, c, KT, 1), (V_BADA, b_ada, 48, 0), (V_CONVB, conv_b, CT, 0),
                                          (V_SSM, ssm_norm_w, KT, 0), (V_ATT, attn_norm_w, KT, 1), (V_N1, norm1_g_2, KT, 1),
                                          (V_N2, norm2_g_2, KT, 1), (V_PS, pool_scale_2, 2, 1)):
                    sp.dma_start(vec_in[at_:at_ + n, side, :], src.rearrange("a (k p) -> (a k) p", k=n)).then_inc(vecs_in, 16)
                sp.dma_start(vec_in[V_CONVW:V_CONVW + 48, 0, :], conv_w[0].rearrange("i (k p) -> (i k) p", p=P)).then_inc(vecs_in, 16)
                sp.dma_start(vec_in[V_CW2:V_CW2 + 6, 1, :], conv_w_2[0].rearrange("i (k p) -> (i k) p", p=P)).then_inc(vecs_in, 16)
                for at_, src in ((V_QG, q_norm_g_2), (V_KG, k_norm_g_2)):
                    for half in range(2):
                        sp.dma_start(vec_in[at_:at_ + 1, 1, half * HD:half * HD + HD], src).then_inc(vecs_in, 16)
                sp.dma_start(xtok, x_v).then_inc(x_in, 16)
                for n in range(4):
                    sp.dma_start(ada[:, n], w_ada_v[:, :, n * 256:n * 256 + 256]).then_inc(ada_in[n], 16)
                with sp.Fori(1, 6) as i:
                    for n in range(4):
                        sp.wait_ge(ada_used, at(i, 4, n - 3))
                        sp.dma_start(ada[:, n], w_ada_v[:, :, bass.ds(i * 1024 + n * 256, 256)]).then_inc(ada_in[n], 16)
                sp.wait_ge(cleared, 3)
                unit = raw[:, 0].rearrange("p (k n) -> p k n", k=8)
                sp.dma_start(unit[:, :, 0:16], w_in_v[:, :, C_DT:C_DT + 16]).then_inc(landed[0], 16)
                sp.dma_start(unit[:, :, 32:48], w_in_v[:, :, C_F:C_F + 16]).then_inc(landed[0], 16)
                for dst, src in ((col64[0:16, 0:1], dt_bias), (col64[32:48, 0:1], f_bias), (col64[0:16, 2:3], a_log)):
                    sp.dma_start(dst, src.rearrange("a h -> h a")).then_inc(small_in, 16)
                sp.dma_start(dsk[:, :], bass.AP(d_skip.tensor, 0, [[0, P], [1, SSM_H]])).then_inc(small_in, 16)

            def feed_forward(u0, w1, w2):
                with sp.Fori(0, QUARTERS) as i:
                    for b in range(4):
                        columns(i, 8, u0 + b, w1, at(i, D, 256 * b))
                    for b in range(4):
                        rows(i, 8, u0 + 4 + b, w2, at(i, 8, 4 * (b % 2)), 512 * (b // 2))

            prelude()
            four_rows(U_Z, w_in_v, 0, C_Z)
            with sp.Fori(0, 3) as i:
                for b in range(2):
                    columns(i, 2, U_XBC + b, w_in_v, at(i, 512, C_XBC + 256 * b))
            four_rows(U_WO1, w_out_v, 0, 0)
            four_rows(U_V, w_in_v, 0, C_V)
            with sp.Fori(0, 4) as i:
                columns(i, 2, U_QK, w_in_v, at(i, 256, C_Q))
                columns(i, 2, U_QK + 1, w_in_v, at(i, 256, C_K))
            four_rows(U_WO2, w_out_v, KT, 0)
            feed_forward(U_FF1, *ff_v[0])
            four_rows(U_QKV2, w_in2_v, 0, 0)
            for b in range(2):
                rows(0, 0, U_QKV2 + 4 + b, w_in2_v, 4 * b, 1024)
            for b in range(4):
                columns(0, 0, U_CP + b, w_in2_v, 1536 + 256 * b)
            four_rows(U_WO3, w_out2_v, 0, 0)
            feed_forward(U_FF2, *ff_v[1])
            for s in range(2):
                sp.wait_ge(evac[s], 4 * (N_FF2[s] + 2 * QUARTERS))
            sp.dma_start(out_v, x1).then_inc(out_sent, 16)
            sp.wait_ge(out_sent, 16)

        @block.gpsimd
        def _(pool):
            link = Link(pool, pool_link)

            def constants():
                pool.memset(vec_in[:], 0.0).then_inc(cleared, 1)
                pool.memset(raw[:, 0], 0.0).then_inc(cleared, 1)
                pool.memset(col64[:], 0.0).then_inc(cleared, 1)
                for m in (ident[:], flip[:], hide):
                    link(pool.memset(m, 0.0))
                link(pool.memset(keep, 1.0))
                pool.memset(ones[:], 1.0).then_inc(consts, 1)
                pool.affine_select(out=ident[:], in_=ident[:], compare_op=ALU.not_equal, fill=1.0, base=0,
                                   pattern=[[-1, P]], channel_multiplier=1).then_inc(consts, 1)
                pool.affine_select(out=flip[:], in_=flip[:], compare_op=ALU.not_equal, fill=1.0, base=1 - P,
                                   pattern=[[1, P]], channel_multiplier=1).then_inc(consts, 1)
                pool.affine_select(out=keep, in_=keep, compare_op=ALU.is_ge, fill=0.0, base=0,
                                   pattern=[[1, P]], channel_multiplier=-1).then_inc(consts, 1)
                pool.affine_select(out=hide, in_=hide, compare_op=ALU.is_ge, fill=NEG, base=0,
                                   pattern=[[-1, P]], channel_multiplier=1).then_inc(consts, 1)
                pool.memset(nhalf[:], -0.5).then_inc(consts, 1)
                pool.wait_ge(cleared, 3)
                link(pool.memset(col64[0:32, 1:2], 1.0))
                link(pool.memset(col64[32:64, 1:2], -1.0))
                pool.memset(col64[:, 3:4], 1.0).then_inc(consts, 1)

            def inv_root(n, src, dst, scale, eps, signal):
                link(pool.tensor_scalar(st2[:, 0:n], src, scale, eps, ALU.mult, ALU.add))
                pool.tensor_tensor(dst, st2[:, 0:n], nhalf[:, 0:n], ALU.pow).then_inc(signal, 1)

            def rms_root(turn, eps):
                pool.wait_ge(y_sq, 4 * turn + 4)
                inv_root(4, st[:, 0:4], st[:, 4:8], 1.0 / D, eps, rs_made)

            def ln_root(turn):
                pool.wait_ge(ln_var, 4 * turn + 4)
                inv_root(4, mv[:, :, 1], st[:, 8:12], 1.0, LN_EPS, ln_rs)

            def ssd_rows():
                pool.wait_ge(scanned, 5)
                pool.dma_start(acs_d, dtf[0:16, 1, :]).then_inc(acs_out, 16)
                pool.dma_start(ncum_d, dtf[32:48, 1, :]).then_inc(cum_out, 16)
                pool.wait_ge(acs_out, 16)
                pool.wait_ge(a_lo_made, T_H + 8)
                for ch in range(TB):
                    if ch >= 2:
                        pool.wait_ge(y_mm, ch - 1)
                    pool.dma_start(bc[:, ch % 2], bass.AP(acs_d.tensor, ch * P, [[0, P], [S, 16], [1, P]]))\
                        .then_inc(bc_in[ch % 2], 16)

            def fox_rows():
                pool.wait_ge(cum_out, 16)
                pool.wait_ge(turned, R_SSM + 8)
                for h in range(16):
                    if h >= 2:
                        pool.wait_ge(s_made, h - 1)
                    pool.dma_start(ncb[:, h % 2], bass.AP(ncum_d.tensor, h * S, [[0, P], [1, S]]))\
                        .then_inc(ncb_in[h % 2], 16)
                    pool.wait_ge(ncb_in[h % 2], 16 * (h // 2 + 1))
                    pool.tensor_tensor(ncm[:, h % 2].rearrange("p (i k) -> p i k", i=TB),
                                       ncb[:, h % 2].rearrange("p (i k) -> p i k", i=TB),
                                       hide.unsqueeze(1).broadcast_to([P, TB, P]), ALU.add).then_inc(ncm_made, 1)

            def load_row(n, src):
                pool.dma_start(row[:, n], bass.AP(src.tensor, 0, [[0, P], [1, D]])).then_inc(rows_in, 16)

            def relative():
                rb = rel_bias_2.tensor
                pool.dma_start(ext_d[:, 0:NREL], rel_bias_2[0]).then_inc(ext_out, 16)
                pool.dma_start(ext_d[:, NREL:NREL + P].unsqueeze(2), bass.AP(rb, NREL - 1, [[NREL, H2], [0, P], [1, 1]]), allow_slow_non_contiguous=True).then_inc(ext_out, 16)
                pool.dma_start(relc[0:1, :].unsqueeze(2), bass.AP(rb, NREL - 1, [[0, 1], [NREL, H2], [1, 1]]), allow_slow_non_contiguous=True).then_inc(rel_in, 16)
                link(pool.memset(poolw[:], 0.0))
                for g in range(4):
                    po = HD * (g % 2)
                    pool.dma_start(poolw[po:po + HD, g // 2, po:po + HD], pool_w_2[0, g]).then_inc(pool_in, 16)
                pool.wait_ge(ext_out, 32)

            def relative_tiles():
                pool.wait_ge(turned, R_N2 + 8)
                for n in range(2):
                    pool.dma_start(relt[:, n], bass.AP(ext_d.tensor, 1 + CLIP * n, [[1, P], [512, H2], [1, P]]))\
                        .then_inc(rel_in, 16)
                pool.wait_ge(rel_in, 48)
                pool.memset(relt[0:64, 0, :, 0:64], NEG).then_inc(rel_made, 1)

            constants()
            ssd_rows()
            rms_root(0, RMS_EPS)
            fox_rows()
            rms_root(1, RMS_EPS)
            pool.wait_ge(o_made, 16)
            pool.dma_start(xre, x_v).then_inc(xre_in, 16)
            load_row(1, ln1_g)
            load_row(2, ln1_b)
            relative()
            pool.wait_ge(evac[0], 4 * (N_WO2[0] + 1))
            pool.wait_ge(evac[1], 4 * (N_WO2[1] + 1))
            pool.wait_ge(sum_made, 8)
            pool.memset(yacc, 0.0).then_inc(acc0, 1)
            ln_root(0)
            pool.wait_ge(ln_made, 4)
            load_row(1, ln2_g)
            load_row(2, ln2_b)
            ln_root(1)
            rms_root(2, EPS2)
            relative_tiles()
            pool.wait_ge(qk_sq, 2)
            inv_root(64, st[:, 0:64], st[:, 0:64], 1.0 / HD, EPS2, qk_rs)
            rms_root(3, EPS2)

        @block.scalar
        def _(act):
            link = Link(act, act_link)

            def hi(u0, i=0, per=0):
                act.wait_ge(landed[u0 % 2], at(i, 8 * per, 16 * (u0 // 2 + 1 + (u0 % 2 == 0))))
                if not (isinstance(i, int) and i * per + u0 < 2):
                    act.wait_ge(ticks, at(i, 2 * per, 2 * u0 - 2))
                act.activation(w_hi[:, u0 % 2], raw[:, u0 % 2], ACT.Copy).then_inc(w_hi_made, 1)

            def tile_hi(t0, buf, k, i=0, per=0):
                act.wait_ge(tile_made, at(i, per, t0 + 1))
                act.activation(a_hi[buf][:, k], tmp[:, t0 % 2], ACT.Copy).then_inc(a_hi_made, 1)

            def read_rows(u0, s, dst, func=ACT.Copy):
                for t in range(TB):
                    act.wait_ge(ticks, 2 * u0 + 3 + t // 2)
                    act.activation(dst(t), bank[4 * s + t][:], func).then_inc(evac[s], 1)

            def pair_rows(u0, s, dst, func=ACT.Copy):
                hi(u0 + 1)
                hi(u0 + 2)
                read_rows(u0, s, dst, func)

            def rms(turn, src, dst, after, n):
                for t in range(TB):
                    act.wait_ge(after, n(t))
                    act.activation(tmp[:].rearrange("p a b -> p (a b)"), src[:, t], ACT.Square,
                                   accum_out=st[:, t:t + 1]).then_inc(y_sq, 1)
                    act.wait_ge(y_sq, 4 * turn + t + 1)
                act.wait_ge(rs_made, turn + 1)
                for t in range(TB):
                    act.activation(dst[:, t], src[:, t], ACT.Copy, scale=st[:, 4 + t:5 + t]).then_inc(y_norm, 1)

            def probabilities(h, src, dst):
                act.wait_ge(mx_made, h + 1)
                if h >= 2:
                    act.wait_ge(o_made, h - 1)
                for q in range(TB):
                    n = (q + 1) * P
                    act.activation(dst[:, QO[q]:QO[q] + n], src(q), ACT.Exp, bias=mxs[:, h % 2, q:q + 1],
                                   accum_out=rsum[:, h % 2, q:q + 1]).then_inc(p_made, 1)

            def copy_probT(h, dst):
                if h:
                    act.wait_ge(o_mm, h)
                for m, (b, n) in enumerate(((7, 4), (2, 4), (3, 2))):
                    act.wait_ge(pt_t, 3 * h + m + 1)
                    act.activation(dst[:, 512 * m:512 * m + n * P], bank[b][:, 0:n * P], ACT.Copy).then_inc(pt_made, 1)

            def feed_forward(u0, t0, n0, i, last):
                for b in range(2):
                    for j in range(4):
                        if j % 2 == 0:
                            hi(u0 + 2 * b + j // 2 + 1, i, 8)
                        k = 4 * b + j
                        act.wait_ge(ticks, at(i, 16, 2 * (u0 + 2 * b) + j + 1))
                        act.wait_ge(tile_made, at(i, 8, t0 + k - 1))
                        act.activation(rl[:, k % 2], bank[4 * b + j][:], ACT.Relu).then_inc(evac[b], 1)
                        act.wait_ge(evac[b], at(i, 8, 4 * n0[b] + j + 1))
                        act.activation(a_hi[1][:, k], rl[:, k % 2], ACT.Square).then_inc(a_hi_made, 1)
                for b in range(4, 8):
                    if not (last and b >= 7):
                        hi(u0 + b + 1, i, 8)

            def g_row(turn, b):
                for half in range(2):
                    act.wait_ge(g_mm, 2 * turn + half + 1)
                    act.activation(row[:, 0, 512 * half:512 * half + 512], bank[b + half][:], ACT.Copy).then_inc(g_made, 1)

            act.wait_ge(vecs_made, 1)
            act.activation(cact[:], v1[:, V_C:V_C + KT], ACT.Silu).then_inc(c_made, 1)
            for k in range(KT):
                tile_hi(T_H + k, 0, k)
            hi(0)
            hi(1)
            act.wait_ge(small_in, 64)
            act.wait_ge(consts, 7)
            act.activation(col64[0:16, 3:4], col64[0:16, 2:3], ACT.Exp).then_inc(a_col, 1)
            act.wait_ge(dtf_abs, 1)
            act.activation(dtf[0:64, 2], dtf[0:64, 1], ACT.Exp, scale=-1.0).then_inc(dtf_exp, 1)
            for half in range(2):
                pair_rows(U_Z + 2 * half, half, lambda t: z_y[:, t, 512 * half:512 * half + 512], ACT.Silu)
            with act.Fori(0, 3) as i:
                for j in range(4):
                    if j % 2 == 0:
                        hi(U_XBC + j // 2 + 1, i, 2)
                    act.wait_ge(evac[0], at(i, 4, 4 * N_XBC[0] + j + 1))
                    tile = xbc[:, bass.ds(at(i, 4, j), 1), :].rearrange("p a b -> p (a b)")
                    act.activation(tile, tile, ACT.Silu).then_inc(conv_act, 1)
            for b in range(8):
                act.wait_ge(xs_t, b + 1)
                act.activation(xs[:, b // 2, 512 * (b % 2):512 * (b % 2) + 512], bank[b][:], ACT.Copy).then_inc(xs_made, 1)
            for b in range(2):
                act.wait_ge(xs_t, 9 + b)
                act.activation(btok[:, 2 * b:2 * b + 2].rearrange("p a b c -> p (a b c)"), bank[b][:], ACT.Copy).then_inc(xs_made, 1)
            for ch in range(TB):
                act.wait_ge(dta_made, 1)
                if ch:
                    act.wait_ge(y_made, ch)
                act.activation(ex[:, 0], dta[:, 4 + ch, 0:16], ACT.Exp).then_inc(ex_made, 1)
                act.wait_ge(bc_in[ch % 2], 16 * (ch // 2 + 1))
                act.activation(ex[:, 1], bc[:, ch % 2, :, P - 1], ACT.Exp).then_inc(ex_made, 1)
                act.wait_ge(ex_in, ch + 1)
                act.activation(ex[:, 2], ex[:, 2], ACT.Exp).then_inc(ex_made, 1)
                act.wait_ge(bc_sub, ch + 1)
                act.activation(bc[:, ch % 2], bc[:, ch % 2], ACT.Exp).then_inc(bc_exp, 1)
            rms(0, z_y, z_y, y_made, lambda t: t + 1)
            for k in range(KT):
                tile_hi(T_SSM + k, 1, k)
            for half in range(2):
                pair_rows(U_WO1 + 2 * half, half, lambda t: yacc[:, t, 512 * half:512 * half + 512])
            for half in range(2):
                pair_rows(U_V + 2 * half, half, lambda t: vtok[:, t, 512 * half:512 * half + 512])

            def qk_tile(g, j):
                act.wait_ge(ticks, 2 * (U_QK + 2 * g) + j + 1)
                act.activation(qk[:, g % 2, j], bank[j % 2][:], ACT.Copy, scale=HD ** -0.5 if j < 2 else 1.0).then_inc(evac[0], 1)

            for s in range(-4, 18):
                g, j = s // 4 + 1, s % 4
                if s >= 2:
                    copy_probT(s - 2, probT)
                if g < 4:
                    if j % 2 == 0:
                        hi(U_QK + 2 * g + j // 2 + 1)
                    qk_tile(g, j)
                if 0 <= s < 16:
                    probabilities(s, lambda q: prob[:, s % 2, QO[q]:QO[q] + (q + 1) * P], prob[:, s % 2])
            rms(1, att, att, o_made, lambda t: 16)
            g_row(0, 4)
            for k in range(KT):
                tile_hi(T_ATT + k, 1, k)
            for b in range(4):
                hi(U_WO2 + b + 1)
            for k in range(KT):
                tile_hi(T_X1 + k, 0, k)
            with act.Fori(0, QUARTERS) as i:
                feed_forward(U_FF1, T_HID1, N_FF1, i, False)
            g_row(1, 0)
            rms(2, x1, n2, ln_made, lambda t: 4 + t + 1)
            for k in range(KT):
                tile_hi(T_N2 + k, 0, k)
            for n in range(3):
                pair_rows(U_QKV2 + 2 * n, n % 2, lambda t: qkv2[:, n, t])
            for n in range(2):
                for j in range(4):
                    if j % 2 == 0:
                        hi(U_CP + 2 * n + j // 2 + 1)
                    act.wait_ge(ticks, 2 * (U_CP + 2 * n) + j + 1)
                    act.activation(cp[:, 4 * n + j], bank[4 * (1 - n) + j][:], ACT.Copy).then_inc(evac[1 - n], 1)
            for k in range(4):
                tile_hi(T_MIX + k, 1, 4 + k)
            for s in range(10):
                if s >= 2:
                    copy_probT(16 + s - 2, prob2T)
                if s < 8:
                    def score(q):
                        b, o = SB[q]
                        return bank[b][:, o:o + (q + 1) * P]
                    probabilities(16 + s, score, prob2[:, s % 2])
            for k in range(4):
                tile_hi(T_MIX + 4 + k, 1, k)
            for b in range(4):
                hi(U_WO3 + b + 1)
            act.wait_ge(evac[0], 4 * (N_WO3[0] + 1))
            rms(3, x1, n2, evac[1], lambda t: 4 * (N_WO3[1] + 1))
            for k in range(KT):
                tile_hi(T_N3 + k, 0, k)
            with act.Fori(0, QUARTERS - 1) as i:
                feed_forward(U_FF2, T_HID2, N_FF2, i, False)
            feed_forward(U_FF2, T_HID2, N_FF2, QUARTERS - 1, True)

        @block.vector
        def _(dve):
            link = Link(dve, dve_link)

            def lo(u0, i=0, per=0):
                dve.wait_ge(w_hi_made, at(i, per, u0 + 1))
                dve.tensor_tensor(w_lo[:, u0 % 2], raw[:, u0 % 2], w_hi[:, u0 % 2].bitcast(F32), ALU.subtract)\
                    .then_inc(w_lo_made, 1)

            def tile_lo(t0, buf, k, i=0, per=0):
                dve.wait_ge(a_hi_made, at(i, per, t0 + 1))
                dve.tensor_tensor(a_lo[buf][:, k], tmp[:, t0 % 2], a_hi[buf][:, k].bitcast(F32), ALU.subtract)\
                    .then_inc(a_lo_made, 1)

            def tmp_free(t0, i=0, per=0):
                if not (isinstance(i, int) and i * per + t0 < 2):
                    dve.wait_ge(a_lo_made, at(i, per, t0 - 1))

            def split_turned(t0, r0, buf, scale, bias, n=KT):
                for k in range(n + 1):
                    if k < n:
                        dve.wait_ge(turned, r0 + k + 1)
                        tmp_free(t0 + k)
                        dve.tensor_scalar(tmp[:, (t0 + k) % 2], bank[k][:], scale(k), bias(k), ALU.mult, ALU.add)\
                            .then_inc(tile_made, 1)
                    if k:
                        tile_lo(t0 + k - 1, buf, k - 1)

            def maxima(h, src):
                if h:
                    dve.wait_ge(mx_made, h)
                for q in range(TB):
                    ins = dve.reduce_max(rinv[:, 0, q:q + 1], src(q), AX)
                    link(ins)
                if h >= 2:
                    dve.wait_ge(p_made, 4 * (h - 1))
                dve.tensor_scalar(mxs[:, h % 2], rinv[:, 0], -1.0, None, ALU.mult).then_inc(mx_made, 1)

            def output(h, dst):
                dve.wait_ge(p_made, 4 * h + 4)
                if h:
                    dve.wait_ge(o_made, h)
                link(dve.reciprocal(rinv[:, 1], rsum[:, h % 2]))
                dve.wait_ge(o_mm, h + 1)
                dve.tensor_tensor(dst, bank[3][:, 256:512].rearrange("p (t d) -> p t d", t=TB),
                                  rinv[:, 1].unsqueeze(2).broadcast_to([P, TB, HD]), ALU.mult).then_inc(o_made, 1)

            def layer_norm(turn, t):
                for half in range(2):
                    link(dve.bn_stats(stat[:, 2 * t + half], x1[:, t, 512 * half:512 * half + 512]))
                dve.bn_aggr(mv[:, t], stat[:, 2 * t:2 * t + 2].rearrange("p a b -> p (a b)")).then_inc(ln_var, 1)

            def layer_scale(turn):
                dve.wait_ge(ln_rs, turn + 1)
                dve.wait_ge(rows_in, 32 * turn + 32)
                for t in range(TB):
                    link(dve.tensor_scalar(x1[:, t], x1[:, t], mv[:, t, 0:1], st[:, 8 + t:9 + t], ALU.subtract, ALU.mult))
                    link(dve.tensor_tensor(x1[:, t], x1[:, t], row[:, 1], ALU.mult))
                    dve.tensor_tensor(x1[:, t], x1[:, t], row[:, 2], ALU.add).then_inc(ln_made, 1)

            def feed_forward(u0, t0, n0, acc, i, last):
                for b in range(2):
                    for j in range(4):
                        k = 4 * b + j
                        if j % 2 == 0:
                            lo(u0 + 2 * b + j // 2 + 1, i, 8)
                        dve.wait_ge(evac[b], at(i, 8, 4 * n0[b] + j + 1))
                        tmp_free(t0 + k, i, 8)
                        dve.tensor_tensor(tmp[:, k % 2], rl[:, k % 2], rl[:, k % 2], ALU.mult).then_inc(tile_made, 1)
                        dve.wait_ge(tile_made, at(i, 8, t0 + k + 1))
                        tile_lo(t0 + k, 1, k, i, 8)
                for b in range(2):
                    for n in range(2):
                        if not (last and b == 1 and n == 1):
                            lo(u0 + 4 + 2 * b + n + 1, i, 8)
                    for t in range(TB):
                        dve.wait_ge(ticks, at(i, 16, 2 * (u0 + 4 + 2 * b) + 3 + t // 2))
                        dve.wait_ge(evac[b], at(i, 8, 4 * (n0[b] + 1) + t))
                        part = acc[:, t, 512 * b:512 * b + 512]
                        dve.tensor_tensor(part, bank[4 * b + t][:], part, ALU.add).then_inc(evac[b], 1)

            def start():
                dve.wait_ge(vecs_t, 1)
                dve.tensor_copy(vec[:].rearrange("p a b -> p (a b)"), bank[0][:, 0:256]).then_inc(vecs_made, 1)
                dve.wait_ge(vecs_made, 1)
                dve.wait_ge(ada_used, 24)
                link(dve.tensor_tensor(mod[:], bank[1][:, 0:48], v0[:, V_BADA:V_BADA + 48], ALU.add))
                link(dve.tensor_scalar(mod[:, 8:24], mod[:, 8:24], 1.0, None, ALU.add))
                dve.tensor_scalar(mod[:, 32:48], mod[:, 32:48], 1.0, None, ALU.add).then_inc(mod_made, 1)
                dve.wait_ge(mod_made, 1)
                split_turned(T_H, R_H, 0, lambda k: mod[:, 8 + k:9 + k], lambda k: mod[:, k:k + 1])

            def softplus():
                W = [dtf[0:64, n] for n in range(6)]
                dve.wait_ge(small_in, 64)
                dve.wait_ge(consts, 7)
                dve.wait_ge(a_col, 1)
                link(dve.tensor_scalar(col64[0:16, 3:4], col64[0:16, 3:4], -1.0, None, ALU.mult))
                dve.wait_ge(ticks, 2)
                link(dve.tensor_scalar(W[0], bank[7][0:64, :], col64[:, 0:1], col64[:, 1:2], ALU.add, ALU.mult))
                dve.scalar_tensor_tensor(W[1], W[0], -1.0, W[0], ALU.mult, ALU.max).then_inc(dtf_abs, 1)
                dve.wait_ge(dtf_exp, 1)
                link(dve.tensor_scalar(W[3], W[2], 2.0, None, ALU.add))
                link(dve.reciprocal(W[3], W[3]))
                link(dve.tensor_tensor(W[3], W[2], W[3], ALU.mult))
                link(dve.tensor_tensor(W[4], W[3], W[3], ALU.mult))
                link(dve.tensor_scalar(W[5], W[4], 1.0 / 19, None, ALU.mult))
                for n in range(17, 1, -2):
                    link(dve.scalar_tensor_tensor(W[5], W[5], 1.0 / n, W[4], ALU.add, ALU.mult))
                link(dve.scalar_tensor_tensor(W[5], W[5], 1.0, W[3], ALU.add, ALU.mult))
                link(dve.tensor_scalar(W[0], W[0], 0.0, None, ALU.max))
                link(dve.scalar_tensor_tensor(W[0], W[5], 2.0, W[0], ALU.mult, ALU.add))
                link(dve.tensor_scalar(W[2], W[0], col64[:, 3:4], None, ALU.mult))
                for ch in range(TB):
                    part = slice(ch * P, ch * P + P)
                    dve.tensor_tensor_scan(dtf[0:16, 1, part], ones[0:16, :], dtf[0:16, 2, part], 0.0,
                                           ALU.mult, ALU.add).then_inc(scanned, 1)
                dve.tensor_tensor_scan(dtf[32:48, 1, :], ones[32:48, 0:1].broadcast_to([16, S]), dtf[32:48, 2, :], 0.0,
                                       ALU.mult, ALU.add).then_inc(scanned, 1)

            def convolve(i):
                for j in range(4):
                    if j % 2 == 0:
                        lo(U_XBC + j // 2 + 1, i, 2)
                    dve.wait_ge(ticks, at(i, 4, 2 * U_XBC + j + 1))
                    tile = xbc[:, bass.ds(at(i, 4, j), 1), :].rearrange("p a b -> p (a b)")

                    def tap(n):
                        return v0[:, bass.ds(at(i, 4, V_CONVW + n * CT + j), 1)]

                    link(dve.tensor_scalar(tile, bank[j][:], tap(3), v0[:, bass.ds(at(i, 4, V_CONVB + j), 1)],
                                           ALU.mult, ALU.add))
                    for lag in (1, 2, 3):
                        ins = dve.scalar_tensor_tensor(tile[:, lag:], bank[j][:, 0:S - lag], tap(3 - lag),
                                                       tile[:, lag:], ALU.mult, ALU.add)
                        if lag < 3:
                            link(ins)
                        else:
                            ins.then_inc(evac[0], 1)

            def by_head(ap):
                return ap.rearrange("p (h d) -> p h d", d=HD)

            def per_head(ap):
                return ap.unsqueeze(2).broadcast_to([P, SSM_H, HD])

            def ssd():
                dve.wait_ge(dta_t, 1)
                dve.tensor_copy(dta[:].rearrange("p a b -> p (a b)"), bank[2][:]).then_inc(dta_made, 1)
                dve.wait_ge(dta_made, 1)
                for b in range(2):
                    dve.wait_ge(cb_done, b + 1)
                    dve.tensor_tensor(cbm[:, 2 * b:2 * b + 2].rearrange("p a (g l) -> p (a g) l", g=2),
                                      bank[3 + b][:].rearrange("p (a l) -> p a l", a=4),
                                      keep.unsqueeze(1).broadcast_to([P, 4, P]), ALU.mult).then_inc(cb_evac, 1)
                dve.wait_ge(cb_evac, 2)
                dve.wait_ge(xs_made, 10)
                dve.wait_ge(cum_out, 16)
                for ch in range(TB):
                    b = bc[:, ch % 2]
                    acs = dta[:, 4 + ch, 0:16]
                    dve.wait_ge(bc_in[ch % 2], 16 * (ch // 2 + 1))
                    if ch:
                        dve.wait_ge(y_made, ch)
                    dve.tensor_tensor(ex[:, 2], b[:, :, P - 1], acs, ALU.subtract).then_inc(ex_in, 1)
                    dve.wait_ge(ex_made, 3 * ch + 3)
                    link(dve.tensor_tensor(b, b, acs.unsqueeze(2).broadcast_to([P, SSM_H, P]), ALU.subtract))
                    dve.tensor_scalar(b, b, 0.0, None, ALU.min).then_inc(bc_sub, 1)
                    x_c = xs[:, ch]
                    if ch:
                        dve.wait_ge(st_mm, ch)
                    link(dve.tensor_tensor(by_head(yc), by_head(x_c), per_head(dsk[:]), ALU.mult))
                    dve.tensor_tensor(by_head(x_c), by_head(x_c), per_head(dta[:, ch, 0:16]), ALU.mult).then_inc(xc_made, 1)
                    dve.wait_ge(xc_made, ch + 1)
                    dve.tensor_tensor(by_head(xd), by_head(x_c), per_head(ex[:, 2]), ALU.mult).then_inc(xd_made, 1)
                    dve.wait_ge(bc_exp, ch + 1)
                    b4 = b.rearrange("p (g e) l -> p g e l", g=2)
                    c4 = cbm[:, ch].rearrange("p (g l) -> p g l", g=2).unsqueeze(2).broadcast_to([P, 2, 8, P])
                    dve.tensor_tensor(b4, b4, c4, ALU.mult).then_inc(score_made, 1)
                    dve.wait_ge(y_mm, ch + 1)
                    for g in range(2):
                        part = slice(512 * g, 512 * g + 512)
                        link(dve.tensor_tensor(yc[:, part], bank[g][:], yc[:, part], ALU.add))
                        if ch:
                            e = ex[:, 0, 8 * g:8 * g + 8].unsqueeze(2).broadcast_to([P, 8, HD])
                            link(dve.tensor_tensor(by_head(off[:, part]), by_head(bank[2 + g][:]), e, ALU.mult))
                            link(dve.tensor_tensor(yc[:, part], off[:, part], yc[:, part], ALU.add))
                    if ch < TB - 1:
                        dve.wait_ge(st_mm, ch + 1)
                        if ch:
                            link(dve.tensor_tensor(by_head(prev), by_head(prev), per_head(ex[:, 1]), ALU.mult))
                        for g in range(2):
                            part = slice(512 * g, 512 * g + 512)
                            if ch:
                                dve.tensor_tensor(prev[:, part], bank[4 + g][:], prev[:, part], ALU.add).then_inc(prev_made, 1)
                            else:
                                dve.tensor_copy(prev[:, part], bank[4 + g][:]).then_inc(prev_made, 1)
                        dve.wait_ge(prev_made, 2 * ch + 2)
                    dve.wait_ge(evac[0], 4)
                    dve.wait_ge(evac[1], 4)
                    dve.tensor_tensor(z_y[:, ch], yc, z_y[:, ch], ALU.mult).then_inc(y_made, 1)

            def fox_scores(h):
                dve.wait_ge(ncm_made, h + 1)
                if h >= 2:
                    dve.wait_ge(pt_t, 3 * (h - 1))
                dve.wait_ge(s_mm, h + 1)
                for q in range(TB):
                    b, o = SB[q]
                    dst = prob[:, h % 2, QO[q]:QO[q] + (q + 1) * P]
                    if q:
                        link(dve.tensor_tensor(dst[:, 0:q * P], bank[b][:, o:o + q * P], ncb[:, h % 2, 0:q * P], ALU.add))
                    ins = dve.tensor_tensor(dst[:, q * P:q * P + P], bank[b][:, o + q * P:o + q * P + P],
                                            ncm[:, h % 2, q * P:q * P + P], ALU.add)
                    if q < TB - 1:
                        link(ins)
                    else:
                        ins.then_inc(s_made, 1)
                dve.wait_ge(s_made, h + 1)
                maxima(h, lambda q: prob[:, h % 2, QO[q]:QO[q] + (q + 1) * P])

            def conv_pool():
                dve.wait_ge(evac[1], 4 * (N_CP[1] + 1))
                dve.wait_ge(evac[0], 4 * (N_CP[0] + 1))
                for n in range(2):
                    z, y = cp[:, 2 + n], tmp[:, n]
                    tmp_free(T_MIX + n)
                    link(dve.tensor_tensor(z, z, cp[:, 4 + n], ALU.mult))
                    link(dve.tensor_scalar(y, z, v1[:, V_CW2 + 4 + n:V_CW2 + 5 + n], None, ALU.mult))
                    for lag in (1, 2):
                        w = v1[:, V_CW2 + 4 - 2 * lag + n:V_CW2 + 5 - 2 * lag + n]
                        link(dve.scalar_tensor_tensor(y[:, lag:], z[:, 0:S - lag], w, y[:, lag:], ALU.mult, ALU.add))
                    dve.tensor_tensor(y, y, cp[:, n], ALU.mult).then_inc(tile_made, 1)
                for n in range(2):
                    tile_lo(T_MIX + n, 1, 4 + n)
                cnt = pinv[:, 1]
                link(dve.tensor_tensor_scan(cnt, ones[:, 0:16], ones[:, 0:16], 0.0, ALU.mult, ALU.add))
                for n, po, w in ((0, 0, 2), (0, 64, 4), (1, 0, 8), (1, 64, 16)):
                    link(dve.tensor_scalar(pinv[po:po + 64, n], cnt[po:po + 64, :], float(w), None, ALU.min))
                link(dve.reciprocal(pinv[:].rearrange("p a b -> p (a b)"), pinv[:].rearrange("p a b -> p (a b)")))
                for n in range(2):
                    u, m = cp[:, 6 + n], cp[:, 2 + n]
                    src, at_ = u, 0
                    for lag in (1, 2) if n == 0 else (1, 2, 4, 8):
                        dst = cp[:, at_]
                        link(dve.tensor_copy(dst[:, 0:lag], src[:, 0:lag]))
                        link(dve.tensor_tensor(dst[:, lag:], src[:, lag:], src[:, 0:S - lag], ALU.add))
                        src, at_ = dst, 1 - at_
                    for po, place, w in ((0, at_, 2 if n == 0 else 8), (64, 1 - at_, 4 if n == 0 else 16)):
                        h = slice(po, po + 64)
                        link(dve.tensor_tensor(m[h, 0:16], cp[h, place, 0:16], pinv[h, n], ALU.mult))
                        link(dve.tensor_tensor(m[h, 0:16], m[h, 0:16], u[h, 0:16], ALU.subtract))
                        ins = dve.scalar_tensor_tensor(m[h, 16:], cp[h, place, 16:], 1.0 / w, u[h, 16:], ALU.mult, ALU.subtract)
                        if po:
                            ins.then_inc(m_made, 1)
                            dve.wait_ge(m_made, n + 1)
                        else:
                            link(ins)
                for n in range(2):
                    dve.wait_ge(m_mm, n + 1)
                    tmp_free(T_MIX + 2 + n)
                    dve.tensor_scalar(tmp[:, n], bank[n][:], v1[:, V_PS + n:V_PS + n + 1], None, ALU.mult).then_inc(tile_made, 1)
                for n in range(2):
                    tile_lo(T_MIX + 2 + n, 1, 6 + n)

            def head_norm():
                dve.wait_ge(evac[0], 4 * (N_QKV2[0] + 1))
                dve.wait_ge(evac[1], 4 * (N_QKV2[1] + 1))
                dve.wait_ge(turned, R_N2 + 8)
                for n in range(2):
                    link(dve.tensor_tensor(sq2, qkv2[:, n], qkv2[:, n], ALU.mult))
                    dve.reduce_sum(st[:, 32 * n:32 * n + 32], sq2.rearrange("p t (h d) -> p (t h) d", d=HD), AX)\
                        .then_inc(qk_sq, 1)
                    dve.wait_ge(qk_sq, n + 1)
                dve.wait_ge(qk_rs, 1)
                for n in range(2):
                    q = qkv2[:, n].rearrange("p t (h d) -> p (t h) d", d=HD)
                    dve.tensor_tensor(q, q, st[:, 32 * n:32 * n + 32].unsqueeze(2).broadcast_to([P, 32, HD]), ALU.mult)\
                        .then_inc(qk_made, 1)

            start()
            lo(0)
            lo(1)
            softplus()
            for half in range(2):
                lo(U_Z + 2 * half + 1)
                lo(U_Z + 2 * half + 2)
            with dve.Fori(0, 3) as i:
                link.enter(i, 12)
                convolve(i)
            link.leave(3)
            ssd()
            split_turned(T_SSM, R_SSM, 1, lambda k: v0[:, V_SSM + k:V_SSM + k + 1], lambda k: 0.0)
            for b in range(4):
                lo(U_WO1 + b + 1)
            for b in range(4):
                lo(U_V + b + 1)
            for s in range(-4, 18):
                g, j = s // 4 + 1, s % 4
                if g < 4 and j % 2 == 0:
                    lo(U_QK + 2 * g + j // 2 + 1)
                if s >= 2:
                    h = s - 2
                    output(h, att[:, :, h * HD:h * HD + HD])
                if 0 <= s < 16:
                    fox_scores(s)
            split_turned(T_ATT, R_ATT, 1, lambda k: v1[:, V_ATT + k:V_ATT + k + 1], lambda k: 0.0)
            dve.wait_ge(xre_in, 16)
            dve.wait_ge(g_made, 2)
            for half in range(2):
                lo(U_WO2 + 2 * half + 1)
                lo(U_WO2 + 2 * half + 2)
                for t in range(TB):
                    part = slice(512 * half, 512 * half + 512)
                    dve.wait_ge(ticks, 2 * (U_WO2 + 2 * half) + 3 + t // 2)
                    dve.tensor_tensor(x1[:, t, part], bank[4 * half + t][:], yacc[:, t, part], ALU.add).then_inc(evac[half], 1)
                    dve.wait_ge(evac[half], 4 * N_WO2[half] + t + 1)
                    link(dve.tensor_tensor(x1[:, t, part], x1[:, t, part], row[:, 0, part], ALU.mult))
                    dve.scalar_tensor_tensor(x1[:, t, part], xre[:, t, part], ALPHA, x1[:, t, part], ALU.mult, ALU.add)\
                        .then_inc(sum_made, 1)
            dve.wait_ge(sum_made, 8)
            for t in range(TB):
                layer_norm(0, t)
            layer_scale(0)
            split_turned(T_X1, R_X1, 0, lambda k: mod[:, 32 + k:33 + k], lambda k: mod[:, 24 + k:25 + k])
            dve.wait_ge(acc0, 1)
            with dve.Fori(0, QUARTERS) as i:
                feed_forward(U_FF1, T_HID1, N_FF1, yacc, i, False)
            dve.wait_ge(g_made, 4)
            for t in range(TB):
                link(dve.tensor_tensor(yacc[:, t], yacc[:, t], row[:, 0], ALU.mult))
                dve.scalar_tensor_tensor(x1[:, t], x1[:, t], ALPHA, yacc[:, t], ALU.mult, ALU.add).then_inc(sum_made, 1)
                dve.wait_ge(sum_made, 8 + t + 1)
                layer_norm(1, t)
            layer_scale(1)
            split_turned(T_N2, R_N2, 0, lambda k: v1[:, V_N1 + k:V_N1 + k + 1], lambda k: 0.0)
            for b in range(6):
                lo(U_QKV2 + b + 1)
            head_norm()
            for b in range(4):
                lo(U_CP + b + 1)
            conv_pool()
            for n in range(2):
                for k in range(4):
                    dve.wait_ge(q2_t, 4 * n + k + 1)
                    dve.tensor_scalar(qkT2[:, n, k], bank[4 * n + k][:], v1[:, V_QG + n:V_QG + n + 1],
                                      HD ** -0.5 if n == 0 else 1.0, ALU.mult, ALU.mult).then_inc(q2_made, 1)
            for s in range(10):
                if s >= 2:
                    h = s - 2
                    output(16 + h, att2[:, :, h * HD:h * HD + HD])
                if s < 8:
                    dve.wait_ge(s_mm, 16 + s + 1)
                    maxima(16 + s, lambda q: bank[SB[q][0]][:, SB[q][1]:SB[q][1] + (q + 1) * P])
            split_turned(T_MIX + 4, R_ATT2, 1, lambda k: 1.0, lambda k: 0.0, 4)
            for half in range(2):
                lo(U_WO3 + 2 * half + 1)
                lo(U_WO3 + 2 * half + 2)
                for t in range(TB):
                    part = x1[:, t, 512 * half:512 * half + 512]
                    dve.wait_ge(ticks, 2 * (U_WO3 + 2 * half) + 3 + t // 2)
                    dve.tensor_tensor(part, bank[4 * half + t][:], part, ALU.add).then_inc(evac[half], 1)
            split_turned(T_N3, R_N3, 0, lambda k: v1[:, V_N2 + k:V_N2 + k + 1], lambda k: 0.0)
            with dve.Fori(0, QUARTERS - 1) as i:
                feed_forward(U_FF2, T_HID2, N_FF2, x1, i, False)
            feed_forward(U_FF2, T_HID2, N_FF2, x1, QUARTERS - 1, True)

        @block.tensor
        def _(pe):
            def three(out_, hi_a, lo_a, hi_b, lo_b, start, stop):
                pe.matmul(out_, hi_a, hi_b, start=start, stop=False)
                pe.matmul(out_, hi_a, lo_b, start=False, stop=False)
                return pe.matmul(out_, lo_a, hi_b, start=False, stop=stop)

            def column_tile(u0, n, act_buf, dst, t0=None, i=0, per=0):
                s = u0 % 2
                if n == 0:
                    pe.wait_ge(w_lo_made, at(i, per, u0 + 1))
                for k in range(KT):
                    if t0 is not None:
                        pe.wait_ge(a_lo_made, t0 + k + 1)
                    w = slice(256 * k + P * n, 256 * k + P * n + P)
                    last = three(dst, w_hi[:, s, w], w_lo[:, s, w], a_hi[act_buf][:, k], a_lo[act_buf][:, k],
                                 k == 0, k == KT - 1)
                last.then_inc(ticks, 1)

            def column_pair(u0, s, n_use, act_buf, t0=None, i=0, per=0, uses=0):
                for j in range(4):
                    pe.wait_ge(evac[s], at(i, 4 * uses, 4 * (n_use - 1) + j + 1))
                    column_tile(u0 + j // 2, j % 2, act_buf, bank[4 * s + j][:], t0 if j == 0 else None, i, per)

            def row_pair(u0, s, n_use, act_buf, t0=None, i=0, per=0, uses=0, tstep=0):
                if not (isinstance(n_use, int) and isinstance(i, int) and n_use + i * uses == 0):
                    pe.wait_ge(evac[s], at(i, 4 * uses, 4 * n_use))
                for b in range(2):
                    slot = (u0 + b) % 2
                    pe.wait_ge(w_lo_made, at(i, per, u0 + b + 1))
                    order = [(k, t) for k in range(4) for t in range(TB)] if b == 0 else [(k, t) for t in range(TB) for k in range(4)]
                    for m, (k, t) in enumerate(order):
                        kk = 4 * b + k
                        if t0 is not None and (t == 0 and b == 0 or m == 0):
                            pe.wait_ge(a_lo_made, at(i, tstep, t0 + (kk + 1 if b == 0 else KT)))
                        a = slice(P * t, P * t + P)
                        w = slice(512 * k, 512 * k + 512)
                        last = three(bank[4 * s + t][:], a_hi[act_buf][:, kk, a], a_lo[act_buf][:, kk, a],
                                     w_hi[:, slot, w], w_lo[:, slot, w], kk == 0, kk == KT - 1)
                        if m % 8 == 7:
                            last.then_inc(ticks, 1)

            def turn(src, n=KT):
                for k in range(n):
                    for t in range(TB):
                        last = pe.transpose(bank[k][:, P * t:P * t + P], src[:, t, P * k:P * k + P], ident[:])
                    last.then_inc(turned, 1)

            def evacuated(n0, n1):
                pe.wait_ge(evac[0], 4 * n0)
                pe.wait_ge(evac[1], 4 * n1)

            def probs_t(h, src):
                pe.wait_ge(p_made, 4 * h + 4)
                for b in range(10):
                    m, o = b // 4, b % 4
                    if o == 0 and h:
                        pe.wait_ge(pt_made, 3 * (h - 1) + m + 1)
                        if m == 2:
                            pe.wait_ge(o_made, h)
                    last = pe.transpose(bank[(7, 2, 3)[m]][:, o * P:o * P + P], src[:, b * P:b * P + P], ident[:])
                    if b in (3, 7, 9):
                        last.then_inc(pt_t, 1)

            def values(h, pT, v):
                pe.wait_ge(pt_made, 3 * h + 3)
                for q in range(TB):
                    for k in range(q + 1):
                        b = q * (q + 1) // 2 + k
                        last = pe.matmul(bank[3][:, 256 + q * HD:256 + q * HD + HD], pT[:, b * P:b * P + P], v(k),
                                         start=k == 0, stop=k == q)
                last.then_inc(o_mm, 1)

            def g_row(col, b):
                for half in range(2):
                    for k in range(4):
                        m = col + 4 * half + k
                        last = pe.matmul(bank[b + half][:, k * P:k * P + P], mod[:, m:m + 1].broadcast_to([P, P]), ident[:],
                                         start=True, stop=True)
                    last.then_inc(g_mm, 1)

            pe.wait_ge(consts, 7)
            pe.wait_ge(vecs_in, 16 * 14)
            for n in range(2):
                last = pe.transpose(bank[0][:, P * n:P * n + P], vec_in[:, n, :], ident[:])
            last.then_inc(vecs_t, 1)
            pe.wait_ge(c_made, 1)
            with pe.Fori(0, 6) as i:
                for n in range(4):
                    pe.wait_ge(ada_in[n], at(i, 16, 16))
                    for h in range(2):
                        for k in range(KT):
                            last = pe.matmul(bank[1][:, bass.ds(at(i, 8, 2 * n + h), 1)], ada[:, n, k, P * h:P * h + P],
                                             cact[:, k:k + 1], start=k == 0, stop=k == KT - 1)
                    last.then_inc(ada_used, 1)
            pe.wait_ge(x_in, 16)
            pe.wait_ge(mod_made, 1)
            turn(xtok)
            pe.wait_ge(tile_made, T_H + 8)
            pe.wait_ge(w_lo_made, 1)
            for k in range(KT):
                pe.wait_ge(a_lo_made, T_H + k + 1)
                w = slice(256 * k, 256 * k + P)
                last = three(bank[7][:], w_hi[:, 0, w], w_lo[:, 0, w], a_hi[0][:, k], a_lo[0][:, k], k == 0, k == KT - 1)
                if k in (3, 7):
                    last.then_inc(ticks, 1)
            row_pair(U_Z, 0, 0, 0)
            pe.wait_ge(dtf_abs, 1)
            row_pair(U_Z + 2, 1, 0, 0)
            with pe.Fori(0, 3) as i:
                column_pair(U_XBC, 0, N_XBC[0], 0, i=i, per=2, uses=1)
            evacuated(N_WO1[0], N_WO1[1])
            pe.wait_ge(conv_act, CT)
            for b in range(8):
                for k in range(4):
                    last = pe.transpose(bank[b][:, P * k:P * k + P], xbc[:, 4 * (b % 2) + k, P * (b // 2):P * (b // 2) + P], ident[:])
                last.then_inc(xs_t, 1)
            for b in range(2):
                pe.wait_ge(xs_made, b + 1)
                for k in range(4):
                    t, g = 2 * b + k // 2, k % 2
                    last = pe.transpose(bank[b][:, P * k:P * k + P], xbc[:, 8 + g, P * t:P * t + P], ident[:])
                last.then_inc(xs_t, 1)
            pe.wait_ge(xs_made, 3)
            pe.wait_ge(scanned, 5)
            for b in range(8):
                last = pe.transpose(bank[2][:, 64 * b:64 * b + 64], dtf[0:64, b // 4, P * (b % 4):P * (b % 4) + P], ident[0:64, 0:64])
            last.then_inc(dta_t, 1)
            for b in range(2):
                pe.wait_ge(xs_made, 4 + b)
                for k in range(4):
                    t, g = 2 * b + k // 2, k % 2
                    part = slice(P * t, P * t + P)
                    last = pe.matmul(bank[3 + b][:, P * k:P * k + P], xbc[:, 8 + g, part], xbc[:, 10 + g, part], start=True, stop=True)
                last.then_inc(cb_done, 1)
            pe.wait_ge(xs_made, 10)
            pe.wait_ge(dta_made, 1)
            for ch in range(TB):
                pe.wait_ge(xc_made, ch + 1)
                pe.wait_ge(score_made, ch + 1)
                if ch:
                    pe.wait_ge(y_made, ch)
                for h in range(SSM_H):
                    last = pe.matmul(bank[h // 8][:, HD * (h % 8):HD * (h % 8) + HD], bc[:, ch % 2, h, :],
                                     xs[:, ch, HD * h:HD * h + HD], start=True, stop=True)
                if ch:
                    pe.wait_ge(prev_made, 2 * ch)
                    for g in range(2):
                        last = pe.matmul(bank[2 + g][:], xbc[:, 10 + g, P * ch:P * ch + P], prev[:, 512 * g:512 * g + 512],
                                         start=True, stop=True)
                last.then_inc(y_mm, 1)
                if ch < TB - 1:
                    pe.wait_ge(xd_made, ch + 1)
                    if ch == 0:
                        pe.wait_ge(cb_evac, 2)
                    for g in range(2):
                        last = pe.matmul(bank[4 + g][:], btok[:, ch, g, :], xd[:, 512 * g:512 * g + 512], start=True, stop=True)
                    last.then_inc(st_mm, 1)
            pe.wait_ge(y_made, TB)
            pe.wait_ge(y_norm, 4)
            turn(z_y)
            pe.wait_ge(tile_made, T_SSM + 4)
            row_pair(U_WO1, 0, N_WO1[0], 1, T_SSM)
            row_pair(U_WO1 + 2, 1, N_WO1[1], 1)
            row_pair(U_V, 0, N_V[0], 0)
            row_pair(U_V + 2, 1, N_V[1], 0)
            evacuated(N_QK[0], N_QK[1])
            for s in range(-4, 18):
                g, j = s // 4 + 1, s % 4
                if s >= 2:
                    probs_t(s - 2, prob[:, s % 2])
                if g < 4:
                    pe.wait_ge(evac[0], 4 * (N_QK[0] + g) + j - 1)
                    column_tile(U_QK + 2 * g + j // 2, j % 2, 0, bank[j % 2][:])
                if s >= 2:
                    h = s - 2
                    values(h, probT, lambda k: vtok[:, k, h * HD:h * HD + HD])
                if 0 <= s < 16:
                    pe.wait_ge(evac[0], 4 * (N_QK[0] + s // 4 + 1))
                    if s:
                        pe.wait_ge(s_made, s)
                    po, tile = HD * (s % 2), (s % 4) // 2
                    q_, k_ = qk[po:po + HD, (s // 4) % 2, tile], qk[po:po + HD, (s // 4) % 2, 2 + tile]
                    for q in range(TB):
                        b, o = SB[q]
                        last = pe.matmul(bank[b][:, o:o + (q + 1) * P], q_[:, P * q:P * q + P], k_[:, 0:(q + 1) * P],
                                         start=True, stop=True)
                    last.then_inc(s_mm, 1)
            pe.wait_ge(s_made, 16)
            g_row(16, 4)
            pe.wait_ge(y_norm, 8)
            pe.wait_ge(pt_made, 48)
            pe.wait_ge(g_made, 2)
            turn(att)
            pe.wait_ge(tile_made, T_ATT + 4)
            row_pair(U_WO2, 0, N_WO2[0], 1, T_ATT)
            row_pair(U_WO2 + 2, 1, N_WO2[1], 1)
            evacuated(N_FF1[0], N_FF1[1])
            pe.wait_ge(ln_made, 4)
            turn(x1)

            def feed_forward(u0, t_act, t0, n0):
                pe.wait_ge(a_lo_made, t_act + KT)
                with pe.Fori(0, QUARTERS) as i:
                    for b in range(2):
                        column_pair(u0 + 2 * b, b, n0[b], 0, i=i, per=8, uses=2)
                    for b in range(2):
                        row_pair(u0 + 4 + 2 * b, b, n0[b] + 1, 1, t0 if b == 0 else None, i=i, per=8, uses=2, tstep=8)

            feed_forward(U_FF1, T_X1, T_HID1, N_FF1)
            evacuated(N_QKV2[0], N_QKV2[1])
            g_row(40, 0)
            pe.wait_ge(y_norm, 12)
            pe.wait_ge(g_made, 4)
            turn(n2)
            pe.wait_ge(tile_made, T_N2 + 4)
            row_pair(U_QKV2, 0, N_QKV2[0], 0, T_N2)
            row_pair(U_QKV2 + 2, 1, N_QKV2[1], 0)
            row_pair(U_QKV2 + 4, 0, N_QKV2[0] + 1, 0)
            column_pair(U_CP, 1, N_CP[1], 0)
            column_pair(U_CP + 2, 0, N_CP[0], 0)
            evacuated(N_WO3[0], N_WO3[1])
            pe.wait_ge(pool_in, 64)
            for n in range(2):
                pe.wait_ge(m_made, n + 1)
                pe.matmul(bank[n][:], poolw[:, n, :], cp[:, 2 + n], start=True, stop=True).then_inc(m_mm, 1)
            pe.wait_ge(tile_made, T_MIX + 4)
            pe.wait_ge(qk_made, 2)
            for n in range(2):
                for k in range(4):
                    for t in range(TB):
                        last = pe.transpose(bank[4 * n + k][:, P * t:P * t + P], qkv2[:, n, t, P * k:P * k + P], ident[:])
                    last.then_inc(q2_t, 1)
            pe.wait_ge(q2_made, 8)
            pe.wait_ge(rel_made, 1)
            for s in range(10):
                if s >= 2:
                    probs_t(16 + s - 2, prob2[:, s % 2])
                    h = s - 2
                    values(16 + h, prob2T, lambda k: qkv2[:, 2, k, h * HD:h * HD + HD])
                if s < 8:
                    if s:
                        pe.wait_ge(p_made, 4 * (16 + s))
                    po, tile = HD * (s % 2), s // 2
                    q_, k_ = qkT2[po:po + HD, 0, tile], qkT2[po:po + HD, 1, tile]
                    for q in range(TB):
                        b, o = SB[q]
                        n = (q + 1) * P
                        pe.matmul(bank[b][:, o:o + n], q_[:, P * q:P * q + P], k_[:, 0:n], start=True, stop=False)
                        if q >= 2:
                            far = (q - 1) * P
                            pe.matmul(bank[b][:, o:o + far], ones[0:1, 0:P], relc[0:1, s:s + 1].broadcast_to([1, far]),
                                      start=False, stop=False)
                        if q >= 1:
                            pe.matmul(bank[b][:, o + n - 2 * P:o + n - P], relt[:, 1, s, :], flip[:], start=False, stop=False)
                        last = pe.matmul(bank[b][:, o + n - P:o + n], relt[:, 0, s, :], flip[:], start=False, stop=True)
                    last.then_inc(s_mm, 1)
            pe.wait_ge(o_made, 24)
            turn(att2, 4)
            pe.wait_ge(tile_made, T_MIX + 8)
            pe.wait_ge(a_lo_made, T_MIX + 8)
            row_pair(U_WO3, 0, N_WO3[0], 1)
            row_pair(U_WO3 + 2, 1, N_WO3[1], 1)
            evacuated(N_FF2[0], N_FF2[1])
            pe.wait_ge(y_norm, 16)
            turn(n2)
            feed_forward(U_FF2, T_N3, T_HID2, N_FF2)


_INS = ["x", "c", "w_ada", "b_ada", "w_in", "conv_w", "conv_b", "dt_bias", "a_log", "d_skip", "ssm_norm_w", "f_bias",
        "attn_norm_w", "w_out", "ln1_g", "ln1_b", "w_ff_in", "w_ff_out", "ln2_g", "ln2_b", "norm1_g_2", "w_in_2",
        "q_norm_g_2", "k_norm_g_2", "rel_bias_2", "conv_w_2", "pool_w_2", "pool_scale_2", "w_out_2", "norm2_g_2",
        "w_mlp1_2", "w_mlp2_2"]


def kernel(**inputs):
    import numpy as _np
    import concourse.bacc as _bacc
    from concourse import mybir as _mybir
    from concourse.bass_utils import run_bass_kernel_spmd as _run

    nc = _bacc.Bacc("TRN2", target_bir_lowering=False, num_devices=1, dynamic_dma_scratch_size=8192)
    arrays, args = {}, []
    for name in _INS:
        a = _np.ascontiguousarray(inputs[name])
        arrays[f"in_{name}_dram"] = a
        args.append(nc.dram_tensor(f"in_{name}_dram", a.shape, _mybir.dt.from_np(a.dtype), kind="ExternalInput").ap())
    args.append(nc.dram_tensor("out_0_dram", (1, S, D), F32, kind="ExternalOutput").ap())
    build(nc, *args)
    r = _run(nc, [arrays], core_ids=[0])
    return r.results[0]["out_0_dram"]
```

```python
from contextlib import ExitStack

import numpy as np

import concourse.bass as bass
from concourse import mybir

F32 = mybir.dt.float32
F32R = mybir.dt.float32r
ALU = mybir.AluOpType
ACT = mybir.ActivationFunctionType
AX = mybir.AxisListType.X

P = 128
S = 512
D = 1024
TB = S // P
KT = D // P
SSM_W, SSM_H, HD, ST = 1024, 16, 64, 128
CONV_DIM = SSM_W + 2 * 2 * ST
CT = CONV_DIM // P
CW = 4
C_Z, C_XBC = 0, SSM_W
C_DT = C_XBC + CONV_DIM
C_Q = C_DT + SSM_H
C_K, C_V = C_Q + 1024, C_Q + 2048
C_F = C_Q + 3072
ALPHA = 2.0 ** 0.25
LN_EPS, RMS_EPS, EPS2 = 1e-5, 1e-5, 1e-6
FF = 4096
QUARTERS = FF // D
NEG = -1e30
H2 = 8
CLIP = 128
NREL = 2 * CLIP + 1
SB = [(4, 384), (6, 0), (4, 0), (5, 0)]
QO = [0, 128, 384, 768]

U_DTF = 0
U_XBC = 1
U_Z = U_XBC + 6
U_QK = U_Z + 4
U_V = U_QK + 2
U_QK1 = U_V + 4
U_WO1 = U_QK1 + 6
U_WO2 = U_WO1 + 4
U_FF1 = U_WO2 + 4
U_QKV2 = U_FF1 + 8 * QUARTERS
U_CP = U_QKV2 + 6
U_WO3 = U_CP + 4
U_FF2 = U_WO3 + 4
UNITS = U_FF2 + 8 * QUARTERS
N_ADA, ADA_EARLY = 24, 8


def ada_before(u):
    return 0 if u < U_XBC + 2 else 2 * ((u - U_XBC) // 2) if u < U_Z + 2 else 7 if u < U_QK else 8


N_XBC = (1, 0)
N_V = (4, 0)
N_WO2 = (5, 1)
N_FF1 = (6, 2)
N_QKV2 = (N_FF1[0] + 2 * QUARTERS, N_FF1[1] + 2 * QUARTERS)
N_CP = (N_QKV2[0] + 2, N_QKV2[1] + 1)
N_WO3 = (N_CP[0] + 1, N_CP[1] + 1)
N_FF2 = (N_WO3[0] + 1, N_WO3[1] + 1)
T_H, T_SSM, T_ATT, T_X1 = 0, 8, 16, 24
T_HID1 = 32
T_N2 = T_HID1 + 32
T_MIX = T_N2 + 8
T_N3 = T_MIX + 8
T_HID2 = T_N3 + 8
M_H, M_X1, M_HID1, M_N2, M_MIX, M_HID2 = 0, 8, 16, 48, 48, 52
R_H, R_SSM, R_ATT, R_X1, R_N2, R_ATT2, R_N3 = 0, 8, 16, 24, 32, 40, 44
ATT_BANKS = (6, 7, 2, 3, 0, 1, 4, 5)
XS_BANKS = (0, 1, 3, 4)
Z_TILES = ((2,), (3,), (4, 5), (6, 7))
WO1_TILES = ((),) * 12 + ((0,), (1,), (2,), (3,), (4, 5), (6, 7))


class Link:

    def __init__(self, eng, sem):
        self.eng, self.sem, self.n, self.extra = eng, sem, 0, 0

    def __call__(self, ins):
        self.n += 1
        ins.then_inc(self.sem, 1)
        self.eng.wait_ge(self.sem, self.extra + self.n)

    def enter(self, i, per):
        self.start, self.per, self.extra = self.n, per, i * per

    def leave(self, times):
        assert self.n - self.start == self.per, (self.n - self.start, self.per)
        self.n, self.extra = self.start + times * self.per, 0


def build(nc, x, c, w_ada, b_ada, w_in, conv_w, conv_b, dt_bias, a_log, d_skip, ssm_norm_w, f_bias,
          attn_norm_w, w_out, ln1_g, ln1_b, w_ff_in, w_ff_out, ln2_g, ln2_b, norm1_g_2, w_in_2,
          q_norm_g_2, k_norm_g_2, rel_bias_2, conv_w_2, pool_w_2, pool_scale_2, w_out_2, norm2_g_2,
          w_mlp1_2, w_mlp2_2, out):
    with ExitStack() as ctx:
        def sb(name, shape, dt=F32):
            return ctx.enter_context(nc.sbuf_tensor(name, shape, dt))

        def sem(name):
            return ctx.enter_context(nc.semaphore(name))

        bank = [ctx.enter_context(nc.psum_tensor(f"bank{b}", [P, 512], F32)) for b in range(8)]

        raw = sb("raw", [P, 2, 2048])
        w_hi = sb("w_hi", [P, 2, 2048], F32R)
        w_lo = sb("w_lo", [P, 2, 2048], F32R)
        a_hi = [sb(f"a_hi{n}", [P, KT, S], F32R) for n in range(2)]
        a_lo = [sb(f"a_lo{n}", [P, KT, S], F32R) for n in range(2)]
        tmp = sb("tmp", [P, 2, S])
        arena = sb("arena", [P, 22528])

        def view(at, *dims):
            n = int(np.prod(dims))
            v = arena[:, at:at + n]
            if len(dims) == 2:
                v = v.rearrange("p (a b) -> p a b", a=dims[0])
            elif len(dims) == 3:
                v = v.rearrange("p (a b c) -> p a b c", a=dims[0], b=dims[1])
            return v

        xtok = view(18432, TB, D)
        ada = view(0, 4, KT, 512)
        z_y = view(0, TB, D)
        xbc = view(4096, CT, S)
        dtf = view(19456, 6, S)
        xs = view(10240, TB, D)
        btok = view(14336, TB, 2, ST)
        bc = view(15360, 2, 16, P)
        xc = view(19456, 1024)
        xd = view(20480, 1024)
        prev = view(21504, 1024)
        cbm = view(4096, 4, 2 * P)
        off = view(5120, 1024)
        yacc = view(10240, TB, D)
        vtok = view(0, TB, D)
        att = view(4096, TB, D)
        ncb = view(8192, 2, S)
        ncm = view(9216, 2, S)
        qk = view(14336, 2, 4, S)
        prob = view(18432, 2, 1280)
        probT = view(20992, 1280)
        xre = view(0, TB, D)
        x1 = view(14336, TB, D)
        row = view(18432, 3, D)
        rl = view(0, 2, S)
        n2 = view(0, TB, D)
        qkv2 = view(4096, 3, TB, 512)
        sq2 = view(0, TB, 512)
        qkT2 = view(10240, 2, 4, S)
        cp = view(18432, 8, S)
        relt = view(2048, 2, H2, P)
        prob2 = view(4096, 2, 1280)
        prob2T = view(6656, 1280)
        att2 = view(0, TB, 512)

        ident = sb("ident", [P, P])
        flip = sb("flip", [P, P])
        masks = sb("masks", [P, 2, P])
        keep = masks[:, 0]
        hide = masks[:, 1]
        poolw = masks
        ones = sb("ones", [P, P])
        vec_in = view(16384, 2, P)
        vec = sb("vec", [P, 2, P])
        cact = sb("cact", [P, KT])
        mod = sb("mod", [P, 48])
        col64 = sb("col64", [64, 4])
        dsk = sb("dsk", [P, SSM_H])
        dta = tmp[:, 0].rearrange("p (a b) -> p a b", a=8)
        ex2 = sb("ex", [P, 2, 3, SSM_H])
        st = sb("st", [P, 64])
        st2 = sb("st2", [P, 64])
        stat = sb("stat", [P, 8, 6])
        mv = sb("mv", [P, TB, 2])
        nhalf = sb("nhalf", [P, 64])
        relc = sb("relc", [P, H2])
        pinv = sb("pinv", [P, 2, 16])
        acs_d = nc.dram_tensor("acs_d", (16, S), F32).ap()
        ncum_d = nc.dram_tensor("ncum_d", (16, S), F32).ap()
        ext_d = nc.dram_tensor("ext_d", (H2, 512), F32).ap()

        v0, v1 = vec[:, 0, :], vec[:, 1, :]
        V_BADA, V_CONVW, V_CONVB, V_SSM = 0, 48, 96, 108
        V_ATT, V_N1, V_N2, V_CW2, V_PS, V_QG, V_KG, V_C = 0, 8, 16, 24, 30, 32, 33, 34
        V1_ROWS = 42

        mxs, rsum, rinv = sb("mxs", [P, 2, 4]), sb("rsum", [P, 2, 4]), sb("rinv", [P, 2, 4])

        landed = [sem("landed0"), sem("landed1")]
        w_hi_made, w_lo_made, ticks = sem("w_hi_made"), sem("w_lo_made"), sem("ticks")
        evac = [sem("evac0"), sem("evac1")]
        turned = sem("turned")
        tile_made, a_hi_made, a_lo_made = sem("tile_made"), sem("a_hi_made"), sem("a_lo_made")
        dve_link, act_link, pool_link = sem("dve_link"), sem("act_link"), sem("pool_link")
        cleared, consts = sem("cleared"), sem("consts")
        vecs_in, vecs_t, vecs_made, c_made = sem("vecs_in"), sem("vecs_t"), sem("vecs_made"), sem("c_made")
        x_in, small_in, mod_made, ada_used = sem("x_in"), sem("small_in"), sem("mod_made"), sem("ada_used")
        ada_in = [sem(f"ada_in{n}") for n in range(4)]
        late_used, late_made = sem("late_used"), sem("late_made")
        z_read, qk_read, yacc_read, yz_made = sem("z_read"), sem("qk_read"), sem("yacc_read"), sem("yz_made")
        dtf_abs, dtf_exp, a_col, scanned = sem("dtf_abs"), sem("dtf_exp"), sem("a_col"), sem("scanned")
        acs_out, cum_out, dta_t, dta_made = sem("acs_out"), sem("cum_out"), sem("dta_t"), sem("dta_made")
        conv_act, xs_t, xs_made, cb_done, cb_evac = sem("conv_act"), sem("xs_t"), sem("xs_made"), sem("cb_done"), sem("cb_evac")
        bc_in = [sem("bc_in0"), sem("bc_in1")]
        bc_sub, bc_exp, score_made = sem("bc_sub"), sem("bc_exp"), sem("score_made")
        ex_in, ex_made, xc_made, xd_made = sem("ex_in"), sem("ex_made"), sem("xc_made"), sem("xd_made")
        y_mm, st_mm, prev_made, y_made = sem("y_mm"), sem("st_mm"), sem("prev_made"), sem("y_made")
        y_sq, rs_made, y_norm = sem("y_sq"), sem("rs_made"), sem("y_norm")
        ncb_in = [sem("ncb_in0"), sem("ncb_in1")]
        ncm_made, s_mm, s_made, mx_made, p_made = sem("ncm_made"), sem("s_mm"), sem("s_made"), sem("mx_made"), sem("p_made")
        pt_t, pt_made, o_mm, o_made = sem("pt_t"), sem("pt_made"), sem("o_mm"), sem("o_made")
        rows_in, g_mm, g_made, xre_in, acc0 = sem("rows_in"), sem("g_mm"), sem("g_made"), sem("xre_in"), sem("acc0")
        ln_var, ln_rs, ln_made, sum_made = sem("ln_var"), sem("ln_rs"), sem("ln_made"), sem("sum_made")
        qk_sq, qk_rs, qk_made, q2_t, q2_made = sem("qk_sq"), sem("qk_rs"), sem("qk_made"), sem("q2_t"), sem("q2_made")
        ext_out, rel_in, rel_made, pool_in = sem("ext_out"), sem("rel_in"), sem("rel_made"), sem("pool_in")
        m_made, m_mm, out_sent = sem("m_made"), sem("m_mm"), sem("out_sent")

        w_in_v = w_in[0].rearrange("(k p) n -> p k n", p=P)
        w_ada_v = w_ada[0].rearrange("(k p) n -> p k n", p=P)
        w_out_v = w_out[0].rearrange("(k p) n -> p k n", p=P)
        w_in2_v = w_in_2[0].rearrange("(k p) n -> p k n", p=P)
        w_out2_v = w_out_2[0].rearrange("(k p) n -> p k n", p=P)
        ff_v = [(w_ff_in[0].rearrange("(k p) n -> p k n", p=P), w_ff_out[0].rearrange("(k p) n -> p k n", p=P)),
                (w_mlp1_2[0].rearrange("(k p) n -> p k n", p=P), w_mlp2_2[0].rearrange("(k p) n -> p k n", p=P))]
        x_v = x[0].rearrange("(t p) d -> p t d", p=P)
        out_v = out[0].rearrange("(t p) d -> p t d", p=P)
        block = ctx.enter_context(nc.Block())

        def rows_of(vector, n):
            return vector.rearrange("a (k p) -> (a k) p", k=n)


        def at(i, per, const):
            return i * per + const

        def left(ap):
            return ap.rearrange("p (k n) -> p k n", k=KT)[:, :, 0:P]

        @block.sync
        def _(sp):
            def load(i, per, u0, src, k, split=True):
                if split and not (isinstance(i, int) and i * per + u0 < 2):
                    sp.wait_ge(w_lo_made, at(i, per, u0 - 1))
                sp.dma_start(raw[:, u0 % 2].rearrange("p (k n) -> p k n", k=k), src).then_inc(landed[u0 % 2], 16)

            def columns(i, per, u0, w, col, split=True):
                load(i, per, u0, w[:, :, bass.ds(col, 256)], 8, split)

            def rows(i, per, u0, w, k, col, split=True):
                load(i, per, u0, w[:, bass.ds(k, 4), bass.ds(col, 512)], 4, split)

            def four_rows(u0, w, k0, col0):
                for b in range(4):
                    rows(0, 0, u0 + b, w, k0 + 4 * (b % 2), col0 + 512 * (b // 2))

            def ada_late(i, per, n):
                sp.dma_start(raw[:, (n + 1) % 2].rearrange("p (k n) -> p k n", k=8),
                             w_ada_v[:, :, bass.ds(at(i, 256 * per, 256 * (ADA_EARLY + n)), 256)]).then_inc(landed[(n + 1) % 2], 16)

            def ada_four(i):
                for m in range(4):
                    if m < 2:
                        sp.wait_ge(w_lo_made, at(i, 2, U_XBC + m + 1))
                    else:
                        sp.wait_ge(late_used, at(i, 4, m - 1))
                    ada_late(i, 4, m)

            def ada_two(n, u):
                for m in range(2):
                    sp.wait_ge(w_lo_made, u + m + 1)
                    ada_late(0, 0, n + m)

            def prelude():
                sp.wait_ge(cleared, 1)
                for at_, src, n, side in ((V_C, c, KT, 1), (V_BADA, b_ada, 48, 0), (V_CONVB, conv_b, CT, 0),
                                          (V_SSM, ssm_norm_w, KT, 0), (V_ATT, attn_norm_w, KT, 1), (V_N1, norm1_g_2, KT, 1),
                                          (V_N2, norm2_g_2, KT, 1), (V_PS, pool_scale_2, 2, 1)):
                    sp.dma_start(vec_in[at_:at_ + n, side, :], src.rearrange("a (k p) -> (a k) p", k=n)).then_inc(vecs_in, 16)
                sp.dma_start(vec_in[V_CONVW:V_CONVW + 48, 0, :], conv_w[0].rearrange("i (k p) -> (i k) p", p=P)).then_inc(vecs_in, 16)
                sp.dma_start(vec_in[V_CW2:V_CW2 + 6, 1, :], conv_w_2[0].rearrange("i (k p) -> (i k) p", p=P)).then_inc(vecs_in, 16)
                for at_, src in ((V_QG, q_norm_g_2), (V_KG, k_norm_g_2)):
                    for half in range(2):
                        sp.dma_start(vec_in[at_:at_ + 1, 1, half * HD:half * HD + HD], src).then_inc(vecs_in, 16)
                sp.dma_start(xtok, x_v).then_inc(x_in, 16)
                for n in range(3):
                    sp.dma_start(ada[:, n], w_ada_v[:, :, n * 512:n * 512 + 512]).then_inc(ada_in[n], 16)
                sp.wait_ge(cleared, 3)
                unit = raw[:, 0].rearrange("p (k n) -> p k n", k=8)
                sp.dma_start(unit[:, :, 0:16], w_in_v[:, :, C_DT:C_DT + 16]).then_inc(landed[0], 16)
                sp.dma_start(unit[:, :, 32:48], w_in_v[:, :, C_F:C_F + 16]).then_inc(landed[0], 16)
                for dst, src in ((col64[0:16, 0:1], dt_bias), (col64[32:48, 0:1], f_bias), (col64[0:16, 2:3], a_log)):
                    sp.dma_start(dst, src.rearrange("a h -> h a")).then_inc(small_in, 16)
                sp.dma_start(ada[:, 3], w_ada_v[:, :, 1536:2048]).then_inc(ada_in[3], 16)
                sp.dma_start(dsk[:, :], bass.AP(d_skip.tensor, 0, [[0, P], [1, SSM_H]])).then_inc(small_in, 16)

            def feed_forward(u0, w1, w2):
                with sp.Fori(0, QUARTERS) as i:
                    for b in range(4):
                        columns(i, 8, u0 + b, w1, at(i, D, 256 * b))
                    for b in range(4):
                        rows(i, 8, u0 + 4 + b, w2, at(i, 8, 4 * (b % 2)), 512 * (b // 2))

            prelude()
            for b in range(2):
                columns(0, 0, U_XBC + b, w_in_v, C_XBC + 256 * b)
            with sp.Fori(0, 2) as i:
                ada_four(i)
                for b in range(2):
                    sp.wait_ge(late_used, at(i, 4, 3 + b))
                    columns(i, 2, U_XBC + 2 + b, w_in_v, at(i, 512, C_XBC + 256 * (2 + b)), False)
            ada_four(2)
            for half in range(2):
                for b in range(2):
                    sp.wait_ge(late_used, 11 + b + 2 * half)
                    rows(0, 0, U_Z + 2 * half + b, w_in_v, 4 * b, C_Z + 512 * half, False)
                ada_two(12 + 2 * half, U_Z + 2 * half)
            for b, col in enumerate((C_Q, C_K)):
                sp.wait_ge(late_used, 15 + b)
                columns(0, 0, U_QK + b, w_in_v, col, False)
            four_rows(U_V, w_in_v, 0, C_V)
            with sp.Fori(0, 3) as i:
                columns(i, 2, U_QK1, w_in_v, at(i, 256, C_Q + 256))
                columns(i, 2, U_QK1 + 1, w_in_v, at(i, 256, C_K + 256))
            four_rows(U_WO1, w_out_v, 0, 0)
            four_rows(U_WO2, w_out_v, KT, 0)
            feed_forward(U_FF1, *ff_v[0])
            four_rows(U_QKV2, w_in2_v, 0, 0)
            for b in range(2):
                rows(0, 0, U_QKV2 + 4 + b, w_in2_v, 4 * b, 1024)
            for b in range(4):
                columns(0, 0, U_CP + b, w_in2_v, 1536 + 256 * b)
            four_rows(U_WO3, w_out2_v, 0, 0)
            feed_forward(U_FF2, *ff_v[1])
            for s in range(2):
                sp.wait_ge(evac[s], 4 * (N_FF2[s] + 2 * QUARTERS))
            sp.dma_start(out_v, x1).then_inc(out_sent, 16)
            sp.wait_ge(out_sent, 16)

        @block.gpsimd
        def _(pool):
            link = Link(pool, pool_link)

            def constants():
                pool.memset(vec_in[:], 0.0).then_inc(cleared, 1)
                pool.memset(raw[:, 0], 0.0).then_inc(cleared, 1)
                pool.memset(col64[:], 0.0).then_inc(cleared, 1)
                for m in (ident[:], flip[:], hide):
                    link(pool.memset(m, 0.0))
                link(pool.memset(keep, 1.0))
                pool.memset(ones[:], 1.0).then_inc(consts, 1)
                pool.affine_select(out=ident[:], in_=ident[:], compare_op=ALU.not_equal, fill=1.0, base=0,
                                   pattern=[[-1, P]], channel_multiplier=1).then_inc(consts, 1)
                pool.affine_select(out=flip[:], in_=flip[:], compare_op=ALU.not_equal, fill=1.0, base=1 - P,
                                   pattern=[[1, P]], channel_multiplier=1).then_inc(consts, 1)
                pool.affine_select(out=keep, in_=keep, compare_op=ALU.is_ge, fill=0.0, base=0,
                                   pattern=[[1, P]], channel_multiplier=-1).then_inc(consts, 1)
                pool.affine_select(out=hide, in_=hide, compare_op=ALU.is_ge, fill=NEG, base=0,
                                   pattern=[[-1, P]], channel_multiplier=1).then_inc(consts, 1)
                pool.memset(nhalf[:], -0.5).then_inc(consts, 1)
                pool.wait_ge(cleared, 3)
                link(pool.memset(col64[0:32, 1:2], 1.0))
                link(pool.memset(col64[32:64, 1:2], -1.0))
                pool.memset(col64[:, 3:4], 1.0).then_inc(consts, 1)

            def inv_root(n, src, dst, scale, eps, signal):
                link(pool.tensor_scalar(st2[:, 0:n], src, scale, eps, ALU.mult, ALU.add))
                pool.tensor_tensor(dst, st2[:, 0:n], nhalf[:, 0:n], ALU.pow).then_inc(signal, 1)

            def rms_root(turn, eps):
                pool.wait_ge(y_sq, 4 * turn + 4)
                inv_root(4, st[:, 0:4], st[:, 4:8], 1.0 / D, eps, rs_made)

            def ln_root(turn):
                pool.wait_ge(ln_var, 4 * turn + 4)
                inv_root(4, mv[:, :, 1], st[:, 8:12], 1.0, LN_EPS, ln_rs)

            def lo(u0, i=0, per=0):
                pool.wait_ge(w_hi_made, at(i, per, u0 + 1))
                pool.tensor_tensor(w_lo[:, u0 % 2], raw[:, u0 % 2], w_hi[:, u0 % 2].bitcast(F32), ALU.subtract)\
                    .then_inc(w_lo_made, 1)

            def save_rows():
                pool.wait_ge(scanned, 5)
                pool.dma_start(acs_d, dtf[0:16, 1, :]).then_inc(acs_out, 16)
                pool.dma_start(ncum_d, dtf[32:48, 1, :]).then_inc(cum_out, 16)

            def ssd_row(ch):
                if ch >= 2:
                    pool.wait_ge(y_mm, ch - 1)
                pool.dma_start(bc[:, ch % 2], bass.AP(acs_d.tensor, ch * P, [[0, P], [S, 16], [1, P]]))\
                    .then_inc(bc_in[ch % 2], 16)

            def fox_row(h):
                if h >= 2:
                    pool.wait_ge(s_made, h - 1)
                pool.dma_start(ncb[:, h % 2], bass.AP(ncum_d.tensor, h * S, [[0, P], [1, S]]))\
                    .then_inc(ncb_in[h % 2], 16)
                pool.wait_ge(ncb_in[h % 2], 16 * (h // 2 + 1))
                pool.tensor_tensor(ncm[:, h % 2].rearrange("p (i k) -> p i k", i=TB),
                                   ncb[:, h % 2].rearrange("p (i k) -> p i k", i=TB),
                                   hide.unsqueeze(1).broadcast_to([P, TB, P]), ALU.add).then_inc(ncm_made, 1)

            def load_row(n, src):
                pool.dma_start(row[:, n], bass.AP(src.tensor, 0, [[0, P], [1, D]])).then_inc(rows_in, 16)

            def relative():
                rb = rel_bias_2.tensor
                pool.dma_start(ext_d[:, 0:NREL], rel_bias_2[0]).then_inc(ext_out, 16)
                pool.dma_start(ext_d[:, NREL:NREL + P].unsqueeze(2), bass.AP(rb, NREL - 1, [[NREL, H2], [0, P], [1, 1]]), allow_slow_non_contiguous=True).then_inc(ext_out, 16)
                pool.dma_start(relc[0:1, :].unsqueeze(2), bass.AP(rb, NREL - 1, [[0, 1], [NREL, H2], [1, 1]]), allow_slow_non_contiguous=True).then_inc(rel_in, 16)
                link(pool.memset(poolw[:], 0.0))
                for g in range(4):
                    po = HD * (g % 2)
                    pool.dma_start(poolw[po:po + HD, g // 2, po:po + HD], pool_w_2[0, g]).then_inc(pool_in, 16)
                pool.wait_ge(ext_out, 32)

            def relative_tiles():
                pool.wait_ge(turned, R_N2 + 8)
                for n in range(2):
                    pool.dma_start(relt[:, n], bass.AP(ext_d.tensor, 1 + CLIP * n, [[1, P], [512, H2], [1, P]]))\
                        .then_inc(rel_in, 16)
                pool.wait_ge(rel_in, 48)
                pool.memset(relt[0:64, 0, :, 0:64], NEG).then_inc(rel_made, 1)

            constants()
            pool.wait_ge(w_hi_made, 1)
            pool.tensor_tensor(left(w_lo[:, 0]), left(raw[:, 0]), left(w_hi[:, 0].bitcast(F32)), ALU.subtract)\
                .then_inc(w_lo_made, 1)
            for u in range(U_XBC, U_XBC + 3):
                lo(u)
            save_rows()
            lo(U_XBC + 3)
            pool.wait_ge(acs_out, 16)
            pool.wait_ge(turned, R_H + 8)
            ssd_row(0)
            ssd_row(1)
            for u in (U_XBC + 4, U_XBC + 5, U_Z, U_Z + 1):
                lo(u)
            ssd_row(2)
            ssd_row(3)
            for u in range(U_Z + 2, U_V + 2):
                lo(u)
            rms_root(0, RMS_EPS)
            for u in range(U_V + 2, U_QK1 + 1):
                lo(u)
            pool.wait_ge(cum_out, 16)
            pool.wait_ge(turned, R_SSM + 8)
            fox_row(0)
            fox_row(1)
            for s in range(16):
                if s % 2 == 0 and s < 12:
                    lo(U_QK1 + s // 2 + 1)
                elif s == 12:
                    lo(U_WO1 + 1)
                if s < 14:
                    fox_row(s + 2)
            for u in range(U_WO1 + 2, U_WO2 + 1):
                lo(u)
            rms_root(1, RMS_EPS)
            pool.wait_ge(o_made, 16)
            pool.dma_start(xre, x_v).then_inc(xre_in, 16)
            load_row(1, ln1_g)
            load_row(2, ln1_b)
            relative()
            for b in range(4):
                lo(U_WO2 + b + 1)
            pool.wait_ge(evac[0], 4 * (N_WO2[0] + 1))
            pool.wait_ge(evac[1], 4 * (N_WO2[1] + 1))
            pool.wait_ge(sum_made, 8)
            pool.memset(yacc, 0.0).then_inc(acc0, 1)
            ln_root(0)

            def feed_forward(u0, times):
                with pool.Fori(0, times) as i:
                    for b in range(8):
                        lo(u0 + b + 1, i, 8)

            feed_forward(U_FF1, QUARTERS)
            load_row(1, ln2_g)
            load_row(2, ln2_b)
            ln_root(1)
            rms_root(2, EPS2)
            lo(U_QKV2 + 1)
            lo(U_QKV2 + 2)
            relative_tiles()
            for u in range(U_QKV2 + 3, U_CP):
                lo(u)
            lo(U_CP)
            pool.wait_ge(qk_sq, 2)
            inv_root(64, st[:, 0:64], st[:, 0:64], 1.0 / HD, EPS2, qk_rs)
            for u in range(U_CP + 1, U_FF2 + 1):
                lo(u)
            rms_root(3, EPS2)
            feed_forward(U_FF2, QUARTERS - 1)
            for b in range(7):
                lo(U_FF2 + 8 * (QUARTERS - 1) + b + 1)

        @block.scalar
        def _(act):
            link = Link(act, act_link)

            def hi(u0, i=0, per=0, ada_per=0, late=False):
                act.wait_ge(landed[u0 % 2], at(i, ada_per * 8 + 8 * per, 16 * (u0 // 2 + 1 + (u0 % 2 == 0) + ada_before(u0))))
                if not (isinstance(i, int) and i * per + u0 < 2):
                    act.wait_ge(ticks, at(i, 2 * per, 2 * u0 - 2 + 2 * late))
                part = left if u0 == U_DTF else lambda ap: ap
                act.activation(part(w_hi[:, u0 % 2]), part(raw[:, u0 % 2]), ACT.Copy).then_inc(w_hi_made, 1)

            def tile_hi(m0, buf, k):
                act.wait_ge(tile_made, m0 + 1)
                act.activation(a_hi[buf][:, k], tmp[:, m0 % 2], ACT.Copy).then_inc(a_hi_made, 1)

            def turned_hi(r0, buf, k, b, scale, bias=None):
                act.wait_ge(turned, r0 + k + 1)
                if bias is None:
                    act.activation(a_hi[buf][:, k], bank[b][:], ACT.Copy, scale=scale).then_inc(a_hi_made, 1)
                else:
                    act.activation(a_hi[buf][:, k], bank[b][:], ACT.Identity, scale=scale, bias=bias).then_inc(a_hi_made, 1)

            def read_rows(u0, s, dst, func=ACT.Copy):
                for t in range(TB):
                    act.wait_ge(ticks, 2 * u0 + 3 + t // 2)
                    act.activation(dst(t), bank[4 * s + t][:], func).then_inc(evac[s], 1)

            def pair_rows(u0, s, dst, func=ACT.Copy):
                hi(u0 + 1)
                hi(u0 + 2)
                read_rows(u0, s, dst, func)

            def rms(turn, src, dst, after, n):
                for t in range(TB):
                    act.wait_ge(after, n(t))
                    act.activation(tmp[:].rearrange("p a b -> p (a b)"), src[:, t], ACT.Square,
                                   accum_out=st[:, t:t + 1]).then_inc(y_sq, 1)
                    act.wait_ge(y_sq, 4 * turn + t + 1)
                act.wait_ge(rs_made, turn + 1)
                for t in range(TB):
                    act.activation(dst[:, t], src[:, t], ACT.Copy, scale=st[:, 4 + t:5 + t]).then_inc(y_norm, 1)

            def squares(turn, src, junk, after, n):
                for t in range(TB):
                    act.wait_ge(after, n(t))
                    act.activation(junk, src[:, t], ACT.Square, accum_out=st[:, t:t + 1]).then_inc(y_sq, 1)
                    act.wait_ge(y_sq, 4 * turn + t + 1)

            def probabilities(h, src, dst):
                act.wait_ge(mx_made, h + 1)
                if h >= 2:
                    act.wait_ge(o_made, h - 1)
                for q in range(TB):
                    n = (q + 1) * P
                    act.activation(dst[:, QO[q]:QO[q] + n], src(q), ACT.Exp, bias=mxs[:, h % 2, q:q + 1],
                                   accum_out=rsum[:, h % 2, q:q + 1]).then_inc(p_made, 1)

            def copy_probT(h, dst):
                if h:
                    act.wait_ge(o_mm, h)
                for m, (b, n) in enumerate(((7, 4), (2, 4), (3, 2))):
                    act.wait_ge(pt_t, 3 * h + m + 1)
                    act.activation(dst[:, 512 * m:512 * m + n * P], bank[b][:, 0:n * P], ACT.Copy).then_inc(pt_made, 1)

            def feed_forward(u0, m0, n0, i, last):
                for b in range(2):
                    for j in range(4):
                        if j % 2 == 0:
                            hi(u0 + 2 * b + j // 2 + 1, i, 8)
                        k = 4 * b + j
                        act.wait_ge(ticks, at(i, 16, 2 * (u0 + 2 * b) + j + 1))
                        act.wait_ge(tile_made, at(i, 8, m0 + k - 1))
                        act.activation(rl[:, k % 2], bank[4 * b + j][:], ACT.Relu).then_inc(evac[b], 1)
                        act.wait_ge(evac[b], at(i, 8, 4 * n0[b] + j + 1))
                        act.activation(a_hi[1][:, k], rl[:, k % 2], ACT.Square).then_inc(a_hi_made, 1)
                for b in range(4, 8):
                    if not (last and b >= 7):
                        hi(u0 + b + 1, i, 8)

            def g_row(turn, b):
                for half in range(2):
                    act.wait_ge(g_mm, 2 * turn + half + 1)
                    act.activation(row[:, 0, 512 * half:512 * half + 512], bank[b + half][:], ACT.Copy).then_inc(g_made, 1)

            act.wait_ge(vecs_made, 1)
            act.activation(cact[:], v1[:, V_C:V_C + KT], ACT.Silu).then_inc(c_made, 1)
            hi(U_DTF)
            act.wait_ge(mod_made, 1)
            for k in range(KT):
                turned_hi(R_H, 0, k, k, mod[:, 8 + k:9 + k], mod[:, k:k + 1])
            hi(U_XBC)
            act.wait_ge(small_in, 64)
            act.wait_ge(consts, 7)
            act.activation(col64[0:16, 3:4], col64[0:16, 2:3], ACT.Exp).then_inc(a_col, 1)
            act.wait_ge(dtf_abs, 1)
            act.activation(dtf[0:64, 2], dtf[0:64, 1], ACT.Exp, scale=-1.0).then_inc(dtf_exp, 1)
            hi(U_XBC + 1)

            def conv_silu(i, last):
                for j in range(4):
                    if j % 2 == 0 and not last:
                        hi(U_XBC + j // 2 + 2, i, 2, 4)
                    act.wait_ge(evac[0], at(i, 4, 4 * N_XBC[0] + j + 1))
                    tile = xbc[:, bass.ds(at(i, 4, j), 1), :].rearrange("p a b -> p (a b)")
                    act.activation(tile, tile, ACT.Silu).then_inc(conv_act, 1)

            def read_z(n):
                act.wait_ge(ticks, 2 * U_Z + n + 1)
                act.activation(z_y[:, n % 4, 512 * (n // 4):512 * (n // 4) + 512], bank[6][:], ACT.Silu).then_inc(z_read, 1)

            def decays(ch):
                e, b = ex2[:, ch % 2], bc[:, ch % 2]
                act.wait_ge(dta_made, 1)
                if ch >= 2:
                    act.wait_ge(prev_made, 2 * ch - 2)
                act.activation(e[:, 0], dta[:, 4 + ch, 0:16], ACT.Exp).then_inc(ex_made, 1)
                act.wait_ge(bc_in[ch % 2], 16 * (ch // 2 + 1))
                act.activation(e[:, 1], b[:, :, P - 1], ACT.Exp).then_inc(ex_made, 1)
                act.wait_ge(ex_in, ch + 1)
                act.activation(e[:, 2], e[:, 2], ACT.Exp).then_inc(ex_made, 1)
                act.wait_ge(bc_sub, ch + 1)
                act.activation(b, b, ACT.Exp).then_inc(bc_exp, 1)

            with act.Fori(0, 2) as i:
                conv_silu(i, False)
            conv_silu(2, True)
            hi(U_Z)
            hi(U_Z + 1)
            read_z(0)
            for b in range(10):
                act.wait_ge(xs_t, b + 1)
                dst = xs[:, b // 2, 512 * (b % 2):512 * (b % 2) + 512] if b < 8 else \
                    btok[:, 2 * (b - 8):2 * (b - 8) + 2].rearrange("p a b c -> p (a b c)")
                act.activation(dst, bank[XS_BANKS[b % 4]][:], ACT.Copy).then_inc(xs_made, 1)
            decays(0)
            read_z(1)
            for ch in range(TB):
                if ch < TB - 1:
                    decays(ch + 1)
                for n in Z_TILES[ch]:
                    read_z(n)
                if ch == 1:
                    hi(U_Z + 2, late=True)
                    hi(U_Z + 3)


            def qk_tile(g, j, u, b):
                act.wait_ge(ticks, 2 * u + j + 1)
                act.activation(qk[:, g % 2, j], bank[b][:], ACT.Copy, scale=HD ** -0.5 if j < 2 else 1.0).then_inc(qk_read, 1)

            hi(U_QK, late=True)
            hi(U_QK + 1)
            for j in range(2):
                qk_tile(0, j, U_QK, (6, 5)[j % 2])
            hi(U_V)
            for k in range(4):
                turned_hi(R_SSM, 1, k, k, v0[:, V_SSM + k:V_SSM + k + 1])
            qk_tile(0, 2, U_QK, 6)
            for k in range(4, 8):
                turned_hi(R_SSM, 1, k, k - 4, v0[:, V_SSM + k:V_SSM + k + 1])
            qk_tile(0, 3, U_QK, 5)
            hi(U_V + 1)
            squares(0, z_y, tmp[:].rearrange("p a b -> p (a b)"), yz_made, lambda t: t + 1)
            hi(U_V + 2)
            read_rows(U_V, 0, lambda t: vtok[:, t, 0:512])
            hi(U_V + 3)
            hi(U_V + 4)
            read_rows(U_V + 2, 1, lambda t: vtok[:, t, 512:1024])

            def wo1_tile(n):
                act.wait_ge(ticks, 2 * U_WO1 + n + 1)
                if n == 0:
                    act.wait_ge(rs_made, 1)
                t, half = n % 4, n // 4
                act.activation(yacc[:, t, 512 * half:512 * half + 512], bank[n % 2][:], ACT.Copy,
                               scale=st[:, 4 + t:5 + t]).then_inc(yacc_read, 1)

            for s in range(18):
                if s == 12:
                    hi(U_WO1 + 1)
                elif s == 16:
                    hi(U_WO1 + 2, late=True)
                    hi(U_WO1 + 3)
                if s >= 2:
                    copy_probT(s - 2, probT)
                if s < 12:
                    if s % 2 == 0:
                        hi(U_QK1 + s // 2 + 1)
                    qk_tile(s // 4 + 1, s % 4, U_QK1 + 2 * (s // 4), s % 2)
                if 1 <= s < 17:
                    h = s - 1
                    probabilities(h, lambda q: prob[:, h % 2, QO[q]:QO[q] + (q + 1) * P], prob[:, h % 2])
                for n in WO1_TILES[s]:
                    wo1_tile(n)
            hi(U_WO2, late=True)
            for k in range(KT):
                if k == 6:
                    g_row(0, 4)
                turned_hi(R_ATT, 1, k, ATT_BANKS[k], v1[:, V_ATT + k:V_ATT + k + 1])
            squares(1, att, tmp[:].rearrange("p a b -> p (a b)"), o_made, lambda t: 16)
            for b in range(4):
                hi(U_WO2 + b + 1)
            for k in range(KT):
                turned_hi(R_X1, 0, k, k, mod[:, 32 + k:33 + k], mod[:, 24 + k:25 + k])
            with act.Fori(0, QUARTERS) as i:
                feed_forward(U_FF1, M_HID1, N_FF1, i, False)
            g_row(1, 0)
            rms(2, x1, n2, ln_made, lambda t: 4 + t + 1)
            for k in range(KT):
                turned_hi(R_N2, 0, k, k, v1[:, V_N1 + k:V_N1 + k + 1])
            for n in range(3):
                pair_rows(U_QKV2 + 2 * n, n % 2, lambda t: qkv2[:, n, t])
            for n in range(2):
                for j in range(4):
                    if j % 2 == 0:
                        hi(U_CP + 2 * n + j // 2 + 1)
                    act.wait_ge(ticks, 2 * (U_CP + 2 * n) + j + 1)
                    act.activation(cp[:, 4 * n + j], bank[4 * (1 - n) + j][:], ACT.Copy).then_inc(evac[1 - n], 1)
            for k in range(4):
                tile_hi(M_MIX + k, 1, 4 + k)
            for s in range(10):
                if 1 <= s < 9:
                    def score(q):
                        b, o = SB[q]
                        return bank[b][:, o:o + (q + 1) * P]
                    probabilities(16 + s - 1, score, prob2[:, (s - 1) % 2])
                if s >= 2:
                    copy_probT(16 + s - 2, prob2T)
            for k in range(4):
                turned_hi(R_ATT2, 1, k, k, 1.0)
            for b in range(4):
                hi(U_WO3 + b + 1)
            act.wait_ge(evac[0], 4 * (N_WO3[0] + 1))
            rms(3, x1, n2, evac[1], lambda t: 4 * (N_WO3[1] + 1))
            for k in range(KT):
                turned_hi(R_N3, 0, k, k, v1[:, V_N2 + k:V_N2 + k + 1])
            with act.Fori(0, QUARTERS - 1) as i:
                feed_forward(U_FF2, M_HID2, N_FF2, i, False)
            feed_forward(U_FF2, M_HID2, N_FF2, QUARTERS - 1, True)

        @block.vector
        def _(dve):
            link = Link(dve, dve_link)

            def tile_lo(t0, m0, buf, k, i=0, per=0):
                dve.wait_ge(a_hi_made, at(i, per, t0 + 1))
                dve.tensor_tensor(a_lo[buf][:, k], tmp[:, m0 % 2], a_hi[buf][:, k].bitcast(F32), ALU.subtract)\
                    .then_inc(a_lo_made, 1)

            def tmp_free(t0, i=0, per=0):
                if not (isinstance(i, int) and i * per + t0 < 2):
                    dve.wait_ge(a_lo_made, at(i, per, t0 - 1))

            def split_affine(t0, m0, buf, scale, bias):
                for k in range(KT):
                    dve.wait_ge(a_hi_made, t0 + k + 1)
                    tmp_free(t0 + k)
                    dve.tensor_scalar(tmp[:, k % 2], bank[k][:], scale(k), bias(k), ALU.mult, ALU.add).then_inc(tile_made, 1)
                    dve.wait_ge(tile_made, m0 + k + 1)
                    tile_lo(t0 + k, m0 + k, buf, k)

            def split_turned(t0, buf, scale, banks):
                for k in range(len(banks)):
                    dve.wait_ge(a_hi_made, t0 + k + 1)
                    dve.scalar_tensor_tensor(a_lo[buf][:, k], bank[banks[k]][:], scale(k), a_hi[buf][:, k].bitcast(F32),
                                             ALU.mult, ALU.subtract).then_inc(a_lo_made, 1)

            def maxima(h, src):
                if h:
                    dve.wait_ge(mx_made, h)
                for q in range(TB):
                    ins = dve.reduce_max(rinv[:, 0, q:q + 1], src(q), AX)
                    link(ins)
                if h >= 2:
                    dve.wait_ge(p_made, 4 * (h - 1))
                dve.tensor_scalar(mxs[:, h % 2], rinv[:, 0], -1.0, None, ALU.mult).then_inc(mx_made, 1)

            def output(h, dst):
                dve.wait_ge(p_made, 4 * h + 4)
                if h:
                    dve.wait_ge(o_made, h)
                link(dve.reciprocal(rinv[:, 1], rsum[:, h % 2]))
                dve.wait_ge(o_mm, h + 1)
                dve.tensor_tensor(dst, bank[3][:, 256:512].rearrange("p (t d) -> p t d", t=TB),
                                  rinv[:, 1].unsqueeze(2).broadcast_to([P, TB, HD]), ALU.mult).then_inc(o_made, 1)

            def layer_norm(turn, t):
                for half in range(2):
                    link(dve.bn_stats(stat[:, 2 * t + half], x1[:, t, 512 * half:512 * half + 512]))
                dve.bn_aggr(mv[:, t], stat[:, 2 * t:2 * t + 2].rearrange("p a b -> p (a b)")).then_inc(ln_var, 1)

            def layer_scale(turn):
                dve.wait_ge(ln_rs, turn + 1)
                dve.wait_ge(rows_in, 32 * turn + 32)
                for t in range(TB):
                    link(dve.tensor_scalar(x1[:, t], x1[:, t], mv[:, t, 0:1], st[:, 8 + t:9 + t], ALU.subtract, ALU.mult))
                    link(dve.tensor_tensor(x1[:, t], x1[:, t], row[:, 1], ALU.mult))
                    dve.tensor_tensor(x1[:, t], x1[:, t], row[:, 2], ALU.add).then_inc(ln_made, 1)

            def feed_forward(u0, t0, m0, n0, acc, i):
                for b in range(2):
                    for j in range(4):
                        k = 4 * b + j
                        dve.wait_ge(evac[b], at(i, 8, 4 * n0[b] + j + 1))
                        tmp_free(t0 + k, i, 8)
                        dve.tensor_tensor(tmp[:, k % 2], rl[:, k % 2], rl[:, k % 2], ALU.mult).then_inc(tile_made, 1)
                        dve.wait_ge(tile_made, at(i, 8, m0 + k + 1))
                        tile_lo(t0 + k, m0 + k, 1, k, i, 8)
                for b in range(2):
                    for t in range(TB):
                        dve.wait_ge(ticks, at(i, 16, 2 * (u0 + 4 + 2 * b) + 3 + t // 2))
                        dve.wait_ge(evac[b], at(i, 8, 4 * (n0[b] + 1) + t))
                        part = acc[:, t, 512 * b:512 * b + 512]
                        dve.tensor_tensor(part, bank[4 * b + t][:], part, ALU.add).then_inc(evac[b], 1)

            def start():
                dve.wait_ge(vecs_t, 1)
                dve.tensor_copy(vec[:].rearrange("p a b -> p (a b)"), bank[7][:, 0:256]).then_inc(vecs_made, 1)
                dve.wait_ge(vecs_made, 1)
                dve.wait_ge(ada_used, ADA_EARLY)
                link(dve.tensor_tensor(mod[:, 0:16], bank[7][:, 256:272], v0[:, V_BADA:V_BADA + 16], ALU.add))
                dve.tensor_scalar(mod[:, 8:16], mod[:, 8:16], 1.0, None, ALU.add).then_inc(mod_made, 1)
                split_affine(T_H, M_H, 0, lambda k: mod[:, 8 + k:9 + k], lambda k: mod[:, k:k + 1])

            def late_mod():
                dve.wait_ge(late_used, N_ADA - ADA_EARLY)
                link(dve.tensor_tensor(mod[:, 16:48], bank[7][:, 0:32], v0[:, V_BADA + 16:V_BADA + 48], ALU.add))
                link(dve.tensor_scalar(mod[:, 16:24], mod[:, 16:24], 1.0, None, ALU.add))
                dve.tensor_scalar(mod[:, 32:48], mod[:, 32:48], 1.0, None, ALU.add).then_inc(late_made, 1)

            def softplus():
                W = [dtf[0:64, n] for n in range(6)]
                dve.wait_ge(small_in, 64)
                dve.wait_ge(consts, 7)
                dve.wait_ge(a_col, 1)
                link(dve.tensor_scalar(col64[0:16, 3:4], col64[0:16, 3:4], -1.0, None, ALU.mult))
                dve.wait_ge(ticks, 2)
                dve.tensor_scalar(W[0], bank[0][0:64, :], col64[:, 0:1], col64[:, 1:2], ALU.add, ALU.mult).then_inc(evac[0], 4)
                dve.wait_ge(evac[0], 4)
                dve.scalar_tensor_tensor(W[1], W[0], -1.0, W[0], ALU.mult, ALU.max).then_inc(dtf_abs, 1)
                dve.wait_ge(dtf_exp, 1)
                link(dve.tensor_scalar(W[3], W[2], 2.0, None, ALU.add))
                link(dve.reciprocal(W[3], W[3]))
                link(dve.tensor_tensor(W[3], W[2], W[3], ALU.mult))
                link(dve.tensor_tensor(W[4], W[3], W[3], ALU.mult))
                link(dve.tensor_scalar(W[5], W[4], 1.0 / 19, None, ALU.mult))
                for n in range(17, 1, -2):
                    link(dve.scalar_tensor_tensor(W[5], W[5], 1.0 / n, W[4], ALU.add, ALU.mult))
                link(dve.scalar_tensor_tensor(W[5], W[5], 1.0, W[3], ALU.add, ALU.mult))
                link(dve.tensor_scalar(W[0], W[0], 0.0, None, ALU.max))
                link(dve.scalar_tensor_tensor(W[0], W[5], 2.0, W[0], ALU.mult, ALU.add))
                link(dve.tensor_scalar(W[2], W[0], col64[:, 3:4], None, ALU.mult))
                for ch in range(TB):
                    part = slice(ch * P, ch * P + P)
                    dve.tensor_tensor_scan(dtf[0:16, 1, part], ones[0:16, :], dtf[0:16, 2, part], 0.0,
                                           ALU.mult, ALU.add).then_inc(scanned, 1)
                dve.tensor_tensor_scan(dtf[32:48, 1, :], ones[32:48, 0:1].broadcast_to([16, S]), dtf[32:48, 2, :], 0.0,
                                       ALU.mult, ALU.add).then_inc(scanned, 1)

            def convolve(i):
                for j in range(4):
                    dve.wait_ge(ticks, at(i, 4, 2 * U_XBC + j + 1))
                    tile = xbc[:, bass.ds(at(i, 4, j), 1), :].rearrange("p a b -> p (a b)")

                    def tap(n):
                        return v0[:, bass.ds(at(i, 4, V_CONVW + n * CT + j), 1)]

                    link(dve.tensor_scalar(tile, bank[j][:], tap(3), v0[:, bass.ds(at(i, 4, V_CONVB + j), 1)],
                                           ALU.mult, ALU.add))
                    for lag in (1, 2, 3):
                        ins = dve.scalar_tensor_tensor(tile[:, lag:], bank[j][:, 0:S - lag], tap(3 - lag),
                                                       tile[:, lag:], ALU.mult, ALU.add)
                        if lag < 3:
                            link(ins)
                        else:
                            ins.then_inc(evac[0], 1)

            def by_head(ap):
                return ap.rearrange("p (h d) -> p h d", d=HD)

            def per_head(ap):
                return ap.unsqueeze(2).broadcast_to([P, SSM_H, HD])

            def ssd():
                dve.wait_ge(dta_t, 1)
                dve.tensor_copy(dta[:].rearrange("p a b -> p (a b)"), bank[2][:]).then_inc(dta_made, 1)
                dve.wait_ge(dta_made, 1)
                for b in range(2):
                    dve.wait_ge(cb_done, b + 1)
                    dve.tensor_tensor(cbm[:, 2 * b:2 * b + 2].rearrange("p a (g l) -> p (a g) l", g=2),
                                      bank[3 + b][:].rearrange("p (a l) -> p a l", a=4),
                                      keep.unsqueeze(1).broadcast_to([P, 4, P]), ALU.mult).then_inc(cb_evac, 1)
                dve.wait_ge(cb_evac, 2)
                dve.wait_ge(xs_made, 10)
                dve.wait_ge(cum_out, 16)

                def decay_in(ch):
                    b, acs = bc[:, ch % 2], dta[:, 4 + ch, 0:16]
                    dve.wait_ge(bc_in[ch % 2], 16 * (ch // 2 + 1))
                    if ch >= 2:
                        dve.wait_ge(prev_made, 2 * ch - 2)
                    dve.tensor_tensor(ex2[:, ch % 2, 2], b[:, :, P - 1], acs, ALU.subtract).then_inc(ex_in, 1)
                    dve.wait_ge(ex_made, 3 * ch + 3)
                    link(dve.tensor_tensor(b, b, acs.unsqueeze(2).broadcast_to([P, SSM_H, P]), ALU.subtract))
                    dve.tensor_scalar(b, b, 0.0, None, ALU.min).then_inc(bc_sub, 1)

                def inputs(ch):
                    if ch:
                        dve.wait_ge(y_mm, ch)
                    dve.tensor_tensor(by_head(xc), by_head(xs[:, ch]), per_head(dta[:, ch, 0:16]), ALU.mult).then_inc(xc_made, 1)
                    dve.wait_ge(xc_made, ch + 1)
                    dve.tensor_tensor(by_head(xd), by_head(xc), per_head(ex2[:, ch % 2, 2]), ALU.mult).then_inc(xd_made, 1)
                    link(dve.tensor_tensor(by_head(xs[:, ch]), by_head(xs[:, ch]), per_head(dsk[:]), ALU.mult))

                decay_in(0)
                dve.wait_ge(xs_made, 10)
                dve.wait_ge(cum_out, 16)
                inputs(0)
                for ch in range(TB):
                    e, yc = ex2[:, ch % 2], xs[:, ch]
                    dve.wait_ge(bc_exp, ch + 1)
                    b4 = bc[:, ch % 2].rearrange("p (g e) l -> p g e l", g=2)
                    c4 = cbm[:, ch].rearrange("p (g l) -> p g l", g=2).unsqueeze(2).broadcast_to([P, 2, 8, P])
                    dve.tensor_tensor(b4, b4, c4, ALU.mult).then_inc(score_made, 1)
                    if ch < TB - 1:
                        decay_in(ch + 1)
                    dve.wait_ge(y_mm, ch + 1)
                    for g in range(2):
                        part = slice(512 * g, 512 * g + 512)
                        if ch:
                            d = e[:, 0, 8 * g:8 * g + 8].unsqueeze(2).broadcast_to([P, 8, HD])
                            link(dve.tensor_tensor(by_head(off[:, part]), by_head(bank[2 + g][:]), d, ALU.mult))
                            link(dve.tensor_tensor(yc[:, part], off[:, part], yc[:, part], ALU.add))
                        dve.tensor_tensor(yc[:, part], bank[g][:], yc[:, part], ALU.add).then_inc(y_made, 1)
                    if ch < TB - 1:
                        if ch:
                            link(dve.tensor_tensor(by_head(prev), by_head(prev), per_head(e[:, 1]), ALU.mult))
                        for g in range(2):
                            part = slice(512 * g, 512 * g + 512)
                            if ch:
                                dve.tensor_tensor(prev[:, part], bank[4 + g][:], prev[:, part], ALU.add).then_inc(prev_made, 1)
                            else:
                                dve.tensor_copy(prev[:, part], bank[4 + g][:]).then_inc(prev_made, 1)
                        dve.wait_ge(prev_made, 2 * ch + 2)
                        inputs(ch + 1)
                dve.wait_ge(y_made, 2 * TB)
                for t in range(TB):
                    dve.wait_ge(z_read, 5 + t)
                    dve.tensor_tensor(z_y[:, t], xs[:, t], z_y[:, t], ALU.mult).then_inc(yz_made, 1)

            def fox_scores(h):
                dve.wait_ge(ncm_made, h + 1)
                if h >= 2:
                    dve.wait_ge(pt_t, 3 * (h - 1))
                dve.wait_ge(s_mm, h + 1)
                for q in range(TB):
                    b, o = SB[q]
                    dst = prob[:, h % 2, QO[q]:QO[q] + (q + 1) * P]
                    if q:
                        link(dve.tensor_tensor(dst[:, 0:q * P], bank[b][:, o:o + q * P], ncb[:, h % 2, 0:q * P], ALU.add))
                    ins = dve.tensor_tensor(dst[:, q * P:q * P + P], bank[b][:, o + q * P:o + q * P + P],
                                            ncm[:, h % 2, q * P:q * P + P], ALU.add)
                    if q < TB - 1:
                        link(ins)
                    else:
                        ins.then_inc(s_made, 1)
                dve.wait_ge(s_made, h + 1)
                maxima(h, lambda q: prob[:, h % 2, QO[q]:QO[q] + (q + 1) * P])

            def conv_pool():
                dve.wait_ge(evac[1], 4 * (N_CP[1] + 1))
                dve.wait_ge(evac[0], 4 * (N_CP[0] + 1))
                for n in range(2):
                    z, y = cp[:, 2 + n], tmp[:, n]
                    tmp_free(T_MIX + n)
                    link(dve.tensor_tensor(z, z, cp[:, 4 + n], ALU.mult))
                    link(dve.tensor_scalar(y, z, v1[:, V_CW2 + 4 + n:V_CW2 + 5 + n], None, ALU.mult))
                    for lag in (1, 2):
                        w = v1[:, V_CW2 + 4 - 2 * lag + n:V_CW2 + 5 - 2 * lag + n]
                        link(dve.scalar_tensor_tensor(y[:, lag:], z[:, 0:S - lag], w, y[:, lag:], ALU.mult, ALU.add))
                    dve.tensor_tensor(y, y, cp[:, n], ALU.mult).then_inc(tile_made, 1)
                for n in range(2):
                    tile_lo(T_MIX + n, M_MIX + n, 1, 4 + n)
                cnt = pinv[:, 1]
                link(dve.tensor_tensor_scan(cnt, ones[:, 0:16], ones[:, 0:16], 0.0, ALU.mult, ALU.add))
                for n, po, w in ((0, 0, 2), (0, 64, 4), (1, 0, 8), (1, 64, 16)):
                    link(dve.tensor_scalar(pinv[po:po + 64, n], cnt[po:po + 64, :], float(w), None, ALU.min))
                link(dve.reciprocal(pinv[:].rearrange("p a b -> p (a b)"), pinv[:].rearrange("p a b -> p (a b)")))
                for n in range(2):
                    u, m = cp[:, 6 + n], cp[:, 2 + n]
                    src, at_ = u, 0
                    for lag in (1, 2) if n == 0 else (1, 2, 4, 8):
                        dst = cp[:, at_]
                        link(dve.tensor_copy(dst[:, 0:lag], src[:, 0:lag]))
                        link(dve.tensor_tensor(dst[:, lag:], src[:, lag:], src[:, 0:S - lag], ALU.add))
                        src, at_ = dst, 1 - at_
                    for po, place, w in ((0, at_, 2 if n == 0 else 8), (64, 1 - at_, 4 if n == 0 else 16)):
                        h = slice(po, po + 64)
                        link(dve.tensor_tensor(m[h, 0:16], cp[h, place, 0:16], pinv[h, n], ALU.mult))
                        link(dve.tensor_tensor(m[h, 0:16], m[h, 0:16], u[h, 0:16], ALU.subtract))
                        ins = dve.scalar_tensor_tensor(m[h, 16:], cp[h, place, 16:], 1.0 / w, u[h, 16:], ALU.mult, ALU.subtract)
                        if po:
                            ins.then_inc(m_made, 1)
                            dve.wait_ge(m_made, n + 1)
                        else:
                            link(ins)
                for n in range(2):
                    dve.wait_ge(m_mm, n + 1)
                    tmp_free(T_MIX + 2 + n)
                    dve.tensor_scalar(tmp[:, n], bank[n][:], v1[:, V_PS + n:V_PS + n + 1], None, ALU.mult).then_inc(tile_made, 1)
                for n in range(2):
                    tile_lo(T_MIX + 2 + n, M_MIX + 2 + n, 1, 6 + n)

            def head_norm():
                dve.wait_ge(evac[0], 4 * (N_QKV2[0] + 1))
                dve.wait_ge(evac[1], 4 * (N_QKV2[1] + 1))
                dve.wait_ge(turned, R_N2 + 8)
                for n in range(2):
                    link(dve.tensor_tensor(sq2, qkv2[:, n], qkv2[:, n], ALU.mult))
                    dve.reduce_sum(st[:, 32 * n:32 * n + 32], sq2.rearrange("p t (h d) -> p (t h) d", d=HD), AX)\
                        .then_inc(qk_sq, 1)
                    dve.wait_ge(qk_sq, n + 1)
                dve.wait_ge(qk_rs, 1)
                for n in range(2):
                    q = qkv2[:, n].rearrange("p t (h d) -> p (t h) d", d=HD)
                    dve.tensor_tensor(q, q, st[:, 32 * n:32 * n + 32].unsqueeze(2).broadcast_to([P, 32, HD]), ALU.mult)\
                        .then_inc(qk_made, 1)

            start()
            softplus()
            with dve.Fori(0, 3) as i:
                link.enter(i, 12)
                convolve(i)
            link.leave(3)
            ssd()
            late_mod()
            split_turned(T_SSM, 1, lambda k: v0[:, V_SSM + k:V_SSM + k + 1], (0, 1, 2, 3, 0, 1, 2, 3))
            for s in range(18):
                if s >= 2:
                    h = s - 2
                    output(h, att[:, :, h * HD:h * HD + HD])
                if s < 16:
                    fox_scores(s)
            split_turned(T_ATT, 1, lambda k: v1[:, V_ATT + k:V_ATT + k + 1], ATT_BANKS)
            dve.wait_ge(xre_in, 16)
            dve.wait_ge(g_made, 2)
            dve.wait_ge(yacc_read, 8)
            for t in range(TB):
                link(dve.tensor_tensor(yacc[:, t], yacc[:, t], row[:, 0], ALU.mult))
                link(dve.scalar_tensor_tensor(yacc[:, t], xre[:, t], ALPHA, yacc[:, t], ALU.mult, ALU.add))
            dve.wait_ge(rs_made, 2)
            for half in range(2):
                for t in range(TB):
                    part = slice(512 * half, 512 * half + 512)
                    dve.wait_ge(ticks, 2 * (U_WO2 + 2 * half) + 3 + t // 2)
                    dve.scalar_tensor_tensor(x1[:, t, part], bank[4 * half + t][:], st[:, 4 + t:5 + t], row[:, 0, part],
                                             ALU.mult, ALU.mult).then_inc(evac[half], 1)
                    dve.wait_ge(evac[half], 4 * N_WO2[half] + t + 1)
                    dve.tensor_tensor(x1[:, t, part], x1[:, t, part], yacc[:, t, part], ALU.add).then_inc(sum_made, 1)
            dve.wait_ge(sum_made, 8)
            for t in range(TB):
                layer_norm(0, t)
            layer_scale(0)
            split_affine(T_X1, M_X1, 0, lambda k: mod[:, 32 + k:33 + k], lambda k: mod[:, 24 + k:25 + k])
            dve.wait_ge(acc0, 1)
            with dve.Fori(0, QUARTERS) as i:
                feed_forward(U_FF1, T_HID1, M_HID1, N_FF1, yacc, i)
            dve.wait_ge(g_made, 4)
            for t in range(TB):
                link(dve.tensor_tensor(yacc[:, t], yacc[:, t], row[:, 0], ALU.mult))
                dve.scalar_tensor_tensor(x1[:, t], x1[:, t], ALPHA, yacc[:, t], ALU.mult, ALU.add).then_inc(sum_made, 1)
                dve.wait_ge(sum_made, 8 + t + 1)
                layer_norm(1, t)
            layer_scale(1)
            split_turned(T_N2, 0, lambda k: v1[:, V_N1 + k:V_N1 + k + 1], range(KT))
            head_norm()
            conv_pool()
            for n in range(2):
                for k in range(4):
                    dve.wait_ge(q2_t, 4 * n + k + 1)
                    dve.tensor_scalar(qkT2[:, n, k], bank[4 * n + k][:], v1[:, V_QG + n:V_QG + n + 1],
                                      HD ** -0.5 if n == 0 else 1.0, ALU.mult, ALU.mult).then_inc(q2_made, 1)
            for s in range(10):
                if s >= 2:
                    h = s - 2
                    output(16 + h, att2[:, :, h * HD:h * HD + HD])
                if s < 8:
                    dve.wait_ge(s_mm, 16 + s + 1)
                    maxima(16 + s, lambda q: bank[SB[q][0]][:, SB[q][1]:SB[q][1] + (q + 1) * P])
            split_turned(T_MIX + 4, 1, lambda k: 1.0, range(4))
            for half in range(2):
                for t in range(TB):
                    part = x1[:, t, 512 * half:512 * half + 512]
                    dve.wait_ge(ticks, 2 * (U_WO3 + 2 * half) + 3 + t // 2)
                    dve.tensor_tensor(part, bank[4 * half + t][:], part, ALU.add).then_inc(evac[half], 1)
            split_turned(T_N3, 0, lambda k: v1[:, V_N2 + k:V_N2 + k + 1], range(KT))
            with dve.Fori(0, QUARTERS) as i:
                feed_forward(U_FF2, T_HID2, M_HID2, N_FF2, x1, i)

        @block.tensor
        def _(pe):
            def three(out_, hi_a, lo_a, hi_b, lo_b, start, stop):
                pe.matmul(out_, hi_a, hi_b, start=start, stop=False)
                pe.matmul(out_, hi_a, lo_b, start=False, stop=False)
                return pe.matmul(out_, lo_a, hi_b, start=False, stop=stop)

            def column_tile(u0, n, act_buf, dst, t0=None, i=0, per=0):
                s = u0 % 2
                if n == 0:
                    pe.wait_ge(w_lo_made, at(i, per, u0 + 1))
                for k in range(KT):
                    if t0 is not None:
                        pe.wait_ge(a_lo_made, t0 + k + 1)
                    w = slice(256 * k + P * n, 256 * k + P * n + P)
                    last = three(dst, w_hi[:, s, w], w_lo[:, s, w], a_hi[act_buf][:, k], a_lo[act_buf][:, k],
                                 k == 0, k == KT - 1)
                last.then_inc(ticks, 1)

            def column_pair(u0, s, n_use, act_buf, t0=None, i=0, per=0, uses=0):
                pe.wait_ge(evac[s], at(i, 4 * uses, 4 * n_use))
                for j in range(4):
                    column_tile(u0 + j // 2, j % 2, act_buf, bank[4 * s + j][:], t0 if j == 0 else None, i, per)

            def row_pair(u0, s, n_use, act_buf, t0=None, i=0, per=0, uses=0, tstep=0):
                if not (isinstance(n_use, int) and isinstance(i, int) and n_use + i * uses == 0):
                    pe.wait_ge(evac[s], at(i, 4 * uses, 4 * n_use))
                for b in range(2):
                    slot = (u0 + b) % 2
                    pe.wait_ge(w_lo_made, at(i, per, u0 + b + 1))
                    order = [(k, t) for k in range(4) for t in range(TB)] if b == 0 else [(k, t) for t in range(TB) for k in range(4)]
                    for m, (k, t) in enumerate(order):
                        kk = 4 * b + k
                        if t0 is not None and (t == 0 and b == 0 or m == 0):
                            pe.wait_ge(a_lo_made, at(i, tstep, t0 + (kk + 1 if b == 0 else KT)))
                        a = slice(P * t, P * t + P)
                        w = slice(512 * k, 512 * k + 512)
                        last = three(bank[4 * s + t][:], a_hi[act_buf][:, kk, a], a_lo[act_buf][:, kk, a],
                                     w_hi[:, slot, w], w_lo[:, slot, w], kk == 0, kk == KT - 1)
                        if m % 8 == 7:
                            last.then_inc(ticks, 1)

            def row_tile(u, n, act_buf, dst):
                for kk in range(KT):
                    slot, a, w = (u + kk // 4) % 2, slice(P * (n % 4), P * (n % 4) + P), slice(512 * (kk % 4), 512 * (kk % 4) + 512)
                    if kk % 4 == 0 and n % 4 == 0:
                        pe.wait_ge(w_lo_made, u + kk // 4 + 1)
                    last = three(dst, a_hi[act_buf][:, kk, a], a_lo[act_buf][:, kk, a],
                                 w_hi[:, slot, w], w_lo[:, slot, w], kk == 0, kk == KT - 1)
                last.then_inc(ticks, 1)

            def ada_unit(src, col, signal):
                for h in range(2):
                    for k in range(KT):
                        last = pe.matmul(bank[7][:, bass.ds(col + h, 1)], src(k, h), cact[:, k:k + 1],
                                         start=k == 0, stop=k == KT - 1)
                last.then_inc(signal, 1)

            def ada_late(n, count, i=0, per=0):
                slot = (n + 1) % 2
                pe.wait_ge(landed[slot], at(i, 48, 16 * count))
                ada_unit(lambda k, h: raw[:, slot, 256 * k + P * h:256 * k + P * h + P], at(i, 2 * per, 2 * n), late_used)

            def turn(src, n=KT, first=0, banks=range(KT)):
                for k in range(first, first + n):
                    for t in range(TB):
                        last = pe.transpose(bank[banks[k]][:, P * t:P * t + P], src[:, t, P * k:P * k + P], ident[:])
                    last.then_inc(turned, 1)

            def evacuated(n0, n1):
                pe.wait_ge(evac[0], 4 * n0)
                pe.wait_ge(evac[1], 4 * n1)

            def probs_t(h, src):
                pe.wait_ge(p_made, 4 * h + 4)
                for b in range(10):
                    m, o = b // 4, b % 4
                    if o == 0 and h:
                        pe.wait_ge(pt_made, 3 * (h - 1) + m + 1)
                        if m == 2:
                            pe.wait_ge(o_made, h)
                    last = pe.transpose(bank[(7, 2, 3)[m]][:, o * P:o * P + P], src[:, b * P:b * P + P], ident[:])
                    if b in (3, 7, 9):
                        last.then_inc(pt_t, 1)

            def values(h, pT, v):
                pe.wait_ge(pt_made, 3 * h + 3)
                for q in range(TB):
                    for k in range(q + 1):
                        b = q * (q + 1) // 2 + k
                        last = pe.matmul(bank[3][:, 256 + q * HD:256 + q * HD + HD], pT[:, b * P:b * P + P], v(k),
                                         start=k == 0, stop=k == q)
                last.then_inc(o_mm, 1)

            def g_row(col, b):
                for half in range(2):
                    for k in range(4):
                        m = col + 4 * half + k
                        last = pe.matmul(bank[b + half][:, k * P:k * P + P], mod[:, m:m + 1].broadcast_to([P, P]), ident[:],
                                         start=True, stop=True)
                    last.then_inc(g_mm, 1)

            pe.wait_ge(consts, 7)
            pe.wait_ge(vecs_in, 16 * 14)
            for n in range(2):
                last = pe.transpose(bank[7][:, P * n:P * n + P], vec_in[:, n, :], ident[:])
            last.then_inc(vecs_t, 1)
            pe.wait_ge(x_in, 16)
            turn(xtok, KT - 1)
            pe.wait_ge(c_made, 1)
            for n in range(ADA_EARLY):
                pe.wait_ge(ada_in[n // 2], 16)
                o = 256 * (n % 2)
                ada_unit(lambda k, h: ada[:, n // 2, k, o + P * h:o + P * h + P], 256 + 2 * n, ada_used)
            pe.wait_ge(mod_made, 1)
            turn(xtok, 1, KT - 1)
            pe.wait_ge(w_lo_made, 1)
            pe.wait_ge(a_lo_made, T_H + 6)
            for k in range(KT):
                pe.wait_ge(a_lo_made, T_H + k + 1)
                w = slice(256 * k, 256 * k + P)
                last = three(bank[0][:], w_hi[:, 0, w], w_lo[:, 0, w], a_hi[0][:, k], a_lo[0][:, k], k == 0, k == KT - 1)
                if k in (3, 7):
                    last.then_inc(ticks, 1)
            with pe.Fori(0, 3) as i:
                for j in range(4):
                    pe.wait_ge(evac[0], at(i, 4, 4 * N_XBC[0]))
                    column_tile(U_XBC + j // 2, j % 2, 0, bank[j][:], None, i, 2)
                    if j == 0:
                        ada_late(0, 2, i, 4)
                        ada_late(1, 4, i, 4)
                    elif j == 1:
                        ada_late(2, 3, i, 4)
                        ada_late(3, 5, i, 4)

            pe.wait_ge(scanned, 5)
            pe.wait_ge(evac[0], 4 * (N_XBC[0] + 3))
            for b in range(8):
                last = pe.transpose(bank[2][:, 64 * b:64 * b + 64], dtf[0:64, b // 4, P * (b % 4):P * (b % 4) + P], ident[0:64, 0:64])
            last.then_inc(dta_t, 1)

            def z_tile(n):
                if n:
                    pe.wait_ge(z_read, n)
                else:
                    pe.wait_ge(a_lo_made, T_H + 8)
                row_tile(U_Z + 2 * (n // 4), n, 0, bank[6][:])

            z_tile(0)
            pe.wait_ge(conv_act, CT)
            for b in range(10):
                if b >= 4:
                    pe.wait_ge(xs_made, b - 3)
                for k in range(4):
                    if b < 8:
                        src = xbc[:, 4 * (b % 2) + k, P * (b // 2):P * (b // 2) + P]
                    else:
                        t, g = 2 * (b - 8) + k // 2, k % 2
                        src = xbc[:, 8 + g, P * t:P * t + P]
                    last = pe.transpose(bank[XS_BANKS[b % 4]][:, P * k:P * k + P], src, ident[:])
                last.then_inc(xs_t, 1)
            for b in range(2):
                pe.wait_ge(xs_made, 7 + b)
                for k in range(4):
                    t, g = 2 * b + k // 2, k % 2
                    part = slice(P * t, P * t + P)
                    last = pe.matmul(bank[3 + b][:, P * k:P * k + P], xbc[:, 8 + g, part], xbc[:, 10 + g, part], start=True, stop=True)
                last.then_inc(cb_done, 1)
            z_tile(1)
            pe.wait_ge(xs_made, 10)
            pe.wait_ge(dta_made, 1)
            pe.wait_ge(cb_evac, 2)
            for ch in range(TB):
                if ch < TB - 1:
                    pe.wait_ge(xd_made, ch + 1)
                    if ch:
                        pe.wait_ge(prev_made, 2 * ch)
                    for g in range(2):
                        last = pe.matmul(bank[4 + g][:], btok[:, ch, g, :], xd[:, 512 * g:512 * g + 512], start=True, stop=True)
                    last.then_inc(st_mm, 1)
                if ch:
                    pe.wait_ge(prev_made, 2 * ch)
                    pe.wait_ge(y_made, 2 * ch)
                    for g in range(2):
                        pe.matmul(bank[2 + g][:], xbc[:, 10 + g, P * ch:P * ch + P], prev[:, 512 * g:512 * g + 512],
                                  start=True, stop=True)
                pe.wait_ge(xc_made, ch + 1)
                pe.wait_ge(score_made, ch + 1)
                for h in range(SSM_H):
                    last = pe.matmul(bank[h // 8][:, HD * (h % 8):HD * (h % 8) + HD], bc[:, ch % 2, h, :],
                                     xc[:, HD * h:HD * h + HD], start=True, stop=True)
                last.then_inc(y_mm, 1)
                if ch == 0:
                    ada_late(12, 11)
                    ada_late(13, 13)
                elif ch == 3:
                    ada_late(14, 13)
                    ada_late(15, 15)
                for n in Z_TILES[ch]:
                    z_tile(n)
            for j in range(4):
                pe.wait_ge(z_read, 8)
                if j >= 2:
                    pe.wait_ge(qk_read, j - 1)
                    pe.wait_ge(yz_made, 4)
                    if j == 3:
                        pe.wait_ge(a_lo_made, T_SSM + 4)
                    turn(z_y, 4, 4 * (j - 2), (0, 1, 2, 3) * 2)
                column_tile(U_QK + j // 2, j % 2, 0, bank[(6, 5)[j % 2]][:])
            pe.wait_ge(a_lo_made, T_SSM + 8)
            row_pair(U_V, 0, N_V[0], 0)
            pe.wait_ge(qk_read, 4)
            pe.wait_ge(late_made, 1)
            row_pair(U_V + 2, 1, N_V[1], 0)
            evacuated(N_V[0] + 1, N_V[1] + 1)

            def filler_free(n):
                if n >= 14:
                    pe.wait_ge(yacc_read, n - 13)
                elif n >= 2:
                    pe.wait_ge(qk_read, 4 + n - 1)

            for s in range(18):
                if s >= 2:
                    probs_t(s - 2, prob[:, s % 2])
                if s < 12:
                    filler_free(s)
                    column_tile(U_QK1 + s // 2, s % 2, 0, bank[s % 2][:])
                if s >= 2:
                    h = s - 2
                    values(h, probT, lambda k: vtok[:, k, h * HD:h * HD + HD])
                if s < 16:
                    pe.wait_ge(qk_read, 4 * (s // 4 + 1))
                    if s:
                        pe.wait_ge(s_made, s)
                    po, tile = HD * (s % 2), (s % 4) // 2
                    q_, k_ = qk[po:po + HD, (s // 4) % 2, tile], qk[po:po + HD, (s // 4) % 2, 2 + tile]
                    for q in range(TB):
                        b, o = SB[q]
                        last = pe.matmul(bank[b][:, o:o + (q + 1) * P], q_[:, P * q:P * q + P], k_[:, 0:(q + 1) * P],
                                         start=True, stop=True)
                    last.then_inc(s_mm, 1)
                for n in WO1_TILES[s]:
                    filler_free(12 + n)
                    row_tile(U_WO1 + 2 * (n // 4), n, 1, bank[n % 2][:])
            pe.wait_ge(s_made, 16)
            pe.wait_ge(pt_made, 48)
            pe.wait_ge(o_made, 16)
            turn(att, 4, 0, ATT_BANKS)
            pe.wait_ge(yacc_read, 8)
            turn(att, 2, 4, ATT_BANKS)
            g_row(16, 4)
            pe.wait_ge(g_made, 2)
            turn(att, 2, 6, ATT_BANKS)
            pe.wait_ge(a_lo_made, T_ATT + 6)
            row_pair(U_WO2, 0, N_WO2[0], 1, T_ATT)
            row_pair(U_WO2 + 2, 1, N_WO2[1], 1)
            evacuated(N_FF1[0], N_FF1[1])
            pe.wait_ge(ln_made, 4)
            turn(x1)

            def feed_forward(u0, t_act, t0, n0):
                pe.wait_ge(a_lo_made, t_act + KT)
                with pe.Fori(0, QUARTERS) as i:
                    for b in range(2):
                        column_pair(u0 + 2 * b, b, n0[b], 0, i=i, per=8, uses=2)
                    for b in range(2):
                        row_pair(u0 + 4 + 2 * b, b, n0[b] + 1, 1, t0 if b == 0 else None, i=i, per=8, uses=2, tstep=8)

            feed_forward(U_FF1, T_X1, T_HID1, N_FF1)
            evacuated(N_QKV2[0], N_QKV2[1])
            g_row(40, 0)
            pe.wait_ge(y_norm, 4)
            pe.wait_ge(g_made, 4)
            turn(n2)
            pe.wait_ge(a_lo_made, T_N2 + 4)
            row_pair(U_QKV2, 0, N_QKV2[0], 0, T_N2)
            row_pair(U_QKV2 + 2, 1, N_QKV2[1], 0)
            row_pair(U_QKV2 + 4, 0, N_QKV2[0] + 1, 0)
            column_pair(U_CP, 1, N_CP[1], 0)
            column_pair(U_CP + 2, 0, N_CP[0], 0)
            evacuated(N_WO3[0], N_WO3[1])
            pe.wait_ge(pool_in, 64)
            for n in range(2):
                pe.wait_ge(m_made, n + 1)
                pe.matmul(bank[n][:], poolw[:, n, :], cp[:, 2 + n], start=True, stop=True).then_inc(m_mm, 1)
            pe.wait_ge(tile_made, M_MIX + 4)
            pe.wait_ge(qk_made, 2)
            for n in range(2):
                for k in range(4):
                    for t in range(TB):
                        last = pe.transpose(bank[4 * n + k][:, P * t:P * t + P], qkv2[:, n, t, P * k:P * k + P], ident[:])
                    last.then_inc(q2_t, 1)
            pe.wait_ge(q2_made, 8)
            pe.wait_ge(rel_made, 1)
            for s in range(10):
                if s >= 2:
                    probs_t(16 + s - 2, prob2[:, s % 2])
                    h = s - 2
                    values(16 + h, prob2T, lambda k: qkv2[:, 2, k, h * HD:h * HD + HD])
                if s < 8:
                    if s:
                        pe.wait_ge(p_made, 4 * (16 + s))
                    po, tile = HD * (s % 2), s // 2
                    q_, k_ = qkT2[po:po + HD, 0, tile], qkT2[po:po + HD, 1, tile]
                    for q in range(TB):
                        b, o = SB[q]
                        n = (q + 1) * P
                        pe.matmul(bank[b][:, o:o + n], q_[:, P * q:P * q + P], k_[:, 0:n], start=True, stop=False)
                        if q >= 2:
                            far = (q - 1) * P
                            pe.matmul(bank[b][:, o:o + far], ones[0:1, 0:P], relc[0:1, s:s + 1].broadcast_to([1, far]),
                                      start=False, stop=False)
                        if q >= 1:
                            pe.matmul(bank[b][:, o + n - 2 * P:o + n - P], relt[:, 1, s, :], flip[:], start=False, stop=False)
                        last = pe.matmul(bank[b][:, o + n - P:o + n], relt[:, 0, s, :], flip[:], start=False, stop=True)
                    last.then_inc(s_mm, 1)
            pe.wait_ge(o_made, 24)
            turn(att2, 4)
            pe.wait_ge(a_lo_made, T_MIX + 8)
            row_pair(U_WO3, 0, N_WO3[0], 1)
            row_pair(U_WO3 + 2, 1, N_WO3[1], 1)
            evacuated(N_FF2[0], N_FF2[1])
            pe.wait_ge(y_norm, 8)
            turn(n2)
            feed_forward(U_FF2, T_N3, T_HID2, N_FF2)


_INS = ["x", "c", "w_ada", "b_ada", "w_in", "conv_w", "conv_b", "dt_bias", "a_log", "d_skip", "ssm_norm_w", "f_bias",
        "attn_norm_w", "w_out", "ln1_g", "ln1_b", "w_ff_in", "w_ff_out", "ln2_g", "ln2_b", "norm1_g_2", "w_in_2",
        "q_norm_g_2", "k_norm_g_2", "rel_bias_2", "conv_w_2", "pool_w_2", "pool_scale_2", "w_out_2", "norm2_g_2",
        "w_mlp1_2", "w_mlp2_2"]


def kernel(**inputs):
    import numpy as _np
    import concourse.bacc as _bacc
    from concourse import mybir as _mybir
    from concourse.bass_utils import run_bass_kernel_spmd as _run

    nc = _bacc.Bacc("TRN2", target_bir_lowering=False, num_devices=1, dynamic_dma_scratch_size=8192)
    arrays, args = {}, []
    for name in _INS:
        a = _np.ascontiguousarray(inputs[name])
        arrays[f"in_{name}_dram"] = a
        args.append(nc.dram_tensor(f"in_{name}_dram", a.shape, _mybir.dt.from_np(a.dtype), kind="ExternalInput").ap())
    args.append(nc.dram_tensor("out_0_dram", (1, S, D), F32, kind="ExternalOutput").ap())
    build(nc, *args)
    r = _run(nc, [arrays], core_ids=[0])
    return r.results[0]["out_0_dram"]
```

```python
from contextlib import ExitStack

import numpy as np

import concourse.bass as bass
from concourse import mybir

F32 = mybir.dt.float32
F32R = mybir.dt.float32r
ALU = mybir.AluOpType
ACT = mybir.ActivationFunctionType
AX = mybir.AxisListType.X

P = 128
S = 512
D = 1024
TB = S // P
KT = D // P
SSM_W, SSM_H, HD, ST = 1024, 16, 64, 128
CONV_DIM = SSM_W + 2 * 2 * ST
CT = CONV_DIM // P
CW = 4
C_Z, C_XBC = 0, SSM_W
C_DT = C_XBC + CONV_DIM
C_Q = C_DT + SSM_H
C_K, C_V = C_Q + 1024, C_Q + 2048
C_F = C_Q + 3072
ALPHA = 2.0 ** 0.25
LN_EPS, RMS_EPS, EPS2 = 1e-5, 1e-5, 1e-6
FF = 4096
QUARTERS = FF // D
NEG = -1e30
H2 = 8
CLIP = 128
NREL = 2 * CLIP + 1
SB = [(4, 384), (6, 0), (4, 0), (5, 0)]
QO = [0, 128, 384, 768]

U_DTF = 0
U_XBC = 1
U_Z = U_XBC + 6
U_QK = U_Z + 4
U_V = U_QK + 2
U_QK1 = U_V + 4
U_WO1 = U_QK1 + 6
U_WO2 = U_WO1 + 4
U_FF1 = U_WO2 + 4
U_QKV2 = U_FF1 + 8 * QUARTERS
U_CP = U_QKV2 + 6
U_WO3 = U_CP + 4
U_FF2 = U_WO3 + 4
UNITS = U_FF2 + 8 * QUARTERS
N_ADA, ADA_EARLY = 24, 8
N_LATE = N_ADA - ADA_EARLY


def ada_before(u):
    return min(max(u - U_XBC, 0) // 2, N_LATE // 2)


N_XBC = (1, 0)
N_V = (4, 0)
N_WO2 = (5, 1)
N_FF1 = (6, 2)
N_QKV2 = (N_FF1[0] + 2 * QUARTERS, N_FF1[1] + 2 * QUARTERS)
N_WO3 = (N_QKV2[0] + 2, N_QKV2[1] + 1)
N_FF2 = (N_WO3[0] + 1, N_WO3[1] + 1)
P_WO2 = 2
P_FF1 = P_WO2 + 2
P_WO3 = P_FF1 + 2 * QUARTERS + 3
P_FF2 = P_WO3 + 2
T_H, T_SSM, T_ATT, T_X1 = 0, 8, 16, 24
T_HID1 = 32
T_N2 = T_HID1 + 32
T_MIX = T_N2 + 8
T_N3 = T_MIX + 8
T_HID2 = T_N3 + 8
M_H, M_X1, M_HID1, M_N2, M_MIX, M_HID2 = 0, 8, 16, 48, 56, 60
R_H, R_SSM, R_ATT, R_X1, R_N2, R_ATT2, R_N3 = 0, 8, 16, 24, 32, 40, 44
ATT_BANKS = (6, 7, 2, 3, 6, 7, 4, 5)
XS_BANKS = (4, 5)
PT_BANKS = ((7, 2, 3), (1, 2, 3))
CP_BANKS = (0, 7)
N3_BANKS = (4, 5, 6, 7, 0, 1, 2, 3)
Z_TILES = ((2,), (3,), (4, 5), ())
WO1_TILES = ((),) * 12 + ((0,), (1,), (2,), (3,), (4, 5), ())


class Link:

    def __init__(self, eng, sem):
        self.eng, self.sem, self.n, self.extra = eng, sem, 0, 0

    def __call__(self, ins):
        self.n += 1
        ins.then_inc(self.sem, 1)
        self.eng.wait_ge(self.sem, self.extra + self.n)

    def enter(self, i, per, first=0):
        self.start, self.per, self.extra = self.n, per, i * per - first * per

    def leave(self, times):
        assert self.n - self.start == self.per, (self.n - self.start, self.per)
        self.n, self.extra = self.start + times * self.per, 0


def build(nc, x, c, w_ada, b_ada, w_in, conv_w, conv_b, dt_bias, a_log, d_skip, ssm_norm_w, f_bias,
          attn_norm_w, w_out, ln1_g, ln1_b, w_ff_in, w_ff_out, ln2_g, ln2_b, norm1_g_2, w_in_2,
          q_norm_g_2, k_norm_g_2, rel_bias_2, conv_w_2, pool_w_2, pool_scale_2, w_out_2, norm2_g_2,
          w_mlp1_2, w_mlp2_2, out):
    with ExitStack() as ctx:
        def sb(name, shape, dt=F32):
            return ctx.enter_context(nc.sbuf_tensor(name, shape, dt))

        def sem(name):
            return ctx.enter_context(nc.semaphore(name))

        bank = [ctx.enter_context(nc.psum_tensor(f"bank{b}", [P, 512], F32)) for b in range(8)]

        raw = sb("raw", [P, 2, 2048])
        w_hi = sb("w_hi", [P, 2, 2048], F32R)
        w_lo = sb("w_lo", [P, 2, 2048], F32R)
        a_hi = [sb(f"a_hi{n}", [P, KT, S], F32R) for n in range(2)]
        a_lo = [sb(f"a_lo{n}", [P, KT, S], F32R) for n in range(2)]
        tmp = sb("tmp", [P, 2, S])
        arena = sb("arena", [P, 22528])

        def view(at, *dims):
            n = int(np.prod(dims))
            v = arena[:, at:at + n]
            if len(dims) == 2:
                v = v.rearrange("p (a b) -> p a b", a=dims[0])
            elif len(dims) == 3:
                v = v.rearrange("p (a b c) -> p a b c", a=dims[0], b=dims[1])
            return v

        xtok = view(18432, TB, D)
        ada = view(0, 4, KT, 512)
        z_y = view(0, TB, D)
        xbc = view(4096, CT, S)
        dtf = view(19456, 6, S)
        xs = view(10240, TB, D)
        btok = view(14336, TB, 2, ST)
        bc = view(15360, 2, 16, P)
        xc = view(19456, 1024)
        xd = view(20480, 1024)
        prev = view(21504, 1024)
        cbm = view(4096, 4, 2 * P)
        off = view(5120, 1024)
        yacc = view(10240, TB, D)
        vtok = view(0, TB, D)
        att = view(4096, TB, D)
        ncb = view(8192, 2, S)
        ncm = view(9216, 2, S)
        qk = view(14336, 2, 4, S)
        prob = view(18432, 2, 1280)
        probT = view(20992, 1280)
        xre = view(0, TB, D)
        x1 = view(14336, TB, D)
        row = view(18432, 4, D)
        rl = view(0, 2, S)
        qkv2 = view(4096, 3, TB, 512)
        sq2 = view(0, TB, 512)
        qkT2 = view(10240, 2, 4, S)
        cp = view(18432, 8, S)
        relt = view(2048, 2, H2, P)
        prob2 = view(4096, 2, 1280)
        prob2T = view(6656, 1280)
        att2 = view(0, TB, 512)

        ident = sb("ident", [P, P])
        flip = sb("flip", [P, P])
        masks = sb("masks", [P, 2, P])
        keep = masks[:, 0]
        hide = masks[:, 1]
        poolw = masks
        ones = sb("ones", [P, P])
        vec_in = view(16384, 2, P)
        vec = sb("vec", [P, 2, P])
        cact = sb("cact", [P, KT])
        mod = sb("mod", [P, 80])
        col64 = sb("col64", [64, 4])
        dsk = sb("dsk", [P, SSM_H])
        dta = tmp[:, 0].rearrange("p (a b) -> p a b", a=8)
        ex2 = sb("ex", [P, 2, 3, SSM_H])
        st = sb("st", [P, 16])
        head_rs = sb("head_rs", [P, 64])
        st2 = sb("st2", [P, 64])
        stat = sb("stat", [P, 8, 6])
        mv = sb("mv", [P, TB, 2])
        nhalf = sb("nhalf", [P, 64])
        relc = sb("relc", [P, H2])
        pinv = sb("pinv", [P, 2, 16])
        acs_d = nc.dram_tensor("acs_d", (16, S), F32).ap()
        ncum_d = nc.dram_tensor("ncum_d", (16, S), F32).ap()
        ext_d = nc.dram_tensor("ext_d", (H2, 512), F32).ap()

        v0, v1 = vec[:, 0, :], vec[:, 1, :]
        V_BADA, V_CONVW, V_CONVB, V_SSM = 0, 48, 96, 108
        V_ATT, V_N1, V_N2, V_CW2, V_PS, V_QG, V_KG, V_C = 0, 8, 16, 24, 30, 32, 33, 34
        V_LN = (42, 58)

        mxs, rsum, rinv = sb("mxs", [P, 2, 4]), sb("rsum", [P, 2, 4]), sb("rinv", [P, 2, 4])

        landed = [sem("landed0"), sem("landed1")]
        w_hi_made, w_lo_made, ticks = sem("w_hi_made"), sem("w_lo_made"), sem("ticks")
        evac = [sem("evac0"), sem("evac1")]
        even_done = sem("even_done")
        turned = sem("turned")
        tile_made, a_hi_made, a_lo_made = sem("tile_made"), sem("a_hi_made"), sem("a_lo_made")
        dve_link, act_link, pool_link = sem("dve_link"), sem("act_link"), sem("pool_link")
        cleared, consts = sem("cleared"), sem("consts")
        vecs_in, vecs_t, vecs_made, c_made = sem("vecs_in"), sem("vecs_t"), sem("vecs_made"), sem("c_made")
        x_in, small_in, mod_made = sem("x_in"), sem("small_in"), sem("mod_made") 
        ada_in = [sem(f"ada_in{n}") for n in range(4)]
        late_sum, col_mm, late_made = sem("late_sum"), sem("col_mm"), sem("late_made")
        ada_sum = sem("ada_sum")
        z_read, qk_read, yacc_read, yz_made = sem("z_read"), sem("qk_read"), sem("yacc_read"), sem("yz_made")
        dtf_abs, dtf_exp, a_col, scanned = sem("dtf_abs"), sem("dtf_exp"), sem("a_col"), sem("scanned")
        acs_out, cum_out, dta_t, dta_made = sem("acs_out"), sem("cum_out"), sem("dta_t"), sem("dta_made")
        tap_made, conv_act, xs_t, xs_made, cb_done, cb_evac = sem("tap_made"), sem("conv_act"), sem("xs_t"), sem("xs_made"), sem("cb_done"), sem("cb_evac")
        bc_in = [sem("bc_in0"), sem("bc_in1")]
        bc_sub, bc_exp, score_made = sem("bc_sub"), sem("bc_exp"), sem("score_made")
        ex_in, ex_made, xc_made, xd_made = sem("ex_in"), sem("ex_made"), sem("xc_made"), sem("xd_made")
        y_mm, st_mm, prev_made, y_made = sem("y_mm"), sem("st_mm"), sem("prev_made"), sem("y_made")
        y_sq, rs_made = sem("y_sq"), sem("rs_made")
        ncb_in = [sem("ncb_in0"), sem("ncb_in1")]
        ncm_made, s_mm, s_made, mx_made, p_made = sem("ncm_made"), sem("s_mm"), sem("s_made"), sem("mx_made"), sem("p_made")
        pt_t, pt_made, o_mm, o_made = sem("pt_t"), sem("pt_made"), sem("o_mm"), sem("o_made")
        rows_in, g_mm, g_made, xre_in, acc0 = sem("rows_in"), sem("g_mm"), sem("g_made"), sem("xre_in"), sem("acc0")
        cp_read, rrow_mm, rrow_made, r2_made, xhat_made = sem("cp_read"), sem("rrow_mm"), sem("rrow_made"), sem("r2_made"), sem("xhat_made")
        ln_var, ln_rs, ln_made, sum_made = sem("ln_var"), sem("ln_rs"), sem("ln_made"), sem("sum_made")
        qk_sq, qk_rs, qk_made, q2_t, q2_made = sem("qk_sq"), sem("qk_rs"), sem("qk_made"), sem("q2_t"), sem("q2_made")
        ext_out, rel_in, rel_made, pool_in = sem("ext_out"), sem("rel_in"), sem("rel_made"), sem("pool_in")
        m_made, m_mm, out_sent = sem("m_made"), sem("m_mm"), sem("out_sent")

        w_in_v = w_in[0].rearrange("(k p) n -> p k n", p=P)
        w_ada_v = w_ada[0].rearrange("(k p) n -> p k n", p=P)
        w_out_v = w_out[0].rearrange("(k p) n -> p k n", p=P)
        w_in2_v = w_in_2[0].rearrange("(k p) n -> p k n", p=P)
        w_out2_v = w_out_2[0].rearrange("(k p) n -> p k n", p=P)
        ff_v = [(w_ff_in[0].rearrange("(k p) n -> p k n", p=P), w_ff_out[0].rearrange("(k p) n -> p k n", p=P)),
                (w_mlp1_2[0].rearrange("(k p) n -> p k n", p=P), w_mlp2_2[0].rearrange("(k p) n -> p k n", p=P))]
        x_v = x[0].rearrange("(t p) d -> p t d", p=P)
        out_v = out[0].rearrange("(t p) d -> p t d", p=P)
        block = ctx.enter_context(nc.Block())

        def rows_of(vector, n):
            return vector.rearrange("a (k p) -> (a k) p", k=n)


        def at(i, per, const):
            return i * per + const

        def late_place(n):
            at_ = 256 * (n % 2)
            return xd[:, at_:at_ + 256] if n >= N_LATE - 2 else tmp[:, 1, at_:at_ + 256]

        def left(ap):
            return ap.rearrange("p (k n) -> p k n", k=KT)[:, :, 0:P]

        @block.sync
        def _(sp):
            def load(i, per, u0, src, k, split=True):
                if split and not (isinstance(i, int) and i * per + u0 < 2):
                    sp.wait_ge(w_lo_made, at(i, per, u0 - 1))
                sp.dma_start(raw[:, u0 % 2].rearrange("p (k n) -> p k n", k=k), src).then_inc(landed[u0 % 2], 16)

            def columns(i, per, u0, w, col, split=True):
                load(i, per, u0, w[:, :, bass.ds(col, 256)], 8, split)

            def rows(i, per, u0, w, k, col, split=True):
                load(i, per, u0, w[:, bass.ds(k, 4), bass.ds(col, 512)], 4, split)

            def four_rows(u0, w, k0, col0):
                for b in range(4):
                    rows(0, 0, u0 + b, w, k0 + 4 * (b % 2), col0 + 512 * (b // 2))

            def ada_two(i, per, n):
                for m in range(n, n + 2):
                    sp.wait_ge(w_lo_made, at(i, per, U_XBC + m + 1))
                    sp.dma_start(raw[:, (m + 1) % 2].rearrange("p (k n) -> p k n", k=8),
                                 w_ada_v[:, :, bass.ds(at(i, 256 * per, 256 * (ADA_EARLY + m)), 256)]).then_inc(landed[(m + 1) % 2], 16)

            def prelude():
                sp.wait_ge(cleared, 1)
                for at_, src, n, side in ((V_C, c, KT, 1), (V_BADA, b_ada, 48, 0), (V_CONVB, conv_b, CT, 0),
                                          (V_SSM, ssm_norm_w, KT, 0), (V_ATT, attn_norm_w, KT, 1), (V_N1, norm1_g_2, KT, 1),
                                          (V_N2, norm2_g_2, KT, 1), (V_PS, pool_scale_2, 2, 1),
                                          (V_LN[0], ln1_g, KT, 1), (V_LN[0] + KT, ln1_b, KT, 1),
                                          (V_LN[1], ln2_g, KT, 1), (V_LN[1] + KT, ln2_b, KT, 1)):
                    sp.dma_start(vec_in[at_:at_ + n, side, :], src.rearrange("a (k p) -> (a k) p", k=n)).then_inc(vecs_in, 16)
                sp.dma_start(vec_in[V_CONVW:V_CONVW + 48, 0, :], conv_w[0].rearrange("i (k p) -> (i k) p", p=P)).then_inc(vecs_in, 16)
                sp.dma_start(vec_in[V_CW2:V_CW2 + 6, 1, :], conv_w_2[0].rearrange("i (k p) -> (i k) p", p=P)).then_inc(vecs_in, 16)
                for at_, src in ((V_QG, q_norm_g_2), (V_KG, k_norm_g_2)):
                    for half in range(2):
                        sp.dma_start(vec_in[at_:at_ + 1, 1, half * HD:half * HD + HD], src).then_inc(vecs_in, 16)
                sp.dma_start(xtok, x_v).then_inc(x_in, 16)
                for n in range(4):
                    sp.dma_start(ada[:, n], w_ada_v[:, :, n * 512:n * 512 + 512]).then_inc(ada_in[n], 16)
                sp.wait_ge(cleared, 3)
                unit = raw[:, 0].rearrange("p (k n) -> p k n", k=8)
                sp.dma_start(unit[:, :, 0:16], w_in_v[:, :, C_DT:C_DT + 16]).then_inc(landed[0], 16)
                sp.dma_start(unit[:, :, 32:48], w_in_v[:, :, C_F:C_F + 16]).then_inc(landed[0], 16)
                for dst, src in ((col64[0:16, 0:1], dt_bias), (col64[32:48, 0:1], f_bias), (col64[0:16, 2:3], a_log)):
                    sp.dma_start(dst, src.rearrange("a h -> h a")).then_inc(small_in, 16)
                sp.dma_start(dsk[:, :], bass.AP(d_skip.tensor, 0, [[0, P], [1, SSM_H]])).then_inc(small_in, 16)

            def feed_forward(u0, w1, w2):
                with sp.Fori(0, QUARTERS) as i:
                    for b in range(4):
                        columns(i, 8, u0 + b, w1, at(i, D, 256 * b))
                    for b in range(4):
                        rows(i, 8, u0 + 4 + b, w2, at(i, 8, 4 * (b % 2)), 512 * (b // 2))

            prelude()
            for b in range(2):
                columns(0, 0, U_XBC + b, w_in_v, C_XBC + 256 * b)
            with sp.Fori(0, 2) as i:
                ada_two(i, 2, 0)
                for b in range(2):
                    sp.wait_ge(late_sum, at(i, 2, 1 + b))
                    columns(i, 2, U_XBC + 2 + b, w_in_v, at(i, 512, C_XBC + 256 * (2 + b)), False)
            ada_two(0, 0, 4)
            for half in range(2):
                for b in range(2):
                    sp.wait_ge(late_sum, 5 + b + 2 * half)
                    rows(0, 0, U_Z + 2 * half + b, w_in_v, 4 * b, C_Z + 512 * half, False)
                ada_two(0, 0, 6 + 2 * half)
            for b, col in enumerate((C_Q, C_K)):
                sp.wait_ge(late_sum, 9 + b)
                columns(0, 0, U_QK + b, w_in_v, col, False)
            ada_two(0, 0, 10)
            for half in range(2):
                for b in range(2):
                    sp.wait_ge(late_sum, 11 + b + 2 * half)
                    rows(0, 0, U_V + 2 * half + b, w_in_v, 4 * b, C_V + 512 * half, False)
                ada_two(0, 0, 12 + 2 * half)
            sp.wait_ge(late_sum, N_LATE)
            with sp.Fori(0, 3) as i:
                columns(i, 2, U_QK1, w_in_v, at(i, 256, C_Q + 256))
                columns(i, 2, U_QK1 + 1, w_in_v, at(i, 256, C_K + 256))
            four_rows(U_WO1, w_out_v, 0, 0)
            four_rows(U_WO2, w_out_v, KT, 0)
            feed_forward(U_FF1, *ff_v[0])
            four_rows(U_QKV2, w_in2_v, 0, 0)
            for b in range(2):
                rows(0, 0, U_QKV2 + 4 + b, w_in2_v, 4 * b, 1024)
            for b in range(4):
                columns(0, 0, U_CP + b, w_in2_v, 1536 + 256 * b)
            for b in range(4):
                rows(0, 0, U_WO3 + b, w_out2_v, 4 * (1 - b % 2), 512 * (b // 2))
            feed_forward(U_FF2, *ff_v[1])
            sp.wait_ge(evac[0], 4 * (N_FF2[0] + 2 * QUARTERS))
            sp.dma_start(out_v[:, :, 0:512], x1[:, :, 0:512]).then_inc(out_sent, 16)
            for t in range(TB):
                sp.wait_ge(evac[1], 4 * (N_FF2[1] + 2 * QUARTERS - 1) + t + 1)
                sp.dma_start(out_v[:, t, 512:1024], x1[:, t, 512:1024]).then_inc(out_sent, 16)
            sp.wait_ge(out_sent, 16 * (TB + 1))

        @block.gpsimd
        def _(pool):
            link = Link(pool, pool_link)

            def constants():
                pool.memset(vec_in[:], 0.0).then_inc(cleared, 1)
                pool.memset(raw[:, 0], 0.0).then_inc(cleared, 1)
                pool.memset(col64[:], 0.0).then_inc(cleared, 1)
                for m in (ident[:], flip[:], hide):
                    link(pool.memset(m, 0.0))
                link(pool.memset(keep, 1.0))
                pool.memset(ones[:], 1.0).then_inc(consts, 1)
                pool.affine_select(out=ident[:], in_=ident[:], compare_op=ALU.not_equal, fill=1.0, base=0,
                                   pattern=[[-1, P]], channel_multiplier=1).then_inc(consts, 1)
                pool.affine_select(out=flip[:], in_=flip[:], compare_op=ALU.not_equal, fill=1.0, base=1 - P,
                                   pattern=[[1, P]], channel_multiplier=1).then_inc(consts, 1)
                pool.affine_select(out=keep, in_=keep, compare_op=ALU.is_ge, fill=0.0, base=0,
                                   pattern=[[1, P]], channel_multiplier=-1).then_inc(consts, 1)
                pool.affine_select(out=hide, in_=hide, compare_op=ALU.is_ge, fill=NEG, base=0,
                                   pattern=[[-1, P]], channel_multiplier=1).then_inc(consts, 1)
                pool.memset(nhalf[:], -0.5).then_inc(consts, 1)
                pool.wait_ge(cleared, 3)
                link(pool.memset(col64[0:32, 1:2], 1.0))
                link(pool.memset(col64[32:64, 1:2], -1.0))
                pool.memset(col64[:, 3:4], 1.0).then_inc(consts, 1)

            def inv_root(n, src, dst, scale, eps, signal, o=0):
                link(pool.tensor_scalar(st2[:, o:o + n], src, scale, eps, ALU.mult, ALU.add))
                pool.tensor_tensor(dst, st2[:, o:o + n], nhalf[:, 0:n], ALU.pow).then_inc(signal, 1)

            def rms_root(turn, eps):
                pool.wait_ge(y_sq, 4 * turn + 4)
                inv_root(4, st[:, 0:4], st[:, 4:8], 1.0 / D, eps, rs_made)

            def ln_root(turn):
                for t in range(TB):
                    pool.wait_ge(ln_var, 4 * turn + t + 1)
                    inv_root(1, mv[:, t, 1:2], st[:, 8 + t:9 + t], 1.0, LN_EPS, ln_rs, 4 + t)

            def lo(u0, i=0, per=0):
                pool.wait_ge(w_hi_made, at(i, per, u0 + 1))
                pool.tensor_tensor(w_lo[:, u0 % 2], raw[:, u0 % 2], w_hi[:, u0 % 2].bitcast(F32), ALU.subtract)\
                    .then_inc(w_lo_made, 1)

            def save_rows():
                pool.wait_ge(scanned, 5)
                pool.dma_start(acs_d, dtf[0:16, 1, :]).then_inc(acs_out, 16)
                pool.dma_start(ncum_d, dtf[32:48, 1, :]).then_inc(cum_out, 16)

            def ssd_row(ch):
                if ch >= 2:
                    pool.wait_ge(y_mm, ch - 1)
                pool.dma_start(bc[:, ch % 2], bass.AP(acs_d.tensor, ch * P, [[0, P], [S, 16], [1, P]]))\
                    .then_inc(bc_in[ch % 2], 16)

            def fox_row(h):
                if h >= 2:
                    pool.wait_ge(s_made, h - 1)
                pool.dma_start(ncb[:, h % 2], bass.AP(ncum_d.tensor, h * S, [[0, P], [1, S]]))\
                    .then_inc(ncb_in[h % 2], 16)
                pool.wait_ge(ncb_in[h % 2], 16 * (h // 2 + 1))
                pool.tensor_tensor(ncm[:, h % 2].rearrange("p (i k) -> p i k", i=TB),
                                   ncb[:, h % 2].rearrange("p (i k) -> p i k", i=TB),
                                   hide.unsqueeze(1).broadcast_to([P, TB, P]), ALU.add).then_inc(ncm_made, 1)

            def load_row(n, src):
                pool.dma_start(row[:, n], bass.AP(src.tensor, 0, [[0, P], [1, D]])).then_inc(rows_in, 16)

            def relative():
                rb = rel_bias_2.tensor
                pool.dma_start(ext_d[:, 0:NREL], rel_bias_2[0]).then_inc(ext_out, 16)
                pool.dma_start(ext_d[:, NREL:NREL + P].unsqueeze(2), bass.AP(rb, NREL - 1, [[NREL, H2], [0, P], [1, 1]]), allow_slow_non_contiguous=True).then_inc(ext_out, 16)
                pool.dma_start(relc[0:1, :].unsqueeze(2), bass.AP(rb, NREL - 1, [[0, 1], [NREL, H2], [1, 1]]), allow_slow_non_contiguous=True).then_inc(rel_in, 16)
                link(pool.memset(poolw[:], 0.0))
                for g in range(4):
                    po = HD * (g % 2)
                    pool.dma_start(poolw[po:po + HD, g // 2, po:po + HD], pool_w_2[0, g]).then_inc(pool_in, 16)

            def relative_tiles():
                pool.wait_ge(ext_out, 32)
                pool.wait_ge(sum_made, 8)
                for n in range(2):
                    pool.dma_start(relt[:, n], bass.AP(ext_d.tensor, 1 + CLIP * n, [[1, P], [512, H2], [1, P]]))\
                        .then_inc(rel_in, 16)
                pool.wait_ge(rel_in, 48)
                pool.memset(relt[0:64, 0, :, 0:64], NEG).then_inc(rel_made, 1)

            constants()
            pool.wait_ge(w_hi_made, 1)
            pool.tensor_tensor(left(w_lo[:, 0]), left(raw[:, 0]), left(w_hi[:, 0].bitcast(F32)), ALU.subtract)\
                .then_inc(w_lo_made, 1)
            for u in range(U_XBC, U_XBC + 5):
                lo(u)
            save_rows()
            lo(U_XBC + 5)
            pool.wait_ge(acs_out, 16)
            pool.wait_ge(turned, R_H + 8)
            ssd_row(0)
            ssd_row(1)
            lo(U_Z)
            lo(U_Z + 1)
            ssd_row(2)
            ssd_row(3)
            for u in range(U_Z + 2, U_V + 2):
                lo(u)
            rms_root(0, RMS_EPS)
            for u in range(U_V + 2, U_QK1 + 1):
                lo(u)
            pool.wait_ge(cum_out, 16)
            pool.wait_ge(turned, R_SSM + 8)
            fox_row(0)
            fox_row(1)
            for s in range(16):
                if s % 2 == 0 and s < 12:
                    lo(U_QK1 + s // 2 + 1)
                elif s == 12:
                    lo(U_WO1 + 1)
                if s < 14:
                    fox_row(s + 2)
            lo(U_WO1 + 2)
            lo(U_WO1 + 3)
            pool.wait_ge(o_made, 16)
            pool.dma_start(xre, x_v).then_inc(xre_in, 16)
            lo(U_WO2)
            lo(U_WO2 + 1)
            rms_root(1, RMS_EPS)
            lo(U_WO2 + 2)
            load_row(1, ln1_g)
            load_row(2, ln1_b)
            relative()
            lo(U_WO2 + 3)
            lo(U_WO2 + 4)
            ln_root(0)
            pool.memset(yacc, 0.0).then_inc(acc0, 1)

            def feed_forward(u0, times):
                with pool.Fori(0, times) as i:
                    for b in range(8):
                        lo(u0 + b + 1, i, 8)

            relative_tiles()
            feed_forward(U_FF1, QUARTERS)
            load_row(1, ln2_g)
            load_row(2, ln2_b)
            ln_root(1)
            lo(U_QKV2 + 1)
            lo(U_QKV2 + 2)
            rms_root(2, EPS2)
            for u in range(U_QKV2 + 3, U_CP):
                lo(u)
            pool.wait_ge(qk_sq, 2)
            inv_root(64, head_rs[:], head_rs[:], 1.0 / HD, EPS2, qk_rs)
            for u in range(U_CP, U_FF2 + 1):
                lo(u)
            rms_root(3, EPS2)
            pool.wait_ge(rs_made, 4)
            pool.tensor_tensor(st[:, 12:16], st[:, 4:8], st[:, 4:8], ALU.mult).then_inc(r2_made, 1)
            feed_forward(U_FF2, QUARTERS - 1)
            for b in range(7):
                lo(U_FF2 + 8 * (QUARTERS - 1) + b + 1)

        @block.scalar
        def _(act):
            link = Link(act, act_link)

            def hi(u0, i=0, per=0, late=False):
                act.wait_ge(landed[u0 % 2], at(i, 8 * per, 16 * (u0 // 2 + 1 + (u0 % 2 == 0) + ada_before(u0))))
                if not (isinstance(i, int) and i * per + u0 < 2):
                    act.wait_ge(ticks, at(i, 2 * per, 2 * u0 - 2 + 2 * late))
                part = left if u0 == U_DTF else lambda ap: ap
                act.activation(part(w_hi[:, u0 % 2]), part(raw[:, u0 % 2]), ACT.Copy).then_inc(w_hi_made, 1)

            def tile_hi(m0, buf, k):
                act.wait_ge(tile_made, m0 + 1)
                act.activation(a_hi[buf][:, k], tmp[:, m0 % 2], ACT.Copy).then_inc(a_hi_made, 1)

            def turned_hi(r0, buf, k, b, scale, bias=None):
                act.wait_ge(turned, r0 + k + 1)
                if bias is None:
                    act.activation(a_hi[buf][:, k], bank[b][:], ACT.Copy, scale=scale).then_inc(a_hi_made, 1)
                else:
                    act.activation(a_hi[buf][:, k], bank[b][:], ACT.Identity, scale=scale, bias=bias).then_inc(a_hi_made, 1)

            def read_rows(u0, s, dst, scale=None):
                for t in range(TB):
                    act.wait_ge(ticks, 2 * u0 + 3 + t // 2)
                    act.activation(dst(t), bank[4 * s + t][:], ACT.Copy, scale=scale(t) if scale else 1.0).then_inc(evac[s], 1)

            def squares(turn, src, junk, after, n):
                for t in range(TB):
                    act.wait_ge(after, n(t))
                    act.activation(junk, src[:, t], ACT.Square, accum_out=st[:, t:t + 1]).then_inc(y_sq, 1)
                    act.wait_ge(y_sq, 4 * turn + t + 1)

            def probabilities(h, src, dst):
                act.wait_ge(mx_made, h + 1)
                if h >= 2:
                    act.wait_ge(o_made, h - 1)
                for q in range(TB):
                    n = (q + 1) * P
                    act.activation(dst[:, QO[q]:QO[q] + n], src(q), ACT.Exp, bias=mxs[:, h % 2, q:q + 1],
                                   accum_out=rsum[:, h % 2, q:q + 1]).then_inc(p_made, 1)

            def copy_probT(h, dst):
                if h:
                    act.wait_ge(o_mm, h)
                for m, (b, n) in enumerate(zip(PT_BANKS[h // 16], (4, 4, 2))):
                    act.wait_ge(pt_t, 3 * h + m + 1)
                    act.activation(dst[:, 512 * m:512 * m + n * P], bank[b][:, 0:n * P], ACT.Copy).then_inc(pt_made, 1)

            def feed_forward(u0, m0, n0, i, last):
                for b in range(2):
                    for j in range(4):
                        if j % 2 == 0:
                            hi(u0 + 2 * b + j // 2 + 1, i, 8)
                        k = 4 * b + j
                        act.wait_ge(ticks, at(i, 16, 2 * (u0 + 2 * b) + j + 1))
                        act.wait_ge(tile_made, at(i, 8, m0 + k - 1))
                        act.activation(rl[:, k % 2], bank[4 * b + j][:], ACT.Relu).then_inc(evac[b], 1)
                        act.wait_ge(evac[b], at(i, 8, 4 * n0[b] + j + 1))
                        act.activation(a_hi[1][:, k], rl[:, k % 2], ACT.Square).then_inc(a_hi_made, 1)
                for b in range(4, 8):
                    if not (last and b >= 7):
                        hi(u0 + b + 1, i, 8)

            def g_row(turn, b, place):
                for half in range(2):
                    act.wait_ge(g_mm, 2 * turn + half + 1)
                    act.activation(row[:, place, 512 * half:512 * half + 512], bank[b + half][:], ACT.Copy).then_inc(g_made, 1)

            act.wait_ge(vecs_made, 1)
            act.activation(cact[:], v1[:, V_C:V_C + KT], ACT.Silu).then_inc(c_made, 1)
            hi(U_DTF)
            act.wait_ge(mod_made, 1)
            for k in range(KT):
                turned_hi(R_H, 0, k, k, mod[:, 8 + k:9 + k], mod[:, k:k + 1])
            hi(U_XBC)
            act.wait_ge(small_in, 64)
            act.wait_ge(consts, 7)
            act.activation(col64[0:16, 3:4], col64[0:16, 2:3], ACT.Exp).then_inc(a_col, 1)
            act.wait_ge(dtf_abs, 1)
            act.activation(dtf[0:64, 2], dtf[0:64, 1], ACT.Exp, scale=-1.0).then_inc(dtf_exp, 1)
            hi(U_XBC + 1)

            def copy_xs(b):
                act.wait_ge(xs_t, b + 1)
                dst = xs[:, b // 2, 512 * (b % 2):512 * (b % 2) + 512] if b < 8 else \
                    btok[:, 2 * (b - 8):2 * (b - 8) + 2].rearrange("p a b c -> p (a b c)")
                act.activation(dst, bank[XS_BANKS[b % 2]][:], ACT.Copy).then_inc(xs_made, 1)

            def conv_silu(q):
                act.wait_ge(evac[0], 4 * N_XBC[0] + q + 1)
                act.activation(xbc[:, q], xbc[:, q], ACT.Silu).then_inc(conv_act, 1)

            def read_z(n, b=6):
                act.wait_ge(ticks, 2 * U_Z + n + 1)
                act.activation(z_y[:, n % 4, 512 * (n // 4):512 * (n // 4) + 512], bank[b][:], ACT.Silu).then_inc(z_read, 1)

            def decays(ch):
                e, b = ex2[:, ch % 2], bc[:, ch % 2]
                act.wait_ge(dta_made, 1)
                if ch >= 2:
                    act.wait_ge(prev_made, 2 * ch - 2)
                act.activation(e[:, 0], dta[:, 4 + ch, 0:16], ACT.Exp).then_inc(ex_made, 1)
                act.wait_ge(bc_in[ch % 2], 16 * (ch // 2 + 1))
                act.activation(e[:, 1], b[:, :, P - 1], ACT.Exp).then_inc(ex_made, 1)
                act.wait_ge(ex_in, ch + 1)
                act.activation(e[:, 2], e[:, 2], ACT.Exp).then_inc(ex_made, 1)
                act.wait_ge(bc_sub, ch + 1)
                act.activation(b, b, ACT.Exp).then_inc(bc_exp, 1)

            for q in range(CT):
                act.wait_ge(ticks, 2 * U_XBC + q + 1)
                act.activation(xbc[:, q], bank[q % 4][:], ACT.Identity, scale=v0[:, V_CONVW + 3 * CT + q:V_CONVW + 3 * CT + q + 1],
                               bias=v0[:, V_CONVB + q:V_CONVB + q + 1]).then_inc(tap_made, 1)
                if q % 2:
                    hi(U_XBC + q // 2 + 2)
                if q:
                    conv_silu(q - 1)
                if q >= 9:
                    copy_xs(2 * q - 18)
                    copy_xs(2 * q - 17)
            copy_xs(6)
            copy_xs(7)
            conv_silu(CT - 1)
            read_z(0)
            copy_xs(8)
            copy_xs(9)
            decays(0)
            read_z(1)
            for ch in range(TB):
                if ch < TB - 1:
                    decays(ch + 1)
                for n in Z_TILES[ch]:
                    read_z(n)
                if ch == 1:
                    hi(U_Z + 2, late=True)
                    hi(U_Z + 3)


            def qk_tile(g, j, u, b):
                act.wait_ge(ticks, 2 * u + j + 1)
                act.activation(qk[:, g % 2, j], bank[b][:], ACT.Copy, scale=HD ** -0.5 if j < 2 else 1.0).then_inc(qk_read, 1)

            act.wait_ge(ticks, 2 * U_Z + 7)
            hi(U_QK)
            act.wait_ge(ticks, 2 * U_Z + 8)
            read_z(6)
            read_z(7, 5)
            hi(U_QK + 1)
            for j in range(2):
                qk_tile(0, j, U_QK, (6, 5)[j % 2])
            hi(U_V)
            for k in range(4):
                turned_hi(R_SSM, 1, k, k, v0[:, V_SSM + k:V_SSM + k + 1])
            qk_tile(0, 2, U_QK, 6)
            for k in range(4, 8):
                turned_hi(R_SSM, 1, k, k - 4, v0[:, V_SSM + k:V_SSM + k + 1])
            qk_tile(0, 3, U_QK, 5)
            hi(U_V + 1)
            squares(0, z_y, xc, yz_made, lambda t: t + 1)
            hi(U_V + 2)
            read_rows(U_V, 0, lambda t: vtok[:, t, 0:512])
            hi(U_V + 3)
            hi(U_V + 4)
            read_rows(U_V + 2, 1, lambda t: vtok[:, t, 512:1024])

            def wo1_tile(n):
                act.wait_ge(ticks, 2 * U_WO1 + n + 1)
                if n == 0:
                    act.wait_ge(rs_made, 1)
                t, half = n % 4, n // 4
                act.activation(yacc[:, t, 512 * half:512 * half + 512], bank[n % 2][:], ACT.Copy,
                               scale=st[:, 4 + t:5 + t]).then_inc(yacc_read, 1)

            for s in range(18):
                if s == 12:
                    hi(U_WO1 + 1)
                elif s == 16:
                    hi(U_WO1 + 2, late=True)
                    hi(U_WO1 + 3)
                if s >= 2:
                    copy_probT(s - 2, probT)
                if s < 12:
                    if s % 2 == 0:
                        hi(U_QK1 + s // 2 + 1)
                    qk_tile(s // 4 + 1, s % 4, U_QK1 + 2 * (s // 4), s % 2)
                if 1 <= s < 17:
                    h = s - 1
                    probabilities(h, lambda q: prob[:, h % 2, QO[q]:QO[q] + (q + 1) * P], prob[:, h % 2])
                for n in WO1_TILES[s]:
                    wo1_tile(n)
            g_row(0, 4, 0)
            for k in range(4):
                turned_hi(R_ATT, 1, k, ATT_BANKS[k], v1[:, V_ATT + k:V_ATT + k + 1])
            g_row(1, 4, 3)
            act.wait_ge(ticks, 2 * U_WO1 + 7)
            hi(U_WO2)
            act.wait_ge(ticks, 2 * U_WO1 + 8)
            for n in (6, 7):
                wo1_tile(n)
            for k in range(4, KT):
                turned_hi(R_ATT, 1, k, ATT_BANKS[k], v1[:, V_ATT + k:V_ATT + k + 1])
            hi(U_WO2 + 1)
            squares(1, att, tmp[:].rearrange("p a b -> p (a b)"), o_made, lambda t: 16)
            hi(U_WO2 + 2)
            hi(U_WO2 + 3)
            hi(U_WO2 + 4)
            for k in range(KT):
                turned_hi(R_X1, 0, k, k, mod[:, 48 + k:49 + k], mod[:, 56 + k:57 + k])
            with act.Fori(0, QUARTERS) as i:
                feed_forward(U_FF1, M_HID1, N_FF1, i, False)
            hi(U_QKV2 + 1)
            for k in range(KT):
                turned_hi(R_N2, 0, k, k, mod[:, 64 + k:65 + k], mod[:, 72 + k:73 + k])
            junk = view(10240, D)
            hi(U_QKV2 + 2)
            squares(2, x1, junk, ln_made, lambda t: 4 + t + 1)
            act.wait_ge(rs_made, 3)
            for n in range(3):
                if n:
                    hi(U_QKV2 + 2 * n + 1)
                    hi(U_QKV2 + 2 * n + 2)
                read_rows(U_QKV2 + 2 * n, n % 2, lambda t: qkv2[:, n, t], lambda t: st[:, 4 + t:5 + t])
            act.wait_ge(rrow_mm, 1)
            act.activation(tmp[:, 1], bank[4][:], ACT.Copy).then_inc(rrow_made, 1)
            hi(U_CP + 1)
            hi(U_CP + 2)
            for s in range(10):
                if s in (2, 4):
                    hi(U_CP + s // 2 + 2)
                if 1 <= s < 9:
                    def score(q):
                        b, o = SB[q]
                        return bank[b][:, o:o + (q + 1) * P]
                    probabilities(16 + s - 1, score, prob2[:, (s - 1) % 2])
                if s >= 2:
                    copy_probT(16 + s - 2, prob2T)
                if s == 6:
                    tile_hi(M_MIX, 1, 4)
                    tile_hi(M_MIX + 1, 1, 5)
            tile_hi(M_MIX + 2, 1, 6)
            tile_hi(M_MIX + 3, 1, 7)
            hi(U_WO3 + 1)
            for k in range(4):
                turned_hi(R_ATT2, 1, k, k, 1.0)
            for b in range(1, 4):
                hi(U_WO3 + b + 1)
            for k in range(KT):
                turned_hi(R_N3, 0, k, N3_BANKS[k], v1[:, V_N2 + k:V_N2 + k + 1])
            squares(3, x1, junk, evac[0], lambda t: 4 * (N_WO3[0] + 1))
            with act.Fori(0, QUARTERS - 1) as i:
                feed_forward(U_FF2, M_HID2, N_FF2, i, False)
            feed_forward(U_FF2, M_HID2, N_FF2, QUARTERS - 1, True)

        @block.vector
        def _(dve):
            link = Link(dve, dve_link)

            def tile_lo(t0, m0, buf, k, i=0, per=0):
                dve.wait_ge(a_hi_made, at(i, per, t0 + 1))
                dve.tensor_tensor(a_lo[buf][:, k], tmp[:, m0 % 2], a_hi[buf][:, k].bitcast(F32), ALU.subtract)\
                    .then_inc(a_lo_made, 1)

            def tmp_free(t0, i=0, per=0):
                if not (isinstance(i, int) and i * per + t0 < 2):
                    dve.wait_ge(a_lo_made, at(i, per, t0 - 1))

            def split_affine(t0, m0, buf, scale, bias):
                for k in range(KT):
                    dve.wait_ge(a_hi_made, t0 + k + 1)
                    tmp_free(t0 + k)
                    dve.tensor_scalar(tmp[:, k % 2], bank[k][:], scale(k), bias(k), ALU.mult, ALU.add).then_inc(tile_made, 1)
                    dve.wait_ge(tile_made, m0 + k + 1)
                    tile_lo(t0 + k, m0 + k, buf, k)

            def split_turned(t0, buf, scale, banks, k0=0):
                for k in range(len(banks)):
                    dve.wait_ge(a_hi_made, t0 + k + 1)
                    dve.scalar_tensor_tensor(a_lo[buf][:, k0 + k], bank[banks[k]][:], scale(k), a_hi[buf][:, k0 + k].bitcast(F32),
                                             ALU.mult, ALU.subtract).then_inc(a_lo_made, 1)

            def maxima(h, src):
                if h:
                    dve.wait_ge(mx_made, h)
                for q in range(TB):
                    ins = dve.reduce_max(rinv[:, 0, q:q + 1], src(q), AX)
                link(ins)
                if h >= 2:
                    dve.wait_ge(p_made, 4 * (h - 1))
                dve.tensor_scalar(mxs[:, h % 2], rinv[:, 0], -1.0, None, ALU.mult).then_inc(mx_made, 1)

            def output(h, dst):
                dve.wait_ge(p_made, 4 * h + 4)
                if h:
                    dve.wait_ge(o_made, h)
                link(dve.reciprocal(rinv[:, 1], rsum[:, h % 2]))
                dve.wait_ge(o_mm, h + 1)
                dve.tensor_tensor(dst, bank[3][:, 256:512].rearrange("p (t d) -> p t d", t=TB),
                                  rinv[:, 1].unsqueeze(2).broadcast_to([P, TB, HD]), ALU.mult).then_inc(o_made, 1)

            def half_stats(t, half):
                ins = dve.bn_stats(stat[:, 2 * t + half], x1[:, t, 512 * half:512 * half + 512])
                if half:
                    link(ins)
                    dve.bn_aggr(mv[:, t], stat[:, 2 * t:2 * t + 2].rearrange("p a b -> p (a b)")).then_inc(ln_var, 1)

            def normalize(turn, t):
                dve.wait_ge(ln_rs, 4 * turn + t + 1)
                dve.tensor_scalar(x1[:, t], x1[:, t], mv[:, t, 0:1], st[:, 8 + t:9 + t], ALU.subtract, ALU.mult).then_inc(xhat_made, 1)

            def gain(turn):
                dve.wait_ge(turned, (R_X1, R_N2)[turn] + 8)
                dve.wait_ge(rows_in, 32 * turn + 32)
                for t in range(TB):
                    link(dve.tensor_tensor(x1[:, t], x1[:, t], row[:, 1], ALU.mult))
                    dve.tensor_tensor(x1[:, t], x1[:, t], row[:, 2], ALU.add).then_inc(ln_made, 1)

            def wait_row(u0, p0, t, i=0, u_per=0, p_per=0):
                if t % 2 == 0:
                    dve.wait_ge(even_done, at(i, 2 * p_per, 2 * p0 + t // 2 + 1))
                else:
                    dve.wait_ge(ticks, at(i, 2 * u_per, 2 * u0 + 3 + t // 2))

            def feed_forward(u0, t0, m0, n0, p0, i, add):
                for b in range(2):
                    for j in range(4):
                        k = 4 * b + j
                        dve.wait_ge(evac[b], at(i, 8, 4 * n0[b] + j + 1))
                        tmp_free(t0 + k, i, 8)
                        dve.tensor_tensor(tmp[:, k % 2], rl[:, k % 2], rl[:, k % 2], ALU.mult).then_inc(tile_made, 1)
                        dve.wait_ge(tile_made, at(i, 8, m0 + k + 1))
                        tile_lo(t0 + k, m0 + k, 1, k, i, 8)
                for b in range(2):
                    for t in range(TB):
                        wait_row(u0 + 4 + 2 * b, p0 + b, t, i, 8, 2)
                        dve.wait_ge(evac[b], at(i, 8, 4 * (n0[b] + 1) + t))
                        add(b, t, slice(512 * b, 512 * b + 512))

            def weigh(acc, src, before, signal):
                for wait in before:
                    dve.wait_ge(*wait)
                link(dve.tensor_scalar(acc, src(0), cact[:, 0:1], None, ALU.mult))
                for k in range(1, KT):
                    ins = dve.scalar_tensor_tensor(acc, src(k), cact[:, k:k + 1], acc, ALU.mult, ALU.add)
                    if k < KT - 1:
                        link(ins)
                    else:
                        ins.then_inc(signal, 1)

            def late_ada(n):
                slot = (n + 1) % 2
                before = [(landed[slot], 16 * (n // 2 * 2 + 2 + 2 * (slot == 0))),
                          (col_mm, 4 + min(n, N_LATE - 3) - 1)]
                weigh(late_place(n), lambda k: raw[:, slot, 256 * k:256 * k + 256],
                      before, late_sum)

            def start():
                dve.wait_ge(vecs_t, 1)
                dve.tensor_copy(vec[:].rearrange("p a b -> p (a b)"), bank[7][:, 0:256]).then_inc(vecs_made, 1)
                dve.wait_ge(vecs_made, 1)
                dve.wait_ge(c_made, 1)
                for n in range(4):
                    before = [(ada_in[n], 16)] + ([(col_mm, n - 1)] if n >= 2 else [])
                    weigh(tmp[:, n % 2], lambda k: ada[:, n, k], before, ada_sum)
                dve.wait_ge(col_mm, 4)
                link(dve.tensor_tensor(mod[:, 0:16], bank[7][:, 256:272], v0[:, V_BADA:V_BADA + 16], ALU.add))
                dve.tensor_scalar(mod[:, 8:16], mod[:, 8:16], 1.0, None, ALU.add).then_inc(mod_made, 1)
                split_affine(T_H, M_H, 0, lambda k: mod[:, 8 + k:9 + k], lambda k: mod[:, k:k + 1])

            def late_mod():
                dve.wait_ge(col_mm, 4 + 12)
                link(dve.tensor_tensor(mod[:, 16:40], bank[7][:, 0:24], v0[:, V_BADA + 16:V_BADA + 40], ALU.add))
                link(dve.tensor_scalar(mod[:, 16:24], mod[:, 16:24], 1.0, None, ALU.add))
                link(dve.tensor_scalar(mod[:, 32:40], mod[:, 32:40], 1.0, None, ALU.add))
                for n, factor in ((48, mod[:, 32:40]), (64, v1[:, V_N1:V_N1 + KT])):
                    for m in range(2):
                        v = V_LN[(n - 48) // 16] + KT * m
                        link(dve.tensor_tensor(mod[:, n + KT * m:n + KT * m + KT], v1[:, v:v + KT], factor, ALU.mult))
                dve.tensor_tensor(mod[:, 56:64], mod[:, 56:64], mod[:, 24:32], ALU.add).then_inc(late_made, 1)

            def last_mod():
                dve.wait_ge(col_mm, 4 + N_LATE)
                link(dve.tensor_tensor(mod[:, 40:48], bank[3][:, 0:8], v0[:, V_BADA + 40:V_BADA + 48], ALU.add))
                dve.tensor_scalar(mod[:, 40:48], mod[:, 40:48], 1.0, None, ALU.add).then_inc(late_made, 1)

            def softplus(part):
                W = [dtf[0:64, n] for n in range(6)]
                if part == 0:
                    dve.wait_ge(small_in, 64)
                    dve.wait_ge(consts, 7)
                    dve.wait_ge(a_col, 1)
                    link(dve.tensor_scalar(col64[0:16, 3:4], col64[0:16, 3:4], -1.0, None, ALU.mult))
                    dve.wait_ge(ticks, 2)
                    dve.tensor_scalar(W[0], bank[0][0:64, :], col64[:, 0:1], col64[:, 1:2], ALU.add, ALU.mult).then_inc(evac[0], 4)
                    dve.wait_ge(evac[0], 4)
                    dve.scalar_tensor_tensor(W[1], W[0], -1.0, W[0], ALU.mult, ALU.max).then_inc(dtf_abs, 1)
                elif part == 1:
                    dve.wait_ge(dtf_exp, 1)
                    link(dve.tensor_scalar(W[3], W[2], 2.0, None, ALU.add))
                    link(dve.reciprocal(W[3], W[3]))
                    link(dve.tensor_tensor(W[3], W[2], W[3], ALU.mult))
                    link(dve.tensor_tensor(W[4], W[3], W[3], ALU.mult))
                    link(dve.tensor_scalar(W[5], W[4], 1.0 / 19, None, ALU.mult))
                    for n in range(17, 9, -2):
                        link(dve.scalar_tensor_tensor(W[5], W[5], 1.0 / n, W[4], ALU.add, ALU.mult))
                else:
                    for n in range(9, 1, -2):
                        link(dve.scalar_tensor_tensor(W[5], W[5], 1.0 / n, W[4], ALU.add, ALU.mult))
                    link(dve.scalar_tensor_tensor(W[5], W[5], 1.0, W[3], ALU.add, ALU.mult))
                    link(dve.tensor_scalar(W[0], W[0], 0.0, None, ALU.max))
                    link(dve.scalar_tensor_tensor(W[0], W[5], 2.0, W[0], ALU.mult, ALU.add))
                    link(dve.tensor_scalar(W[2], W[0], col64[:, 3:4], None, ALU.mult))
                    for ch in range(TB):
                        cols = slice(ch * P, ch * P + P)
                        dve.tensor_tensor_scan(dtf[0:16, 1, cols], ones[0:16, :], dtf[0:16, 2, cols], 0.0,
                                               ALU.mult, ALU.add).then_inc(scanned, 1)
                    dve.tensor_tensor_scan(dtf[32:48, 1, :], ones[32:48, 0:1].broadcast_to([16, S]), dtf[32:48, 2, :], 0.0,
                                           ALU.mult, ALU.add).then_inc(scanned, 1)

            def convolve(q):
                dve.wait_ge(tap_made, q + 1)
                for lag in (1, 2, 3):
                    w = V_CONVW + (3 - lag) * CT + q
                    ins = dve.scalar_tensor_tensor(xbc[:, q, lag:], bank[q % 4][:, 0:S - lag], v0[:, w:w + 1],
                                                   xbc[:, q, lag:], ALU.mult, ALU.add)
                    if lag < 3:
                        link(ins)
                    else:
                        ins.then_inc(evac[0], 1)

            def by_head(ap):
                return ap.rearrange("p (h d) -> p h d", d=HD)

            def per_head(ap):
                return ap.unsqueeze(2).broadcast_to([P, SSM_H, HD])

            def ssd():
                dve.wait_ge(dta_t, 1)
                dve.tensor_copy(dta[:].rearrange("p a b -> p (a b)"), bank[2][:]).then_inc(dta_made, 1)
                dve.wait_ge(dta_made, 1)
                dve.wait_ge(xs_made, 10)
                dve.wait_ge(cum_out, 16)

                def decay_in(ch):
                    b, acs = bc[:, ch % 2], dta[:, 4 + ch, 0:16]
                    dve.wait_ge(bc_in[ch % 2], 16 * (ch // 2 + 1))
                    if ch >= 2:
                        dve.wait_ge(prev_made, 2 * ch - 2)
                    dve.tensor_tensor(ex2[:, ch % 2, 2], b[:, :, P - 1], acs, ALU.subtract).then_inc(ex_in, 1)
                    dve.wait_ge(ex_made, 3 * ch + 3)
                    link(dve.tensor_tensor(b, b, acs.unsqueeze(2).broadcast_to([P, SSM_H, P]), ALU.subtract))
                    dve.tensor_scalar(b, b, 0.0, None, ALU.min).then_inc(bc_sub, 1)

                def inputs(ch):
                    if ch:
                        dve.wait_ge(y_mm, ch)
                    dve.tensor_tensor(by_head(xc), by_head(xs[:, ch]), per_head(dta[:, ch, 0:16]), ALU.mult).then_inc(xc_made, 1)
                    dve.wait_ge(xc_made, ch + 1)
                    dve.tensor_tensor(by_head(xd), by_head(xc), per_head(ex2[:, ch % 2, 2]), ALU.mult).then_inc(xd_made, 1)
                    link(dve.tensor_tensor(by_head(xs[:, ch]), by_head(xs[:, ch]), per_head(dsk[:]), ALU.mult))

                decay_in(0)
                dve.wait_ge(xs_made, 8)
                dve.wait_ge(cum_out, 16)
                inputs(0)
                for b in range(2):
                    dve.wait_ge(cb_done, b + 1)
                    dve.tensor_tensor(cbm[:, 2 * b:2 * b + 2].rearrange("p a (g l) -> p (a g) l", g=2),
                                      bank[3 + b][:].rearrange("p (a l) -> p a l", a=4),
                                      keep.unsqueeze(1).broadcast_to([P, 4, P]), ALU.mult).then_inc(cb_evac, 1)
                dve.wait_ge(cb_evac, 2)
                for ch in range(TB):
                    e, yc = ex2[:, ch % 2], xs[:, ch]
                    dve.wait_ge(bc_exp, ch + 1)
                    b4 = bc[:, ch % 2].rearrange("p (g e) l -> p g e l", g=2)
                    c4 = cbm[:, ch].rearrange("p (g l) -> p g l", g=2).unsqueeze(2).broadcast_to([P, 2, 8, P])
                    dve.tensor_tensor(b4, b4, c4, ALU.mult).then_inc(score_made, 1)
                    if ch < TB - 1:
                        decay_in(ch + 1)
                    if ch == 0:
                        late_ada(6)
                        late_ada(7)
                    dve.wait_ge(y_mm, ch + 1)
                    if ch:
                        for g in range(2):
                            part = slice(512 * g, 512 * g + 512)
                            d = e[:, 0, 8 * g:8 * g + 8].unsqueeze(2).broadcast_to([P, 8, HD])
                            ins = dve.tensor_tensor(by_head(off[:, part]), by_head(bank[2 + g][:]), d, ALU.mult)
                        link(ins)
                        link(dve.tensor_tensor(yc, off, yc, ALU.add))
                    for g in range(2):
                        part = slice(512 * g, 512 * g + 512)
                        dve.tensor_tensor(yc[:, part], bank[g][:], yc[:, part], ALU.add).then_inc(y_made, 1)
                    if ch < TB - 1:
                        if ch:
                            link(dve.tensor_tensor(by_head(prev), by_head(prev), per_head(e[:, 1]), ALU.mult))
                        for g in range(2):
                            part = slice(512 * g, 512 * g + 512)
                            if ch:
                                dve.tensor_tensor(prev[:, part], bank[4 + g][:], prev[:, part], ALU.add).then_inc(prev_made, 1)
                            else:
                                dve.tensor_copy(prev[:, part], bank[4 + g][:]).then_inc(prev_made, 1)
                        dve.wait_ge(prev_made, 2 * ch + 2)
                        inputs(ch + 1)
                    if ch >= 2:
                        late_ada(6 + ch)
                dve.wait_ge(y_made, 2 * TB)
                for t in range(TB):
                    dve.wait_ge(z_read, 5 + t)
                    dve.tensor_tensor(z_y[:, t], xs[:, t], z_y[:, t], ALU.mult).then_inc(yz_made, 1)

            def fox_scores(h):
                dve.wait_ge(ncm_made, h + 1)
                if h >= 2:
                    dve.wait_ge(pt_t, 3 * (h - 1))
                dve.wait_ge(s_mm, h + 1)
                for q in range(TB):
                    b, o = SB[q]
                    dst = prob[:, h % 2, QO[q]:QO[q] + (q + 1) * P]
                    if q:
                        dve.tensor_tensor(dst[:, 0:q * P], bank[b][:, o:o + q * P], ncb[:, h % 2, 0:q * P], ALU.add)
                    ins = dve.tensor_tensor(dst[:, q * P:q * P + P], bank[b][:, o + q * P:o + q * P + P],
                                            ncm[:, h % 2, q * P:q * P + P], ALU.add)
                    if q == TB - 1:
                        ins.then_inc(s_made, 1)
                dve.wait_ge(s_made, h + 1)
                maxima(h, lambda q: prob[:, h % 2, QO[q]:QO[q] + (q + 1) * P])

            def short_conv():
                for n in range(2):
                    z, y = cp[:, 2 + n], tmp[:, n]
                    tmp_free(T_MIX + n)
                    link(dve.tensor_tensor(z, z, cp[:, 4 + n], ALU.mult))
                    link(dve.tensor_scalar(y, z, v1[:, V_CW2 + 4 + n:V_CW2 + 5 + n], None, ALU.mult))
                    for lag in (1, 2):
                        w = v1[:, V_CW2 + 4 - 2 * lag + n:V_CW2 + 5 - 2 * lag + n]
                        link(dve.scalar_tensor_tensor(y[:, lag:], z[:, 0:S - lag], w, y[:, lag:], ALU.mult, ALU.add))
                    dve.tensor_tensor(y, y, cp[:, n], ALU.mult).then_inc(tile_made, 1)

            def split_conv():
                for n in range(2):
                    tile_lo(T_MIX + n, M_MIX + n, 1, 4 + n)

            def pool_counts():
                cnt = pinv[:, 1]
                link(dve.tensor_tensor_scan(cnt, ones[:, 0:16], ones[:, 0:16], 0.0, ALU.mult, ALU.add))
                for n, po, w in ((0, 0, 2), (0, 64, 4), (1, 0, 8), (1, 64, 16)):
                    link(dve.tensor_scalar(pinv[po:po + 64, n], cnt[po:po + 64, :], float(w), None, ALU.min))
                link(dve.reciprocal(pinv[:].rearrange("p a b -> p (a b)"), pinv[:].rearrange("p a b -> p (a b)")))

            def pooling(n):
                if n == 0:
                    pool_counts()
                for n in (n,):
                    u, m = cp[:, 6 + n], cp[:, 2 + n]
                    src, at_ = u, 0
                    for lag in (1, 2) if n == 0 else (1, 2, 4, 8):
                        dst = cp[:, at_]
                        link(dve.tensor_copy(dst[:, 0:lag], src[:, 0:lag]))
                        link(dve.tensor_tensor(dst[:, lag:], src[:, lag:], src[:, 0:S - lag], ALU.add))
                        src, at_ = dst, 1 - at_
                    for po, place, w in ((0, at_, 2 if n == 0 else 8), (64, 1 - at_, 4 if n == 0 else 16)):
                        h = slice(po, po + 64)
                        link(dve.tensor_tensor(m[h, 0:16], cp[h, place, 0:16], pinv[h, n], ALU.mult))
                        link(dve.tensor_tensor(m[h, 0:16], m[h, 0:16], u[h, 0:16], ALU.subtract))
                        ins = dve.scalar_tensor_tensor(m[h, 16:], cp[h, place, 16:], 1.0 / w, u[h, 16:], ALU.mult, ALU.subtract)
                        if po:
                            ins.then_inc(m_made, 1)
                            dve.wait_ge(m_made, n + 1)
                        else:
                            link(ins)

            def split_pool():
                for n in range(2):
                    dve.wait_ge(m_mm, n + 1)
                    tmp_free(T_MIX + 2 + n)
                    dve.tensor_scalar(tmp[:, n], bank[CP_BANKS[n]][:], v1[:, V_PS + n:V_PS + n + 1], None, ALU.mult).then_inc(tile_made, 1)
                for n in range(2):
                    tile_lo(T_MIX + 2 + n, M_MIX + 2 + n, 1, 6 + n)

            def head_norm():
                for n in range(2):
                    dve.wait_ge(evac[n], 4 * (N_QKV2[n] + 1))
                    link(dve.tensor_tensor(sq2, qkv2[:, n], qkv2[:, n], ALU.mult))
                    dve.reduce_sum(head_rs[:, 32 * n:32 * n + 32], sq2.rearrange("p t (h d) -> p (t h) d", d=HD), AX)\
                        .then_inc(qk_sq, 1)
                    dve.wait_ge(qk_sq, n + 1)
                dve.wait_ge(qk_rs, 1)
                for n in range(2):
                    q = qkv2[:, n].rearrange("p t (h d) -> p (t h) d", d=HD)
                    dve.tensor_tensor(q, q, head_rs[:, 32 * n:32 * n + 32].unsqueeze(2).broadcast_to([P, 32, HD]), ALU.mult)\
                        .then_inc(qk_made, 1)

            start()
            softplus(0)
            dve.wait_ge(a_lo_made, T_H + 8)
            for q in range(CT):
                if q % 4 < 2:
                    late_ada(q // 4 * 2 + q % 4)
                if q in (2, 4):
                    softplus(q // 2)
                convolve(q)
            ssd()
            for half in range(2):
                if half == 0:
                    late_ada(10)
                split_turned(T_SSM + 4 * half, 1, lambda k: v0[:, V_SSM + k + 4 * half:V_SSM + k + 4 * half + 1], range(4), 4 * half)
            late_ada(11)
            late_mod()
            for n in range(12, N_LATE):
                late_ada(n)
            for s in range(18):
                if s == 1:
                    last_mod()
                if s >= 2:
                    h = s - 2
                    output(h, att[:, :, h * HD:h * HD + HD])
                if s < 16:
                    fox_scores(s)
            split_turned(T_ATT, 1, lambda k: v1[:, V_ATT + k:V_ATT + k + 1], ATT_BANKS)
            dve.wait_ge(g_made, 2)
            dve.wait_ge(yacc_read, 8)
            for t in range(TB):
                ins = dve.tensor_tensor(yacc[:, t], yacc[:, t], row[:, 0], ALU.mult)
            link(ins)
            dve.wait_ge(xre_in, 16)
            for t in range(TB):
                link(dve.scalar_tensor_tensor(yacc[:, t], xre[:, t], ALPHA, yacc[:, t], ALU.mult, ALU.add))
            dve.wait_ge(rs_made, 2)
            dve.wait_ge(g_made, 2)
            for half in range(2):
                for t in range(TB):
                    part = slice(512 * half, 512 * half + 512)
                    wait_row(U_WO2 + 2 * half, P_WO2 + half, t)
                    dve.scalar_tensor_tensor(x1[:, t, part], bank[4 * half + t][:], st[:, 4 + t:5 + t], row[:, 0, part],
                                             ALU.mult, ALU.mult).then_inc(evac[half], 1)
                    dve.wait_ge(evac[half], 4 * N_WO2[half] + t + 1)
                    dve.tensor_tensor(x1[:, t, part], x1[:, t, part], yacc[:, t, part], ALU.add).then_inc(sum_made, 1)
                    dve.wait_ge(sum_made, 4 * half + t + 1)
                    half_stats(t, half)
                    if half and t:
                        normalize(0, t - 1)
            normalize(0, TB - 1)
            split_affine(T_X1, M_X1, 0, lambda k: mod[:, 48 + k:49 + k], lambda k: mod[:, 56 + k:57 + k])
            gain(0)
            dve.wait_ge(acc0, 1)

            def accumulate(b, t, part):
                dve.tensor_tensor(yacc[:, t, part], bank[4 * b + t][:], yacc[:, t, part], ALU.add).then_inc(evac[b], 1)

            def accumulate_last(b, t, part):
                accumulate(b, t, part)
                dve.wait_ge(evac[b], 4 * (N_FF1[b] + 2 * QUARTERS - 1) + t + 1)
                link(dve.tensor_tensor(yacc[:, t, part], yacc[:, t, part], row[:, 3, part], ALU.mult))
                dve.scalar_tensor_tensor(x1[:, t, part], x1[:, t, part], ALPHA, yacc[:, t, part], ALU.mult, ALU.add).then_inc(sum_made, 1)
                dve.wait_ge(sum_made, 8 + 4 * b + t + 1)
                half_stats(t, b)
                if b and t:
                    normalize(1, t - 1)

            with dve.Fori(0, QUARTERS - 1) as i:
                feed_forward(U_FF1, T_HID1, M_HID1, N_FF1, P_FF1, i, accumulate)
            dve.wait_ge(g_made, 4)
            dve.wait_ge(ln_made, 4)
            feed_forward(U_FF1, T_HID1, M_HID1, N_FF1, P_FF1, QUARTERS - 1, accumulate_last)
            normalize(1, TB - 1)
            split_affine(T_N2, M_N2, 0, lambda k: mod[:, 64 + k:65 + k], lambda k: mod[:, 72 + k:73 + k])
            gain(1)
            head_norm()

            def read_cp(n):
                dve.wait_ge(rrow_made, 1)
                dve.wait_ge(ticks, 2 * U_CP + n + 1)
                dve.tensor_tensor(cp[:, n], bank[CP_BANKS[n % 2]][:], tmp[:, 1], ALU.mult).then_inc(cp_read, 1)

            read_cp(0)
            for n in range(2):
                for k in range(4):
                    dve.wait_ge(q2_t, 4 * n + k + 1)
                    dve.tensor_scalar(qkT2[:, n, k], bank[3 + k][:], v1[:, V_QG + n:V_QG + n + 1],
                                      HD ** -0.5 if n == 0 else 1.0, ALU.mult, ALU.mult).then_inc(q2_made, 1)
                if n == 0:
                    read_cp(1)
            for s in range(10):
                if s < 6:
                    read_cp(2 + s)
                if s >= 2:
                    h = s - 2
                    output(16 + h, att2[:, :, h * HD:h * HD + HD])
                if s < 8:
                    dve.wait_ge(s_mm, 16 + s + 1)
                    maxima(16 + s, lambda q: bank[SB[q][0]][:, SB[q][1]:SB[q][1] + (q + 1) * P])
                if s == 5:
                    short_conv()
                elif s == 6:
                    pooling(0)
                    split_conv()
                elif s == 7:
                    pooling(1)
            split_pool()
            split_turned(T_MIX + 4, 1, lambda k: 1.0, range(4))
            for half in range(2):
                for t in range(TB):
                    part = x1[:, t, 512 * half:512 * half + 512]
                    wait_row(U_WO3 + 2 * half, P_WO3 + half, t)
                    dve.tensor_tensor(part, bank[4 * (1 - half) + t][:], part, ALU.add).then_inc(evac[1 - half], 1)
            split_turned(T_N3, 0, lambda k: v1[:, V_N2 + k:V_N2 + k + 1], N3_BANKS)
            def add_scaled(b, t, part):
                dve.scalar_tensor_tensor(x1[:, t, part], bank[4 * b + t][:], st[:, 12 + t:13 + t], x1[:, t, part],
                                         ALU.mult, ALU.add).then_inc(evac[b], 1)

            dve.wait_ge(r2_made, 1)
            with dve.Fori(0, QUARTERS) as i:
                feed_forward(U_FF2, T_HID2, M_HID2, N_FF2, P_FF2, i, add_scaled)

        @block.tensor
        def _(pe):
            def three(out_, hi_a, lo_a, hi_b, lo_b, start, stop):
                pe.matmul(out_, hi_a, hi_b, start=start, stop=False)
                pe.matmul(out_, hi_a, lo_b, start=False, stop=False)
                return pe.matmul(out_, lo_a, hi_b, start=False, stop=stop)

            def column_tile(u0, n, act_buf, dst, t0=None, i=0, per=0):
                s = u0 % 2
                if n == 0:
                    pe.wait_ge(w_lo_made, at(i, per, u0 + 1))
                for k in range(KT):
                    if t0 is not None:
                        pe.wait_ge(a_lo_made, t0 + k + 1)
                    w = slice(256 * k + P * n, 256 * k + P * n + P)
                    last = three(dst, w_hi[:, s, w], w_lo[:, s, w], a_hi[act_buf][:, k], a_lo[act_buf][:, k],
                                 k == 0, k == KT - 1)
                last.then_inc(ticks, 1)

            def column_pair(u0, s, n_use, act_buf, t0=None, i=0, per=0, uses=0):
                pe.wait_ge(evac[s], at(i, 4 * uses, 4 * n_use))
                for j in range(4):
                    column_tile(u0 + j // 2, j % 2, act_buf, bank[4 * s + j][:], t0 if j == 0 else None, i, per)

            def row_half(u0, b, s, act_buf, kk0, first, final, wait=None, i=0, per=0):
                slot = (u0 + b) % 2
                pe.wait_ge(w_lo_made, at(i, per, u0 + b + 1))
                order = [(k, t) for k in range(4) for t in range(TB)] if b == 0 else [(k, t) for t in range(TB) for k in range(4)]
                for m, (k, t) in enumerate(order):
                    kk = kk0 + k
                    if wait and t == 0:
                        pe.wait_ge(a_lo_made, wait(kk))
                    a = slice(P * t, P * t + P)
                    w = slice(512 * k, 512 * k + 512)
                    last = three(bank[4 * s + t][:], a_hi[act_buf][:, kk, a], a_lo[act_buf][:, kk, a],
                                 w_hi[:, slot, w], w_lo[:, slot, w], first and k == 0, final and k == 3)
                    if m % 8 == 7:
                        last.then_inc(ticks, 1)
                    elif b == 1 and m % 8 == 3:
                        last.then_inc(even_done, 1)

            def row_pair(u0, s, n_use, act_buf, t0=None, i=0, per=0, uses=0, tstep=0):
                if n_use:
                    pe.wait_ge(evac[s], at(i, 4 * uses, 4 * n_use))
                for b in range(2):
                    wait = None if t0 is None else lambda kk: at(i, tstep, t0 + kk + 1)
                    row_half(u0, b, s, act_buf, 4 * b, b == 0, b == 1, wait, i, per)

            def turn_blocks(src, banks, ready, set_free):
                for half in range(2):
                    if half:
                        set_free()
                    for t in range(TB):
                        if half == 0:
                            ready(t)
                        for k in range(4 * half, 4 * half + 4):
                            last = pe.transpose(bank[banks[k]][:, P * t:P * t + P], src[:, t, P * k:P * k + P], ident[:])
                            if t == TB - 1:
                                last.then_inc(turned, 1)

            def row_tile(u, n, act_buf, dst):
                for kk in range(KT):
                    slot, a, w = (u + kk // 4) % 2, slice(P * (n % 4), P * (n % 4) + P), slice(512 * (kk % 4), 512 * (kk % 4) + 512)
                    if kk % 4 == 0 and n % 4 == 0:
                        pe.wait_ge(w_lo_made, u + kk // 4 + 1)
                    last = three(dst, a_hi[act_buf][:, kk, a], a_lo[act_buf][:, kk, a],
                                 w_hi[:, slot, w], w_lo[:, slot, w], kk == 0, kk == KT - 1)
                last.then_inc(ticks, 1)

            def last_tiles(u, act_buf, b6, b7, between=None):
                for b in range(2):
                    for n, dst in ((6, b6), (7, b7)):
                        slot = (u + b) % 2
                        for k in range(4):
                            a, w, kk = slice(P * (n - 4), P * (n - 4) + P), slice(512 * k, 512 * k + 512), 4 * b + k
                            last = three(dst[:], a_hi[act_buf][:, kk, a], a_lo[act_buf][:, kk, a],
                                         w_hi[:, slot, w], w_lo[:, slot, w], kk == 0, kk == KT - 1)
                    last.then_inc(ticks, 1)
                    if b == 0 and between:
                        between()

            def sum_columns(src, b, col, n, signal):
                for h in range(n):
                    last = pe.matmul(bank[b][:, col + h:col + h + 1], src[:, P * h:P * h + P], ones[:, 0:1], start=True, stop=True)
                last.then_inc(signal, 1)

            def late_columns(n, b=7, col=0):
                pe.wait_ge(late_sum, n + 1)
                sum_columns(late_place(n), b, 2 * n - col, 2, col_mm)

            def turn(src, n=KT, first=0, banks=range(KT)):
                for k in range(first, first + n):
                    for t in range(TB):
                        last = pe.transpose(bank[banks[k]][:, P * t:P * t + P], src[:, t, P * k:P * k + P], ident[:])
                    last.then_inc(turned, 1)

            def evacuated(n0, n1):
                pe.wait_ge(evac[0], 4 * n0)
                pe.wait_ge(evac[1], 4 * n1)

            def probs_t(h, src):
                pe.wait_ge(p_made, 4 * h + 4)
                for b in range(10):
                    m, o = b // 4, b % 4
                    if o == 0 and h:
                        pe.wait_ge(pt_made, 3 * (h - 1) + m + 1)
                        if m == 2:
                            pe.wait_ge(o_made, h)
                    last = pe.transpose(bank[PT_BANKS[h // 16][m]][:, o * P:o * P + P], src[:, b * P:b * P + P], ident[:])
                    if b in (3, 7, 9):
                        last.then_inc(pt_t, 1)

            def values(h, pT, v):
                pe.wait_ge(pt_made, 3 * h + 3)
                for q in range(TB):
                    for k in range(q + 1):
                        b = q * (q + 1) // 2 + k
                        last = pe.matmul(bank[3][:, 256 + q * HD:256 + q * HD + HD], pT[:, b * P:b * P + P], v(k),
                                         start=k == 0, stop=k == q)
                last.then_inc(o_mm, 1)

            def g_row(col, b):
                for half in range(2):
                    for k in range(4):
                        m = col + 4 * half + k
                        last = pe.matmul(bank[b + half][:, k * P:k * P + P], mod[:, m:m + 1].broadcast_to([P, P]), ident[:],
                                         start=True, stop=True)
                    last.then_inc(g_mm, 1)

            pe.wait_ge(consts, 7)
            pe.wait_ge(vecs_in, 16 * 18)
            for n in range(2):
                last = pe.transpose(bank[7][:, P * n:P * n + P], vec_in[:, n, :], ident[:])
            last.then_inc(vecs_t, 1)
            pe.wait_ge(x_in, 16)
            turn(xtok, KT - 1)
            for n in range(4):
                pe.wait_ge(ada_sum, n + 1)
                sum_columns(tmp[:, n % 2], 7, 256 + 4 * n, 4, col_mm)
            pe.wait_ge(mod_made, 1)
            turn(xtok, 1, KT - 1)
            pe.wait_ge(w_lo_made, 1)
            for k in range(KT):
                pe.wait_ge(a_lo_made, T_H + k + 1)
                w = slice(256 * k, 256 * k + P)
                last = three(bank[0][:], w_hi[:, 0, w], w_lo[:, 0, w], a_hi[0][:, k], a_lo[0][:, k], k == 0, k == KT - 1)
                if k in (3, 7):
                    last.then_inc(ticks, 1)
            def turn_xs(b):
                pe.wait_ge(conv_act, 8 if b < 8 else 10)
                if b >= 2:
                    pe.wait_ge(xs_made, b - 1)
                for k in range(4):
                    if b < 8:
                        src = xbc[:, 4 * (b % 2) + k, P * (b // 2):P * (b // 2) + P]
                    else:
                        t, g = 2 * (b - 8) + k // 2, k % 2
                        src = xbc[:, 8 + g, P * t:P * t + P]
                    last = pe.transpose(bank[XS_BANKS[b % 2]][:, P * k:P * k + P], src, ident[:])
                last.then_inc(xs_t, 1)

            for q in range(CT):
                pe.wait_ge(evac[0], 4 * (N_XBC[0] - 1) + q + 1)
                column_tile(U_XBC + q // 2, q % 2, 0, bank[q % 4][:])
                if q >= 4 and q % 4 < 2:
                    late_columns(2 * (q // 4 - 1) + q % 4)
                if q >= 9:
                    turn_xs(2 * q - 18)
                    turn_xs(2 * q - 17)
            turn_xs(6)
            turn_xs(7)

            def z_tile(n):
                if n:
                    pe.wait_ge(z_read, n)
                row_tile(U_Z + 2 * (n // 4), n, 0, bank[6][:])

            z_tile(0)
            late_columns(4)
            late_columns(5)
            pe.wait_ge(scanned, 5)
            pe.wait_ge(evac[0], 4 * (N_XBC[0] + 3))
            for b in range(8):
                last = pe.transpose(bank[2][:, 64 * b:64 * b + 64], dtf[0:64, b // 4, P * (b % 4):P * (b % 4) + P], ident[0:64, 0:64])
            last.then_inc(dta_t, 1)
            turn_xs(8)
            turn_xs(9)
            pe.wait_ge(conv_act, CT)
            for b in range(2):
                pe.wait_ge(xs_made, 9)
                for k in range(4):
                    t, g = 2 * b + k // 2, k % 2
                    part = slice(P * t, P * t + P)
                    last = pe.matmul(bank[3 + b][:, P * k:P * k + P], xbc[:, 8 + g, part], xbc[:, 10 + g, part], start=True, stop=True)
                last.then_inc(cb_done, 1)
            z_tile(1)
            pe.wait_ge(xs_made, 10)
            pe.wait_ge(dta_made, 1)
            pe.wait_ge(cb_evac, 2)
            for ch in range(TB):
                if ch < TB - 1:
                    pe.wait_ge(xd_made, ch + 1)
                    if ch:
                        pe.wait_ge(prev_made, 2 * ch)
                    for g in range(2):
                        last = pe.matmul(bank[4 + g][:], btok[:, ch, g, :], xd[:, 512 * g:512 * g + 512], start=True, stop=True)
                    last.then_inc(st_mm, 1)
                if ch:
                    pe.wait_ge(prev_made, 2 * ch)
                    pe.wait_ge(y_made, 2 * ch)
                    for g in range(2):
                        pe.matmul(bank[2 + g][:], xbc[:, 10 + g, P * ch:P * ch + P], prev[:, 512 * g:512 * g + 512],
                                  start=True, stop=True)
                pe.wait_ge(xc_made, ch + 1)
                pe.wait_ge(score_made, ch + 1)
                for h in range(SSM_H):
                    last = pe.matmul(bank[h // 8][:, HD * (h % 8):HD * (h % 8) + HD], bc[:, ch % 2, h, :],
                                     xc[:, HD * h:HD * h + HD], start=True, stop=True)
                last.then_inc(y_mm, 1)
                if ch == 0:
                    late_columns(6)
                    late_columns(7)
                for n in Z_TILES[ch]:
                    z_tile(n)
            pe.wait_ge(z_read, 6)
            last_tiles(U_Z + 2, 0, bank[6], bank[5])
            late_columns(8)
            for j in range(4):
                if j == 1:
                    late_columns(9)
                pe.wait_ge(z_read, 8)
                if j >= 2:
                    pe.wait_ge(qk_read, j - 1)
                    pe.wait_ge(yz_made, 4)
                    if j == 3:
                        pe.wait_ge(a_lo_made, T_SSM + 4)
                    turn(z_y, 4, 4 * (j - 2), (0, 1, 2, 3) * 2)
                column_tile(U_QK + j // 2, j % 2, 0, bank[(6, 5)[j % 2]][:])
            pe.wait_ge(a_lo_made, T_SSM + 8)
            late_columns(10)
            late_columns(11)
            row_pair(U_V, 0, N_V[0], 0)
            pe.wait_ge(qk_read, 4)
            pe.wait_ge(late_made, 1)
            row_pair(U_V + 2, 1, N_V[1], 0)
            pe.wait_ge(evac[0], 4 * (N_V[0] + 1))
            late_columns(12, b=3, col=24)
            late_columns(13, b=3, col=24)
            evacuated(N_V[0] + 1, N_V[1] + 1)

            def filler_free(n):
                if n >= 14:
                    pe.wait_ge(yacc_read, n - 13)
                elif n >= 2:
                    pe.wait_ge(qk_read, 4 + n - 1)

            for s in range(18):
                if s >= 2:
                    if s == 2:
                        pe.wait_ge(late_made, 2)
                    probs_t(s - 2, prob[:, s % 2])
                if s < 12:
                    filler_free(s)
                    column_tile(U_QK1 + s // 2, s % 2, 0, bank[s % 2][:])
                if s < 2:
                    late_columns(14 + s, b=3, col=24)
                if s >= 2:
                    h = s - 2
                    values(h, probT, lambda k: vtok[:, k, h * HD:h * HD + HD])
                if s < 16:
                    pe.wait_ge(qk_read, 4 * (s // 4 + 1))
                    if s:
                        pe.wait_ge(s_made, s)
                    po, tile = HD * (s % 2), (s % 4) // 2
                    q_, k_ = qk[po:po + HD, (s // 4) % 2, tile], qk[po:po + HD, (s // 4) % 2, 2 + tile]
                    for q in range(TB):
                        b, o = SB[q]
                        last = pe.matmul(bank[b][:, o:o + (q + 1) * P], q_[:, P * q:P * q + P], k_[:, 0:(q + 1) * P],
                                         start=True, stop=True)
                    last.then_inc(s_mm, 1)
                for n in WO1_TILES[s]:
                    filler_free(12 + n)
                    row_tile(U_WO1 + 2 * (n // 4), n, 1, bank[n % 2][:])
            pe.wait_ge(s_made, 16)
            g_row(16, 4)
            pe.wait_ge(yacc_read, 6)

            def turn_att():
                pe.wait_ge(pt_made, 48)
                pe.wait_ge(o_made, 16)
                turn(att, 4, 0, ATT_BANKS)
                pe.wait_ge(g_made, 2)
                g_row(40, 4)

            last_tiles(U_WO1 + 2, 1, bank[0], bank[1], turn_att)
            pe.wait_ge(g_made, 4)
            pe.wait_ge(a_lo_made, T_ATT + 4)
            turn(att, 4, 4, ATT_BANKS)
            pe.wait_ge(yacc_read, 8)
            row_pair(U_WO2, 0, N_WO2[0], 1, T_ATT)
            pe.wait_ge(a_lo_made, T_ATT + 8)
            row_pair(U_WO2 + 2, 1, N_WO2[1], 1)

            def norm_ready(turn, n0):
                def ready(t):
                    if t == 0:
                        pe.wait_ge(evac[0], 4 * n0[0])
                    pe.wait_ge(xhat_made, 4 * turn + t + 1)
                return ready

            turn_blocks(x1, range(KT), norm_ready(0, N_FF1), lambda: pe.wait_ge(evac[1], 4 * N_FF1[1]))

            def feed_forward(u0, t_act, t0, n0):
                with pe.Fori(0, QUARTERS) as i:
                    for b in range(2):
                        column_pair(u0 + 2 * b, b, n0[b], 0, t_act if b == 0 else None, i=i, per=8, uses=2)
                    for b in range(2):
                        row_pair(u0 + 4 + 2 * b, b, n0[b] + 1, 1, t0 if b == 0 else None, i=i, per=8, uses=2, tstep=8)

            feed_forward(U_FF1, T_X1, T_HID1, N_FF1)
            turn_blocks(x1, range(KT), norm_ready(1, N_QKV2), lambda: pe.wait_ge(evac[1], 4 * N_QKV2[1]))
            pe.wait_ge(a_lo_made, T_N2 + 4)
            row_pair(U_QKV2, 0, N_QKV2[0], 0, T_N2)
            row_pair(U_QKV2 + 2, 1, N_QKV2[1], 0)
            row_pair(U_QKV2 + 4, 0, N_QKV2[0] + 1, 0)
            pe.wait_ge(evac[1], 4 * N_WO3[1])
            for t in range(TB):
                last = pe.matmul(bank[4][:, P * t:P * t + P], st[:, 4 + t:5 + t].broadcast_to([P, P]), ident[:], start=True, stop=True)
            last.then_inc(rrow_mm, 1)
            pe.wait_ge(evac[0], 4 * N_WO3[0])

            def cp_tile(n):
                if n >= 2:
                    pe.wait_ge(cp_read, n - 1)
                column_tile(U_CP + n // 2, n % 2, 0, bank[CP_BANKS[n % 2]][:])

            cp_tile(0)
            pe.wait_ge(rrow_made, 1)
            for n in range(2):
                pe.wait_ge(qk_made, n + 1)
                for k in range(4):
                    if n:
                        pe.wait_ge(q2_made, k + 1)
                    for t in range(TB):
                        last = pe.transpose(bank[3 + k][:, P * t:P * t + P], qkv2[:, n, t, P * k:P * k + P], ident[:])
                    last.then_inc(q2_t, 1)
                if n == 0:
                    cp_tile(1)
            pe.wait_ge(q2_made, 8)
            pe.wait_ge(rel_made, 1)
            for s in range(10):
                if s >= 2:
                    probs_t(16 + s - 2, prob2[:, s % 2])
                if s < 6:
                    cp_tile(2 + s)
                if s >= 2:
                    h = s - 2
                    values(16 + h, prob2T, lambda k: qkv2[:, 2, k, h * HD:h * HD + HD])
                if s < 8:
                    if s:
                        pe.wait_ge(p_made, 4 * (16 + s))
                    po, tile = HD * (s % 2), s // 2
                    q_, k_ = qkT2[po:po + HD, 0, tile], qkT2[po:po + HD, 1, tile]
                    for q in range(TB):
                        b, o = SB[q]
                        n = (q + 1) * P
                        pe.matmul(bank[b][:, o:o + n], q_[:, P * q:P * q + P], k_[:, 0:n], start=True, stop=False)
                        if q >= 2:
                            far = (q - 1) * P
                            pe.matmul(bank[b][:, o:o + far], ones[0:1, 0:P], relc[0:1, s:s + 1].broadcast_to([1, far]),
                                      start=False, stop=False)
                        if q >= 1:
                            pe.matmul(bank[b][:, o + n - 2 * P:o + n - P], relt[:, 1, s, :], flip[:], start=False, stop=False)
                        last = pe.matmul(bank[b][:, o + n - P:o + n], relt[:, 0, s, :], flip[:], start=False, stop=True)
                    last.then_inc(s_mm, 1)
                if s == 8:
                    pe.wait_ge(cp_read, 8)
                    pe.wait_ge(pool_in, 64)
                    for n in range(2):
                        pe.wait_ge(m_made, n + 1)
                        pe.matmul(bank[CP_BANKS[n]][:], poolw[:, n, :], cp[:, 2 + n], start=True, stop=True).then_inc(m_mm, 1)
            pe.wait_ge(p_made, 4 * 24)
            pe.wait_ge(tile_made, M_MIX + 4)
            row_half(U_WO3, 0, 1, 1, 4, True, False, lambda kk: T_MIX + kk - 3)
            pe.wait_ge(pt_made, 3 * 24)
            pe.wait_ge(o_made, 24)
            turn(att2, 4)
            row_half(U_WO3, 1, 1, 1, 0, False, True, lambda kk: T_MIX + 4 + kk + 1)
            pe.wait_ge(a_lo_made, T_MIX + 8)
            for b in range(2):
                row_half(U_WO3 + 2, b, 0, 1, 4 * (1 - b), b == 0, b == 1)
            turn_blocks(x1, N3_BANKS, lambda t: (pe.wait_ge(evac[1], 4 * N_FF2[1]), pe.wait_ge(evac[0], 4 * N_WO3[0] + t + 1)),
                        lambda: None)
            pe.wait_ge(a_lo_made, T_N3 + 8)
            feed_forward(U_FF2, T_N3, T_HID2, N_FF2)


_INS = ["x", "c", "w_ada", "b_ada", "w_in", "conv_w", "conv_b", "dt_bias", "a_log", "d_skip", "ssm_norm_w", "f_bias",
        "attn_norm_w", "w_out", "ln1_g", "ln1_b", "w_ff_in", "w_ff_out", "ln2_g", "ln2_b", "norm1_g_2", "w_in_2",
        "q_norm_g_2", "k_norm_g_2", "rel_bias_2", "conv_w_2", "pool_w_2", "pool_scale_2", "w_out_2", "norm2_g_2",
        "w_mlp1_2", "w_mlp2_2"]


def kernel(**inputs):
    import numpy as _np
    import concourse.bacc as _bacc
    from concourse import mybir as _mybir
    from concourse.bass_utils import run_bass_kernel_spmd as _run

    nc = _bacc.Bacc("TRN2", target_bir_lowering=False, num_devices=1, dynamic_dma_scratch_size=8192)
    arrays, args = {}, []
    for name in _INS:
        a = _np.ascontiguousarray(inputs[name])
        arrays[f"in_{name}_dram"] = a
        args.append(nc.dram_tensor(f"in_{name}_dram", a.shape, _mybir.dt.from_np(a.dtype), kind="ExternalInput").ap())
    args.append(nc.dram_tensor("out_0_dram", (1, S, D), F32, kind="ExternalOutput").ap())
    build(nc, *args)
    r = _run(nc, [arrays], core_ids=[0])
    return r.results[0]["out_0_dram"]
```
